# Optimizing a Trainium2 kernel written in Bass

```python
import jax, jax.numpy as jnp
from jax import lax
import numpy as np
import math

D_MODEL = 1024
BATCH = 1
SEQ = 1024
DEPTH = 2

N_HEADS = D_MODEL // 128
QK_NOPE_DIM = 64
QK_ROPE_DIM = 32
QK_HEAD_DIM = QK_NOPE_DIM + QK_ROPE_DIM
V_HEAD_DIM = 64
ATTN_WIDTH = N_HEADS * V_HEAD_DIM
Q_LORA_RANK = D_MODEL // 4
KV_LORA_RANK = D_MODEL // 4
ROPE_THETA = 10000.0
Q_BLOCK = 128
FOURIER_WIDTH = D_MODEL // 2
FOURIER_GROUP_DIM = 128
N_FOURIER_GROUPS = FOURIER_WIDTH // FOURIER_GROUP_DIM
N_BRANCHES = 2
NORM_EPS = 1e-6
IN_WIDTH = (Q_LORA_RANK + KV_LORA_RANK + QK_ROPE_DIM + ATTN_WIDTH
            + 2 * FOURIER_WIDTH + N_BRANCHES * D_MODEL)


def _rms_norm(x, g):
    xf = x.astype(jnp.float32)
    y = xf * lax.rsqrt(jnp.mean(xf * xf, axis=-1, keepdims=True) + NORM_EPS)
    return (y * g.astype(jnp.float32)).astype(x.dtype)

def _rope_tables(seq_len, dtype):
    half = QK_ROPE_DIM // 2
    inv_freq = ROPE_THETA ** (-jnp.arange(half, dtype=jnp.float32) / half)
    pos = jnp.arange(seq_len, dtype=jnp.float32)
    ang = pos[:, None] * inv_freq[None, :]
    return jnp.cos(ang).astype(dtype), jnp.sin(ang).astype(dtype)

def _apply_rope(x, cos, sin):
    half = QK_ROPE_DIM // 2
    x1, x2 = x[..., :half], x[..., half:]
    c, s = cos[:, None, :], sin[:, None, :]
    return jnp.concatenate([x1 * c - x2 * s, x2 * c + x1 * s], axis=-1)

def _split_in(p):
    sizes = [Q_LORA_RANK, KV_LORA_RANK, QK_ROPE_DIM, ATTN_WIDTH,
             FOURIER_WIDTH, FOURIER_WIDTH, D_MODEL]
    idx = []
    acc = 0
    for s in sizes:
        acc += s
        idx.append(acc)
    return jnp.split(p, idx, axis=-1)

def _bidirectional_attention(q, k, v):
    b, h, s, dk = q.shape
    nb = s // Q_BLOCK
    scale = QK_HEAD_DIM ** -0.5
    qb = q.reshape(b, h, nb, Q_BLOCK, dk).transpose(2, 0, 1, 3, 4)

    def one_block(q_blk):
        sc = jnp.einsum('bhqd,bhkd->bhqk', q_blk, k).astype(jnp.float32) * scale
        p = jax.nn.softmax(sc, axis=-1)
        return jnp.einsum('bhqk,bhkd->bhqd', p.astype(v.dtype), v)

    o = lax.map(one_block, qb)
    return o.transpose(1, 2, 0, 3, 4).reshape(b, h, s, V_HEAD_DIM)

def _mla_branch(c_q, c_kv, k_pe, q_latent_g, kv_latent_g, w_uq, w_ukv,
                q_head_g, k_head_g, cos, sin):
    b, s, _ = c_q.shape
    q = (_rms_norm(c_q, q_latent_g) @ w_uq).reshape(b, s, N_HEADS, QK_HEAD_DIM)
    kv = (_rms_norm(c_kv, kv_latent_g) @ w_ukv).reshape(b, s, N_HEADS, QK_NOPE_DIM + V_HEAD_DIM)
    k_nope, v = kv[..., :QK_NOPE_DIM], kv[..., QK_NOPE_DIM:]
    k_pe_h = jnp.broadcast_to(k_pe[:, :, None, :], (b, s, N_HEADS, QK_ROPE_DIM))
    k = jnp.concatenate([k_nope, k_pe_h], axis=-1)
    q = _rms_norm(q, q_head_g)
    k = _rms_norm(k, k_head_g)
    q = jnp.concatenate([q[..., :QK_NOPE_DIM], _apply_rope(q[..., QK_NOPE_DIM:], cos, sin)], axis=-1)
    k = jnp.concatenate([k[..., :QK_NOPE_DIM], _apply_rope(k[..., QK_NOPE_DIM:], cos, sin)], axis=-1)
    o = _bidirectional_attention(q.transpose(0, 2, 1, 3), k.transpose(0, 2, 1, 3),
                                 v.transpose(0, 2, 1, 3))
    return o.transpose(0, 2, 1, 3).reshape(b, s, ATTN_WIDTH)

def _fourier_branch(u):
    b, s, _ = u.shape
    ug = u.astype(jnp.float32).reshape(b, s, N_FOURIER_GROUPS, FOURIER_GROUP_DIM)
    f = jnp.real(jnp.fft.fft2(ug, axes=(1, 3), norm='ortho'))
    return f.reshape(b, s, FOURIER_WIDTH).astype(u.dtype)

def first_inputs(seed: int = 0) -> dict:
    key = jax.random.key(seed)
    ks = jax.random.split(key, 14)
    L, D = DEPTH, D_MODEL

    def nrm(k, shape, fan_in):
        return jax.random.normal(k, shape, jnp.float32) * fan_in ** -0.5

    def gain(k, shape):
        return 1.0 + 0.05 * jax.random.normal(k, shape, jnp.float32)

    return {
        "x": jax.random.normal(ks[0], (BATCH, SEQ, D), jnp.float32),
        "norm_g": gain(ks[1], (L, D)),
        "w_in": nrm(ks[2], (L, D, IN_WIDTH), D),
        "q_latent_g": gain(ks[3], (L, Q_LORA_RANK)),
        "kv_latent_g": gain(ks[4], (L, KV_LORA_RANK)),
        "w_uq": nrm(ks[5], (L, Q_LORA_RANK, N_HEADS * QK_HEAD_DIM), Q_LORA_RANK),
        "w_ukv": nrm(ks[6], (L, KV_LORA_RANK, N_HEADS * (QK_NOPE_DIM + V_HEAD_DIM)), KV_LORA_RANK),
        "q_head_g": gain(ks[7], (L, QK_HEAD_DIM)),
        "k_head_g": gain(ks[8], (L, QK_HEAD_DIM)),
        "w_attn_proj": nrm(ks[9], (L, ATTN_WIDTH, D), ATTN_WIDTH),
        "w_fourier_proj": nrm(ks[10], (L, FOURIER_WIDTH, D), FOURIER_WIDTH),
        "b_merge": 0.1 * jax.random.normal(ks[11], (L, N_BRANCHES, D), jnp.float32),
        "w_out": nrm(ks[12], (L, D, D), D) * (2 * DEPTH) ** -0.5,
    }

def first_block(x, norm_g, w_in, q_latent_g, kv_latent_g, w_uq, w_ukv, q_head_g,
              k_head_g, w_attn_proj, w_fourier_proj, b_merge, w_out):
    _, s, _ = x.shape
    cos, sin = _rope_tables(s, x.dtype)
    for l in range(DEPTH):
        h = _rms_norm(x, norm_g[l])
        p = h @ w_in[l]
        c_q, c_kv, k_pe, z_a, u_f, z_f, g_a, g_f = _split_in(p)
        o_a = _mla_branch(c_q, c_kv, k_pe, q_latent_g[l], kv_latent_g[l], w_uq[l], w_ukv[l],
                          q_head_g[l], k_head_g[l], cos, sin)
        y_a = (o_a * jax.nn.silu(z_a)) @ w_attn_proj[l]
        y_f = (_fourier_branch(u_f) * jax.nn.silu(z_f)) @ w_fourier_proj[l]
        m = (jax.nn.sigmoid(g_a + b_merge[l, 0]) * y_a
             + jax.nn.sigmoid(g_f + b_merge[l, 1]) * y_f)
        x = x + m @ w_out[l]
    return x


DEPTH_2 = 1

D_MIX = D_MODEL
ATT_HEADS = 8
ATT_HEAD_DIM = 64
ATT_WIDTH = ATT_HEADS * ATT_HEAD_DIM
KV_LATENT = 128
IDX_HEADS = 8
IDX_DIM = 32
TOPK_MAX = 256
SSM_WIDTH = D_MIX - ATT_WIDTH
GROUP_CH = 16
N_GROUPS = SSM_WIDTH // GROUP_CH
STATE = 64
DT_MIN = 0.001
DT_MAX = 0.1
LN_EPS = 1e-5
RMS_EPS = 1e-6
DEEPNORM_ALPHA = (2 * DEPTH_2) ** 0.25
DEEPNORM_BETA = (8 * DEPTH_2) ** -0.25
SPLITS = (ATT_WIDTH, KV_LATENT, IDX_HEADS * IDX_DIM, IDX_DIM, IDX_HEADS, ATT_WIDTH, SSM_WIDTH, SSM_WIDTH)
D_IN = sum(SPLITS)


def _split_points():
    pts, acc = [], 0
    for s in SPLITS[:-1]:
        acc += s
        pts.append(acc)
    return pts

def layer_norm(x, g, b):
    xf = x.astype(jnp.float32)
    mu = jnp.mean(xf, axis=-1, keepdims=True)
    var = jnp.mean(jnp.square(xf - mu), axis=-1, keepdims=True)
    y = (xf - mu) * lax.rsqrt(var + LN_EPS) * g.astype(jnp.float32) + b.astype(jnp.float32)
    return y.astype(x.dtype)

def rms_norm(x, g):
    xf = x.astype(jnp.float32)
    y = xf * lax.rsqrt(jnp.mean(jnp.square(xf), axis=-1, keepdims=True) + RMS_EPS)
    return y * g.astype(jnp.float32)

def dsa_attention(q, c_kv, q_idx, k_idx, w_idx, kv_g, w_uk, w_uv):
    bsz, seq, _ = q.shape
    n_sel = min(TOPK_MAX, seq // 4)
    n_blk = seq // Q_BLOCK
    c = rms_norm(c_kv, kv_g)
    qh = q.reshape(bsz, seq, ATT_HEADS, ATT_HEAD_DIM)
    q_lat = jnp.einsum('bshd,hcd->bshc', qh, w_uk).astype(jnp.float32) * (ATT_HEAD_DIM ** -0.5)
    qi = q_idx.reshape(bsz, seq, IDX_HEADS, IDX_DIM).astype(jnp.float32) * (IDX_DIM ** -0.5)
    ki = k_idx.astype(jnp.float32)
    wi = w_idx.astype(jnp.float32) * (IDX_HEADS ** -0.5)
    key_pos = jnp.arange(seq, dtype=jnp.int32)
    neg = jnp.finfo(jnp.float32).min

    def to_blocks(a):
        return jnp.moveaxis(a.reshape(bsz, n_blk, Q_BLOCK, *a.shape[2:]), 1, 0)

    def block(args):
        blk, ql_b, qi_b, wi_b = args
        q_pos = blk * Q_BLOCK + jnp.arange(Q_BLOCK, dtype=jnp.int32)
        causal = key_pos[None, :] <= q_pos[:, None]
        idx_logits = jnp.einsum('bthd,bsd->bths', qi_b, ki)
        index_score = jnp.einsum('bths,bth->bts', jax.nn.relu(idx_logits), wi_b)
        index_score = jnp.where(causal[None], index_score, neg)
        _, sel = lax.top_k(index_score, n_sel)
        valid = sel <= q_pos[None, :, None]
        c_sel = jax.vmap(lambda cb, ib: cb[ib])(c, sel)
        s = jnp.einsum('bthc,btkc->bthk', ql_b, c_sel)
        s = jnp.where(valid[:, :, None, :], s, neg)
        p = jax.nn.softmax(s, axis=-1)
        return jnp.einsum('bthk,btkc->bthc', p, c_sel)

    o_lat = lax.map(block, (jnp.arange(n_blk, dtype=jnp.int32), to_blocks(q_lat), to_blocks(qi), to_blocks(wi)))
    o_lat = jnp.moveaxis(o_lat, 0, 1).reshape(bsz, seq, ATT_HEADS, KV_LATENT)
    out = jnp.einsum('bshc,hcd->bshd', o_lat.astype(w_uv.dtype), w_uv)
    return out.reshape(bsz, seq, ATT_WIDTH).astype(q.dtype)

def _ssm_combine(e_i, e_j):
    a_i, b_i = e_i
    a_j, b_j = e_j
    return a_j * a_i, a_j * b_i + b_j

def s5_branch(u, log_dt, a_re, a_im, b_re, b_im, c_re, c_im, d_skip, w_glu, b_glu):
    bsz, seq, _ = u.shape
    f32 = jnp.float32
    u32 = u.astype(f32).reshape(bsz, seq, N_GROUPS, GROUP_CH)
    lam = lax.complex(a_re.astype(f32), a_im.astype(f32))
    dt = jnp.exp(log_dt.astype(f32))[:, None]
    a_bar = jnp.exp(lam * dt)
    b_bar = ((a_bar - 1.0) / lam)[..., None] * lax.complex(b_re.astype(f32), b_im.astype(f32))
    c_mat = lax.complex(c_re.astype(f32), c_im.astype(f32))
    bu = jnp.einsum('bsgc,gpc->bsgp', u32.astype(jnp.complex64), b_bar)
    a_seq = jnp.broadcast_to(a_bar[None, None], (1, seq, N_GROUPS, STATE))
    _, states = lax.associative_scan(_ssm_combine, (a_seq, bu), axis=1)
    y = jnp.einsum('bsgp,gcp->bsgc', states, c_mat).real + d_skip.astype(f32) * u32
    y = jax.nn.gelu(y.reshape(bsz, seq, SSM_WIDTH))
    h = jnp.einsum('bsc,ce->bse', y, w_glu.astype(f32)) + b_glu.astype(f32)
    val, gate = jnp.split(h, 2, axis=-1)
    return (val * jax.nn.sigmoid(gate)).astype(u.dtype)

def hybrid_layer(x, w_in, kv_g, w_uk, w_uv, log_dt, a_re, a_im, b_re, b_im, c_re, c_im, d_skip, w_glu, b_glu, w_out, ln_g, ln_b):
    proj = jnp.einsum('bsd,de->bse', x, w_in)
    q, c_kv, q_idx, k_idx, w_idx, gate_a, u, gate_s = jnp.split(proj, _split_points(), axis=-1)
    att = dsa_attention(q, c_kv, q_idx, k_idx, w_idx, kv_g, w_uk, w_uv)
    ssm = s5_branch(u, log_dt, a_re, a_im, b_re, b_im, c_re, c_im, d_skip, w_glu, b_glu)
    mixed = jnp.concatenate([att * jax.nn.silu(gate_a), ssm * jax.nn.silu(gate_s)], axis=-1)
    y = jnp.einsum('bse,ed->bsd', mixed, w_out)
    return layer_norm(DEEPNORM_ALPHA * x + y, ln_g, ln_b)

def second_inputs(seed: int = 0) -> dict:
    key = jax.random.key(seed)
    ks = jax.random.split(key, 19)
    f = jnp.float32
    L = DEPTH_2
    nrm = jax.random.normal
    x = nrm(ks[0], (BATCH, SEQ, D_MODEL), f)
    w_in = nrm(ks[1], (L, D_MODEL, D_IN), f) * (D_MODEL ** -0.5)
    kv_norm_g = 1.0 + 0.1 * nrm(ks[2], (L, KV_LATENT), f)
    w_uk = nrm(ks[3], (L, ATT_HEADS, KV_LATENT, ATT_HEAD_DIM), f) * (KV_LATENT ** -0.5)
    w_uv = nrm(ks[4], (L, ATT_HEADS, KV_LATENT, ATT_HEAD_DIM), f) * (KV_LATENT ** -0.5) * DEEPNORM_BETA
    log_dt = jax.random.uniform(ks[5], (L, N_GROUPS), f, minval=math.log(DT_MIN), maxval=math.log(DT_MAX))
    n = jnp.arange(STATE, dtype=f)
    a_re = -0.5 + 0.01 * nrm(ks[6], (L, N_GROUPS, STATE), f)
    a_im = jnp.pi * n + 0.01 * nrm(ks[7], (L, N_GROUPS, STATE), f)
    b_re = nrm(ks[8], (L, N_GROUPS, STATE, GROUP_CH), f) * ((2 * GROUP_CH) ** -0.5)
    b_im = nrm(ks[9], (L, N_GROUPS, STATE, GROUP_CH), f) * ((2 * GROUP_CH) ** -0.5)
    c_re = nrm(ks[10], (L, N_GROUPS, GROUP_CH, STATE), f) * ((2 * STATE) ** -0.5)
    c_im = nrm(ks[11], (L, N_GROUPS, GROUP_CH, STATE), f) * ((2 * STATE) ** -0.5)
    d_skip = nrm(ks[12], (L, N_GROUPS, GROUP_CH), f)
    w_glu = nrm(ks[13], (L, SSM_WIDTH, 2 * SSM_WIDTH), f) * (SSM_WIDTH ** -0.5)
    b_glu = 0.01 * nrm(ks[14], (L, 2 * SSM_WIDTH), f)
    w_out = nrm(ks[15], (L, D_MIX, D_MODEL), f) * (D_MIX ** -0.5) * DEEPNORM_BETA
    ln_g = 1.0 + 0.1 * nrm(ks[16], (L, D_MODEL), f)
    ln_b = 0.01 * nrm(ks[17], (L, D_MODEL), f)
    return {'x': x, 'w_in': w_in, 'kv_norm_g': kv_norm_g, 'w_uk': w_uk, 'w_uv': w_uv,
            'log_dt': log_dt, 'a_re': a_re, 'a_im': a_im, 'b_re': b_re, 'b_im': b_im,
            'c_re': c_re, 'c_im': c_im, 'd_skip': d_skip, 'w_glu': w_glu, 'b_glu': b_glu,
            'w_out': w_out, 'ln_g': ln_g, 'ln_b': ln_b}

def second_block(x, w_in, kv_norm_g, w_uk, w_uv, log_dt, a_re, a_im, b_re, b_im, c_re, c_im, d_skip, w_glu, b_glu, w_out, ln_g, ln_b):
    h = x
    for l in range(DEPTH_2):
        h = hybrid_layer(h, w_in[l], kv_norm_g[l], w_uk[l], w_uv[l], log_dt[l], a_re[l], a_im[l],
                         b_re[l], b_im[l], c_re[l], c_im[l], d_skip[l], w_glu[l], b_glu[l],
                         w_out[l], ln_g[l], ln_b[l])
    return h


def setup_inputs(seed=0):
    out = dict(first_inputs(seed))
    for name, value in second_inputs(seed + 1).items():
        if name != "x":
            out[name + "_2"] = value
    return out


def reference(
    x, norm_g, w_in, q_latent_g, kv_latent_g, w_uq, w_ukv, q_head_g, k_head_g, w_attn_proj,
    w_fourier_proj, b_merge, w_out, w_in_2, kv_norm_g_2, w_uk_2, w_uv_2, log_dt_2, a_re_2,
    a_im_2, b_re_2, b_im_2, c_re_2, c_im_2, d_skip_2, w_glu_2, b_glu_2, w_out_2, ln_g_2, ln_b_2,
):
    x = first_block(
        x, norm_g, w_in, q_latent_g, kv_latent_g, w_uq, w_ukv, q_head_g, k_head_g, w_attn_proj,
        w_fourier_proj, b_merge, w_out,
    )
    return second_block(
        x, w_in_2, kv_norm_g_2, w_uk_2, w_uv_2, log_dt_2, a_re_2, a_im_2, b_re_2, b_im_2,
        c_re_2, c_im_2, d_skip_2, w_glu_2, b_glu_2, w_out_2, ln_g_2, ln_b_2,
    )


_drawn_inputs = setup_inputs


def setup_inputs(seed=0):
    import zlib

    import numpy as np

    out = dict(_drawn_inputs(seed))
    spreads = {}
    factors = {'norm_g': 4.479,
     'q_latent_g': 8.0,
     'kv_latent_g': 8.0,
     'w_uq': 3.597,
     'w_ukv': 3.25,
     'q_head_g': 8.0,
     'k_head_g': 8.0,
     'w_attn_proj': 3.245,
     'b_merge': 8.0,
     'kv_norm_g_2': 8.0,
     'w_uk_2': 3.288,
     'w_uv_2': 2.678,
     'log_dt_2': 64.0,
     'a_re_2': 64.0,
     'a_im_2': 64.0,
     'b_re_2': 64.0,
     'b_im_2': 64.0,
     'c_re_2': 64.0,
     'c_im_2': 64.0,
     'b_glu_2': 64.0,
     'ln_b_2': 5.699}
    for name, (base, spread) in spreads.items():
        noise = np.random.default_rng([zlib.crc32(name.encode()), seed]).standard_normal(out[name].shape)
        drawn = base * np.exp(spread * noise) if base else spread * noise
        out[name] = __import__('jax').numpy.asarray(drawn.astype(out[name].dtype))
    for name, factor in factors.items():
        out[name] = (out[name] * factor).astype(out[name].dtype)
    return out
```

```python
from contextlib import ExitStack

import numpy as np

import concourse.bass as bass
from concourse import mybir

ALU = mybir.AluOpType
ACT = mybir.ActivationFunctionType
AX = mybir.AxisListType
F32 = mybir.dt.float32

P = 128
S = 1024
D = 1024
NT = S // P
KD = D // P
L = 2
H = 8
QL = KVL = 256
NOPE, ROPE, VD = 64, 32, 64
QK = NOPE + ROPE
HR = ROPE // 2
AW = H * VD
FW = 512
FG = FW // P
EPS = 1e-6
C_PE, C_ZA, C_U, C_ZF = 512, 544, 1056, 1568
C_GA, C_GF = 2080, 3104
UNITS = H * NT
N_ROWS = KD + 4 + 2 * KD

ROUND = [1 + 2 * NT, NT + 1, 8, NT, 4 * NT, NT, 8, NT, 8, 8, 8 * KD, 2 * NT]
FIXED = [UNITS // 2, 0, UNITS // 2, 0, UNITS, UNITS, H, 4 * H]
BANK_USES = [sum((n + 7 - b) // 8 for n in ROUND) + FIXED[b] for b in range(8)]

CHUNKS = [(1, "c"), (1, "u"), (2, "up"), (1, "dft0"), (1, "dft1"), (1, "za"), (1, "zf")]
CHUNKS += [(4, f"gate{m}") for m in range(KD)] + [(1, "out0"), (1, "out1")]
CHUNKS += [(0, "pad")] * (len(CHUNKS) % 2)
W_SLOTS = 2
W_DMAS = [sum(n for n, _ in CHUNKS[s::W_SLOTS]) for s in range(W_SLOTS)]
W_TAKES = [sum(n > 0 for n, _ in CHUNKS[s::W_SLOTS]) for s in range(W_SLOTS)]

KVC = 128
IH, ID = 8, 32
TOPK = 256
CH, NG, NST = 16, 32, 64
SW = CH * NG
CL = 8
NC = S // CL
NPAIR = NG // 2
HP = NPAIR // 4
ALPHA = 2 ** 0.25
LN_EPS = 1e-5
MASKED = -3.0e38
TAKEN = -3.4e38
C2_C, C2_GA, C2_U, C2_GS = 512, 936, 1448, 1960
NIDX = C2_GA - C2_C
S5_LOADS = 4 + 2
CHUNKS2 = ["idx", "u", "ga", "gs", "glu", "q", "out0", "out1"]


class Banks:

    def __init__(self, full, free):
        self.full, self.free = full, free
        self.n = [1] * 8
        self.layer = None

    def enter(self, layer):
        self.layer, self.start = layer, list(self.n)

    def leave(self, layers):
        assert [n - s for n, s in zip(self.n, self.start)] == BANK_USES, (self.n, self.start, BANK_USES)
        self.layer = None
        self.n = [s + layers * u for s, u in zip(self.start, BANK_USES)]

    def count(self, b):
        return self.n[b] if self.layer is None else self.layer * BANK_USES[b] + self.n[b]

    def take(self, b):
        self.n[b] += 1
        return self.count(b) - 1 if self.layer is None else self.layer * BANK_USES[b] + (self.n[b] - 1)

    def skip(self, n):
        for i in range(n):
            self.n[i % 8] += 1


class Steps:

    def __init__(self, eng, sem):
        self.eng, self.sem, self.n, self.layer, self.per = eng, sem, 0, None, 0

    def enter(self, layer, per):
        self.layer, self.per, self.start = layer, per, self.n

    def leave(self, layers):
        assert self.n - self.start == self.per, (self.n - self.start, self.per)
        self.layer, self.n = None, self.start + layers * self.per

    def done(self, ins):
        ins.then_inc(self.sem, 1)
        self.n += 1

    def wait(self):
        self.eng.wait_ge(self.sem, self.n if self.layer is None else self.layer * self.per + self.n)

    def link(self, ins):
        self.done(ins)
        self.wait()


def build(nc, a, out, dbg=None):
    with ExitStack() as ctx:
        def sb(name, shape, dt=F32):
            return ctx.enter_context(nc.sbuf_tensor(name, shape, dt))

        def sem(name):
            return ctx.enter_context(nc.semaphore(name))

        PS = ctx.enter_context(nc.psum_tensor("PS", [P, 8, 512], F32))

        hT = sb("hT", [P, KD, S])
        R0 = sb("R0", [P, 8, 1024])
        R1 = sb("R1", [P, 8, 1024])
        R2a = sb("R2a", [P, 4, 1024])
        R2b = sb("R2b", [P, 4, 1024])
        R3a = sb("R3a", [P, 4, 1024])
        R3b = sb("R3b", [P, 4, 1024])
        W = sb("W", [P, W_SLOTS, 4096])
        wpe = sb("wpe", [P, KD, ROPE])
        ident = sb("ident", [P, P])
        dft_d = sb("dft_d", [P, 2 * P])
        u_mid = sb("u_mid", [P, FG, P])
        cosT = sb("cosT", [P, NT, HR])
        sinT = sb("sinT", [P, NT, HR])
        eps = sb("eps", [P, 1])
        rows = sb("rows", [P, P])
        pT = sb("pT", [P, N_ROWS])
        gq = sb("gq", [P, QK])
        gk = sb("gk", [P, QK])
        ssx = sb("ssx", [P, NT])
        rsx = sb("rsx", [P, NT])
        ssc = sb("ssc", [P, 2 * NT])
        rsc = sb("rsc", [P, 2 * NT])
        ssh = sb("ssh", [P, 2, NT, H])
        rsh = sb("rsh", [P, 2, NT, H])
        kss = sb("kss", [P, NT])
        kpe = sb("kpe", [P, NT, ROPE])
        kro = sb("kro", [P, NT, ROPE])
        rt = sb("rt", [P, 4, NT, HR])
        rtp = sb("rtp", [P, 4, NT, HR])
        negm = sb("negm", [P, UNITS])
        rsum = sb("rsum", [P, UNITS])
        rinv = sb("rinv", [P, UNITS])

        mark = sb("mark", [P, 1])
        epsl = sb("epsl", [P, 1])

        x1 = R1
        xn = [R2a[:, t, :] if t < 4 else R2b[:, t - 4, :] for t in range(NT)]
        c_tok = R2a[:, :, :].rearrange("p a b -> p (a b)").rearrange("p (t c) -> p t c", t=NT)
        cT = R2b
        uT = R3a
        fold = R3b[:, :, :].rearrange("p a b -> p (a b)").rearrange("p (g e s) -> p g e s", g=FG, e=2)
        V = R3a[:, :, :].rearrange("p a b -> p (a b)").rearrange("p (j c) -> p j c", j=NT)
        fT = R3b
        r0 = R0[:, :, :].rearrange("p a b -> p (a b)")
        r1 = R1[:, :, :].rearrange("p a b -> p (a b)")
        q_tok = r0[:, 0:NT * H * QK].rearrange("p (t c) -> p t c", t=NT)
        stage = r0[:, NT * H * QK:NT * H * QK + 2 * NT * QK].rearrange("p (s t c) -> p s t c", s=2, t=NT)
        tmp = r0[:, NT * H * QK:NT * H * QK + 1024].rearrange("p (i c) -> p i c", i=2)
        k_tok = r1[:, 0:4096].rearrange("p (t h c) -> p t h c", t=NT, h=H)
        v_tok = r1[:, 4096:8192].rearrange("p (t h c) -> p t h c", t=NT, h=H)
        r2a = R2a[:, :, :].rearrange("p a b -> p (a b)")
        o_tok = r2a.rearrange("p (t c) -> p t c", t=NT)
        Pb = [R2b[:, 0, :], R2b[:, 1, :]]
        PT = [R2b[:, 2, :], R2b[:, 3, :]]
        qT = [R3a[:, 0, :], R3a[:, 1, :]]
        kT = [R3a[:, 2, :], R3a[:, 3, :]]
        oT = R2b
        mT = R0
        sg = R3a[:, :, :].rearrange("p a b -> p (a b)").rearrange("p (i c) -> p i c", c=512)

        def flat(t):
            return t[:, :, :].rearrange("p a b -> p (a b)")

        r3a, r3b, r2b, hTf = flat(R3a), flat(R3b), flat(R2b), flat(hT)
        xT = hT
        sel, at = [], 0
        for t in range(NT):
            w = (t + 1) * P
            half, lo = (r2a, at) if t < 7 else (r2b, 0)
            sel.append(half[:, lo:lo + w])
            at += w
        c2 = r2b[:, 1024:2048].rearrange("p (t c) -> p t c", t=NT)
        c2T = r2b[:, 2048:3072]
        kiT = r2b[:, 3072:4096]
        qiT = r3a[:, 0:2048].rearrange("p (m s) -> p m s", m=2)
        rl = [r3a[:, 2048:3072], r3a[:, 3072:4096]]
        wtok = ssh[:, 0, :, :]
        m8 = ssc[:, 0:8]
        U = r0[:, 0:4096].rearrange("p (j c) -> p j c", j=CL)
        U4 = r0[:, 0:4096].rearrange("p (g j c) -> p g j c", g=NG, j=CL)
        Y = U
        UT = r0[:, 4096:8192].rearrange("p (g c) -> p g c", g=NG)
        yT = r0[:, 4096:8192].rearrange("p (k s) -> p k s", k=4)
        prow = r3b[:, 3328:3712].rearrange("p (i c) -> p i c", i=3)
        lrow = r3b[0:NPAIR, 3712:3714]
        drow = r3b[0:NG, 3716:3716 + CH]
        craw = r3b[:, 0:1024].rearrange("p (i c) -> p i c", i=8)
        lam = r3b[:, 1024:1072].rearrange("p (i q) -> p i q", i=3)
        scr = r3b[:, 1088:1088 + 40 * NPAIR].rearrange("p (i q) -> p i q", i=40)
        CT = flat(u_mid).rearrange("p (i q c) -> p i q c", i=2, q=NPAIR)
        Bb = rt[:, :, :, :].rearrange("p a b c -> p (a b c)").rearrange("p (i q c) -> p i q c", i=2, q=NPAIR)
        Braw = r3b[:, 1728:2240].rearrange("p (i q c) -> p i q c", i=2, q=NPAIR)
        s5c = gk[:, 0:3 * NPAIR].rearrange("p (i q) -> p i q", i=3)
        apow = kpe[:, :, :].rearrange("p a b -> p (a b)").rearrange("p (i q j) -> p i q j", i=2, q=NPAIR)

        def part(t, lo, f, n=1024):
            return t[:, lo + n * (f % 2):lo + n * (f % 2) + n]

        G = [part(r3b, 0, f).rearrange("p (i q j c) -> p i q j c", i=2, q=HP, j=CL) for f in range(2)]
        st_ = [part(r3b, 0, f).rearrange("p (i q c) -> p i q c", i=2, q=HP) for f in range(2)]
        M1 = [part(r3b, 2048, f).rearrange("p (i q c) -> p i q c", i=2, q=HP) for f in range(2)]
        X = M1
        K16 = [part(r3a, 0, f)[0:CH].rearrange("p (g c) -> p g c", g=2 * HP) for f in range(2)]
        rot = [part(r3a, 0, f).rearrange("p (i q c) -> p i q c", i=2, q=HP) for f in range(2)]
        TT = [part(r3a, 2048, f).rearrange("p (g c) -> p g c", g=2 * HP) for f in range(2)]
        ca_re = [part(r2b, 3072, f, 512).rearrange("p (q i c) -> p q i c", q=HP, i=CL) for f in range(2)]
        ca_ni = [x.rearrange("p (q i c) -> p q i c", q=HP, i=CL) for x in
                 (r2a[:, 3584:4096], rtp[:, :, :, :].rearrange("p a b c -> p (a b c)"))]
        mix = R1
        DT = rinv[0:CH, 0:NG]
        dtmp = kro[0:CH, 0:2 * HP, 0:CH]
        vb = [r3b[:, 0:512], r3b[:, 512:1024]]
        gb = [r3b[:, 1024:1536], r3b[:, 1536:2048]]
        kvg = wpe[:, :, :].rearrange("p a b -> p (a b)")[:, 0:KVC]
        qT2 = R3a
        wuk = r3b[:, 2048:2560]
        wukT = CT.rearrange("p i q c -> p (i q c)").rearrange("p (m c) -> p m c", m=4)
        wuv = Bb.rearrange("p i q c -> p (i q c)").rearrange("p (h d) -> p h d", h=H)
        qlT = R0
        Pb2 = [r3b[:, 0:1024], r3b[:, 1024:2048]]
        xt = [r3b[:, 2048:3072], r3b[:, 3072:4096]]
        lng, lnb = r3a[:, 0:1024], r3a[:, 1024:2048]
        att = [r3a[:, 2048:2560], r3a[:, 2560:3072]]
        olT = [r3a[:, 3072:3584], r3a[:, 3584:4096]]
        PT2 = [hTf[:, i * 4096:(i + 1) * 4096].rearrange("p (k c) -> p k c", k=NT) for i in range(2)]
        tri = dft_d[:, 0:P]
        ki4 = r3b[:, 2304:2304 + KD * 4 * ID].rearrange("p (k c) -> p k c", k=KD)

        xres = nc.dram_tensor("xres", (S, D), F32, kind="Internal").ap()

        full = [sem(f"bank_full{b}") for b in range(8)]
        free = [sem(f"bank_free{b}") for b in range(8)]
        w_in_slot = [sem(f"w_loaded{s}") for s in range(W_SLOTS)]
        w_used = [sem(f"w_used{s}") for s in range(W_SLOTS)]
        s_const = sem("constants_loaded")
        s_xin = sem("x_loaded")
        s_par = sem("parameters_loaded")
        s_wpe = sem("wpe_loaded")
        s_xsave = sem("x_saved")
        s_xback = sem("x_reloaded")
        s_init = sem("memsets_done")
        s_std = sem("x_std_ready")
        s_xn = sem("x_normed")
        s_hT = sem("hT_ready")
        s_pT = sem("parameters_turned")
        s_c = sem("c_evacuated")
        s_cstd = sem("c_std_ready")
        s_cn = sem("c_normed")
        s_cT = sem("cT_ready")
        s_kpe = sem("kpe_evacuated")
        s_uT = sem("uT_ready")
        s_fold = sem("folded")
        s_V = sem("spectrum_ready")
        s_fT = sem("fT_ready")
        s_sq = sem("head_squares_ready")
        s_ss = sem("head_sums_ready")
        s_q = sem("q_evacuated")
        s_ssall = sem("all_head_sums_ready")
        s_hstd = sem("head_std_ready")
        s_hrs = sem("head_rstd_ready")
        s_stage = sem("qk_staged")
        s_qkT = sem("qkT_ready")
        s_nm = sem("neg_max_ready")
        s_o = sem("head_output_ready")
        s_oT = sem("oT_ready")
        s_silu = sem("silu_ready")
        s_sm = sem("silu_multiplied")
        s_sig = sem("sigmoid_ready")
        s_sigused = sem("sigmoid_used")
        s_mT = sem("mT_ready")
        s_xnew = sem("x_new_ready")
        s2_par = sem("second_parameters_loaded")
        s2_rows = sem("second_rows_loaded")
        s2_ld = sem("log_dt_spread")
        s2_ki = sem("indexer_key_weights_repeated")
        s2_c = sem("second_latent_normed")
        s2_relu = sem("index_relu_ready")
        s2_acc = sem("index_relu_added")
        s2_sel = sem("selection_ready")
        s2_prep = sem("s5_parameters_ready")
        s2_G = sem("s5_input_powers_ready")
        s2_CA = sem("s5_output_powers_ready")
        s2_K = sem("s5_kernel_ready")
        s2_TT = [sem(f"s5_toeplitz_loaded{i}") for i in range(2)]
        s2_TT0 = sem("s5_toeplitz_zeroed")
        s2_w = sem("s5_states_turned_back")
        s2_z = sem("s5_scanned")
        s2_X = sem("s5_states_ready")
        s2_glu = sem("glu_ready")
        s2_wk = sem("wuk_loaded")
        s2_wv = sem("wuv_loaded")
        s2_ln = sem("ln_parameters_loaded")
        s2_nm = sem("masked_scores_ready")
        s2_xt = [sem(f"x_tile_loaded{i}") for i in range(2)]
        s2_r = sem("centred_ready")
        s2_sq = sem("ln_std_ready")
        s2_o = sem("out_tile_ready")
        s2_od = [sem(f"out_tile_written{i}") for i in range(2)]
        s_dve = sem("dve_steps")
        s_act = sem("act_steps")
        s_pool = sem("pool_steps")
        s_out = sem("output_written")

        marks = {}
        block = ctx.enter_context(nc.Block())

        @block.tensor
        def _(pe):
            bk = Banks(full, free)
            pe.wait_ge(s_const, 64)
            pe.wait_ge(s_init, 3)

            def begin(b):
                pe.wait_ge(free[b], bk.take(b))
                return PS[:, b, :]

            def weights(l, i):
                s = i % W_SLOTS
                pe.wait_ge(w_in_slot[s], 16 * (l * W_DMAS[s] + sum(n for n, _ in CHUNKS[s:i + 1:W_SLOTS])))
                return W[:, s, :]

            def k_of(slot):
                return slot.rearrange("p (k c) -> p k c", k=8)

            with pe.Fori(0, L) as l:
                bk.enter(l)
                pe.wait_ge(s_par, 96 * l + 96)
                b0 = begin(0)
                pe.transpose(b0[:, 0:P], rows[:, :], ident[:, :]).then_inc(full[0], 1)
                hT_free = []
                for t in range(NT):
                    pe.wait_ge(s_xn, l * NT + t + 1)
                    for j in range(2):
                        b = (1 + 2 * t + j) % 8
                        o = begin(b)
                        for k in range(4):
                            f = 4 * j + k
                            mm = pe.transpose(o[:, k * P:(k + 1) * P], xn[t][:, f * P:(f + 1) * P], ident[:, :])
                        mm.then_inc(full[b], 1)
                    hT_free.append((b, bk.count(b)))
                wc = k_of(weights(l, 0))
                for t in range(NT):
                    pe.wait_ge(free[hT_free[t][0]], hT_free[t][1])
                    o = begin(t % 8)
                    for k in range(KD):
                        mm = pe.matmul(o, hT[:, k, t * P:(t + 1) * P], wc[:, k, :], start=(k == 0), stop=(k == 7))
                    mm.then_inc(full[t % 8], 1)
                pe.wait_ge(s_wpe, 16 * l + 16)
                o = begin(0)
                for t in range(NT):
                    for k in range(KD):
                        mm = pe.matmul(o[:, t * ROPE:(t + 1) * ROPE], hT[:, k, t * P:(t + 1) * P], wpe[:, k, :],
                                       start=(k == 0), stop=(k == 7))
                mm.then_inc(full[0], 1)
                wu = k_of(weights(l, 1))
                for m in range(4):
                    for n in range(2):
                        b = 2 * m + n
                        o = begin(b)
                        for k in range(KD):
                            mm = pe.matmul(o, wu[:, k, m * P:(m + 1) * P], hT[:, k, n * 512:(n + 1) * 512],
                                           start=(k == 0), stop=(k == 7))
                            if m == n == k == 0:
                                mm.then_inc(w_used[0], 1)
                        mm.then_inc(full[b], 1)
                for t in range(NT):
                    pe.wait_ge(s_cn, l * NT + t + 1)
                    o = begin(t % 8)
                    for k in range(4):
                        mm = pe.transpose(o[:, k * P:(k + 1) * P], c_tok[:, t, k * P:(k + 1) * P], ident[:, :])
                        if t == k == 0:
                            mm.then_inc(w_used[1], 1)
                    mm.then_inc(full[t % 8], 1)
                cT_free = [bk.count(b) for b in range(8)]
                wup = weights(l, 2)
                wq = wup[:, 0:2 * H * QK].rearrange("p (k c) -> p k c", k=2)
                wkv = wup[:, 2 * H * QK:2 * H * QK + 2048].rearrange("p (k c) -> p k c", k=2)
                for t in range(NT):
                    pe.wait_ge(free[t], cT_free[t])
                    for j in range(4):
                        b = (4 * t + j) % 8
                        o = begin(b)
                        for k in range(2):
                            if j < 2:
                                mm = pe.matmul(o[:, 0:4 * QK], cT[:, k, t * P:(t + 1) * P],
                                               wq[:, k, j * 4 * QK:(j + 1) * 4 * QK], start=(k == 0), stop=(k == 1))
                            else:
                                mm = pe.matmul(o, cT[:, 2 + k, t * P:(t + 1) * P],
                                               wkv[:, k, (j - 2) * 512:(j - 1) * 512], start=(k == 0), stop=(k == 1))
                        mm.then_inc(full[b], 1)
                pe.wait_ge(s_fold, l + 1)
                for j in range(NT):
                    o = begin(j % 8)
                    e, s0 = j // 4, (j % 4) * P
                    for g in range(FG):
                        og = o[:, g * P:(g + 1) * P]
                        mm = pe.matmul(og, fold[:, g, e, s0:s0 + P], dft_d[:, e * P:(e + 1) * P],
                                       start=True, stop=(j != 4))
                        if j == g == 0:
                            mm.then_inc(w_used[0], 1)
                        if j == 4:
                            mm = pe.matmul(og, u_mid[:, g, :], dft_d[:, 0:P], start=False, stop=True)
                    mm.then_inc(full[j % 8], 1)
                pe.wait_ge(free[7], bk.count(7))
                for n in range(2):
                    wd = k_of(weights(l, 3 + n))
                    for g in range(FG):
                        b = 4 * n + g
                        o = begin(b)
                        for j in range(NT):
                            mm = pe.matmul(o, V[:, j, g * P:(g + 1) * P], wd[:, j, :], start=(j == 0), stop=(j == 7))
                            if n == 1 and g == j == 0:
                                mm.then_inc(w_used[1], 1)
                        mm.then_inc(full[b], 1)

                def qk_turn(h, i):
                    pe.wait_ge(s_stage, l * 2 * H + 2 * h + i // 2 + 1)
                    o = begin(7)
                    for j in range(4):
                        t = 4 * (i % 2) + j
                        mm = pe.transpose(o[0:QK, j * P:(j + 1) * P], stage[:, i // 2, t, :], ident[:, :])
                        if h == i == j == 0:
                            mm.then_inc(w_used[0], 1)
                    mm.then_inc(full[7], 1)

                def scores(u):
                    h, t = u // NT, u % NT
                    b = 2 * (u % 2)
                    if u < 2:
                        pe.wait_ge(free[b + 1], bk.count(b + 1))
                    begin(b)
                    if t == 0:
                        pe.wait_ge(free[7], bk.count(7))
                    for n in range(2):
                        mm = pe.matmul(PS[:, b + n, :], qT[h % 2][0:QK, t * P:(t + 1) * P],
                                       kT[h % 2][0:QK, n * 512:(n + 1) * 512], start=True, stop=True)
                    mm.then_inc(full[b], 1)

                def p_turn(u):
                    pe.wait_ge(free[2 * (u % 2)], bk.count(2 * (u % 2)))
                    for j in range(2):
                        o = begin(4 + j)
                        for k in range(4):
                            c = 4 * j + k
                            mm = pe.transpose(o[:, k * P:(k + 1) * P], Pb[u % 2][:, c * P:(c + 1) * P], ident[:, :])
                        mm.then_inc(full[4 + j], 1)
                    pt_count.append((bk.count(4), bk.count(5)))

                def pv(u):
                    h, t = u // NT, u % NT
                    if t == 0:
                        begin(6)
                    pe.wait_ge(free[4], pt_count[u][0])
                    pe.wait_ge(free[5], pt_count[u][1])
                    for k in range(NT):
                        mm = pe.matmul(PS[:, 6, t * VD:(t + 1) * VD], PT[u % 2][:, k * P:(k + 1) * P],
                                       v_tok[:, k, h, :], start=(k == 0), stop=(k == 7))
                    if t == NT - 1:
                        mm.then_inc(full[6], 1)

                pt_count = []
                for i in range(4):
                    qk_turn(0, i)
                scores(0)
                for u in range(UNITS + 1):
                    if u + 1 < UNITS:
                        scores(u + 1)
                    if u < UNITS:
                        p_turn(u)
                    if u >= 1:
                        pv(u - 1)
                    if 1 <= u % NT <= 4 and u // NT + 1 < H:
                        qk_turn(u // NT + 1, u % NT - 1)

                pe.wait_ge(s_o, l + 1)
                for t in range(NT):
                    o = begin(t % 8)
                    for k in range(4):
                        mm = pe.transpose(o[:, k * P:(k + 1) * P], o_tok[:, t, k * P:(k + 1) * P], ident[:, :])
                    mm.then_inc(full[t % 8], 1)
                for i in (5, 6):
                    wz = k_of(weights(l, i))
                    for m in range(4):
                        for n in range(2):
                            b = 2 * m + n
                            o = begin(b)
                            for k in range(KD):
                                mm = pe.matmul(o, wz[:, k, m * P:(m + 1) * P], hT[:, k, n * 512:(n + 1) * 512],
                                               start=(k == 0), stop=(k == 7))
                                if i == 6 and m == n == k == 0:
                                    mm.then_inc(w_used[1], 1)
                            mm.then_inc(full[b], 1)
                pe.wait_ge(s_sm, l * 16 + 16)
                for m in range(KD):
                    g = weights(l, 7 + m)[:, 0:24 * P].rearrange("p (k c) -> p k c", c=P)
                    first = True
                    for n in range(2):
                        for br in range(4):
                            b = 4 * n + br
                            o = begin(b)
                            k0, nk, rhs = [(0, 8, hT), (8, 8, hT), (16, 4, oT), (20, 4, fT)][br]
                            for k in range(nk):
                                mm = pe.matmul(o, g[:, k0 + k, :], rhs[:, k, n * 512:(n + 1) * 512],
                                               start=(k == 0), stop=(k == nk - 1))
                                if first:
                                    mm.then_inc(w_used[(6 + m) % W_SLOTS], 1)
                                    first = False
                            mm.then_inc(full[b], 1)
                for n in range(2):
                    wo = k_of(weights(l, 15 + n))
                    for t in range(NT):
                        b = t % 8
                        o = begin(b)
                        if n == 0 and t == 0:
                            pe.wait_ge(s_mT, l * 16 + 16)
                        for k in range(KD):
                            mm = pe.matmul(o, mT[:, k, t * P:(t + 1) * P], wo[:, k, :], start=(k == 0), stop=(k == 7))
                            if t == k == 0:
                                mm.then_inc(w_used[(14 + n) % W_SLOTS], 1)
                        mm.then_inc(full[b], 1)
                pe.wait_ge(free[7], bk.count(7))
                pe.nop().then_inc(w_used[0], 1)
            bk.leave(L)

            def weights2(i):
                sl = i % W_SLOTS
                pe.wait_ge(w_in_slot[sl], 16 * (L * W_DMAS[sl] + i // W_SLOTS + 1))
                return W[:, sl, :]

            pe.wait_ge(s_xnew, L + 1)
            for t in range(NT):
                for j in range(2):
                    b = (2 * t + j) % 8
                    o = begin(b)
                    for k in range(4):
                        f = 4 * j + k
                        mm = pe.transpose(o[:, k * P:(k + 1) * P], x1[:, t, f * P:(f + 1) * P], ident[:, :])
                    mm.then_inc(full[b], 1)
            x_done = [bk.count(b) for b in range(8)]
            pe.wait_ge(s2_rows, 16 * 7)
            pe.wait_ge(s2_ld, 1)
            o = begin(0)
            for i in range(3):
                pe.transpose(o[:, i * NPAIR:(i + 1) * NPAIR], prow[0:NPAIR, i, :], ident[0:NPAIR, 0:NPAIR])
            pe.transpose(o[0:CH, 64:64 + NG], drow, ident[0:NG, 0:NG])
            pe.transpose(o[:, P:P + KD], rows[0:KD, :], ident[0:KD, 0:KD]).then_inc(full[0], 1)
            wi = weights2(0)[:, 0:KD * NIDX].rearrange("p (k c) -> p k c", k=KD)
            for b in range(8):
                pe.wait_ge(free[b], x_done[b])
            for i in range(6):
                m, n = i // 2, i % 2
                if i == 4:
                    pe.wait_ge(s2_ki, 1)
                o = begin(i)
                for k in range(KD):
                    if m < 2:
                        w = wi[:, k, KVC + m * P:KVC + (m + 1) * P]
                    else:
                        w = ki4[:, k, :]
                    mm = pe.matmul(o, w, xT[:, k, n * 512:(n + 1) * 512], start=(k == 0), stop=(k == 7))
                mm.then_inc(full[i], 1)
            for t in range(NT):
                b = (6 + t) % 8
                o = begin(b)
                for c0, w in ((0, KVC), (KVC + IH * ID + ID, IH)):
                    p0 = 0 if w == KVC else KVC
                    for k in range(KD):
                        mm = pe.matmul(o[:, p0:p0 + w], xT[:, k, t * P:(t + 1) * P], wi[:, k, c0:c0 + w],
                                       start=(k == 0), stop=(k == 7))
                mm.then_inc(full[b], 1)
            pe.wait_ge(s2_par, 16 * S5_LOADS)
            for i in range(2):
                b = (7 + i) % 8
                o = begin(b)
                for k in range(4):
                    mm = pe.transpose(o[:, k * P:(k + 1) * P], craw[:, 4 * i + k, :], ident[:, :])
                mm.then_inc(full[b], 1)
            marks["C"] = (bk.count(7), bk.count(0))
            for b in range(8):
                pe.wait_ge(free[b], bk.count(b))
            for v in range((NT - 2) * IH):
                t, h = 2 + v // IH, v % IH
                b = 2 * (v % 4)
                begin(b)
                w = (t + 1) * P
                r0_ = 32 * (h % 4)
                for n in range((w + 511) // 512):
                    mm = pe.matmul(PS[:, b + n, 0:min(512, w - 512 * n)],
                                   qiT[r0_:r0_ + ID, h // 4, t * P:(t + 1) * P],
                                   kiT[r0_:r0_ + ID, n * 512:min(w, n * 512 + 512)], start=True, stop=True)
                    if n == 0 and w > 512 and v == 2 * IH:
                        mm.then_inc(w_used[0], 1)
                mm.then_inc(full[b], 1)
            for b in range(0, 8, 2):
                pe.wait_ge(free[b], bk.count(b))
            for j in range(2):
                o = begin(j)
                for k in range(4):
                    t = 4 * j + k
                    pe.wait_ge(s2_c, t + 1)
                    mm = pe.transpose(o[:, k * P:(k + 1) * P], c2[:, t, :], ident[:, :])
                mm.then_inc(full[j], 1)
            wu = k_of(weights2(1))
            for j in range(CL):
                o = begin(j)
                for k in range(KD):
                    mm = pe.matmul(o, xT[:, k, j:S:CL], wu[:, k, :], start=(k == 0), stop=(k == 7))
                mm.then_inc(full[j], 1)
            for b in range(8):
                pe.wait_ge(free[b], bk.count(b))
            for b in range(8):
                o = begin(b)
                for k in range(4):
                    g = 4 * b + k
                    mm = pe.transpose(o[:, k * P:(k + 1) * P], r0[:, g * P:(g + 1) * P], ident[:, :])
                    if b == k == 0:
                        mm.then_inc(w_used[1], 1)
                mm.then_inc(full[b], 1)

            def gates(i, last):
                wz = k_of(weights2(i))
                for m in range(4):
                    for n in range(2):
                        b = 2 * m + n
                        o = begin(b)
                        for k in range(KD):
                            mm = pe.matmul(o, wz[:, k, m * P:(m + 1) * P], xT[:, k, n * 512:(n + 1) * 512],
                                           start=(k == 0), stop=(k == 7))
                            if m == n == k == 0 and last is not None:
                                mm.then_inc(w_used[last], 1)
                        mm.then_inc(full[b], 1)

            def s5_a(f):
                p = f % 2
                pe.wait_ge(s2_G, f + 1)
                for i in range(2):
                    o = begin(i)
                    for q in range(HP):
                        mm = pe.transpose(o[:, q * P:(q + 1) * P], G[p][:, i, q, :, :], ident[:, :])
                    mm.then_inc(full[i], 1)
                m1 = bk.count(1)
                pe.wait_ge(s2_CA, f + 1)
                for i in range(2):
                    o = begin(2 + i)
                    for k in range(HP):
                        q, r_ = k, slice(NST * i, NST * i + NST)
                        qq = f * HP + q
                        for (lo, hi, cr, ci) in ((0, CH, CT[r_, 0, qq, :], CT[r_, 1, qq, :]),
                                                 (CH, P, ca_re[p][r_, q, 0:CL - 1, :], ca_ni[p][r_, q, 0:CL - 1, :])):
                            oo = o[0:CH, k * P + lo:k * P + hi]
                            pe.matmul(oo, Bb[r_, 0, qq, :], cr, start=True, stop=False)
                            mm = pe.matmul(oo, Bb[r_, 1, qq, :], ci, start=False, stop=True)
                    mm.then_inc(full[2 + i], 1)
                pe.wait_ge(free[1], m1)
                for i in range(2):
                    o = begin(4 + i)
                    for q in range(HP):
                        for hh in range(2):
                            mm = pe.matmul(o[hh * NST:(hh + 1) * NST, q * NC:(q + 1) * NC],
                                           M1[p][:, i, q, hh * NST:(hh + 1) * NST], UT[:, 2 * (f * HP + q) + hh, :],
                                           start=True, stop=True)
                    mm.then_inc(full[4 + i], 1)
                marks["kernel", f] = bk.count(3)
                marks["states", f] = bk.count(5)

            def s5_b(f):
                p = f % 2
                pe.wait_ge(s2_TT[f % 2], 16 * CL * (f // 2 + 1))
                pe.wait_ge(s2_X, f + 1)
                for i in range(2):
                    o = begin(6 + i)
                    for k in range(HP):
                        g = 2 * k + i
                        q, r_ = k, slice(NST * i, NST * i + NST)
                        og = o[:, k * P:(k + 1) * P]
                        pe.matmul(og, UT[:, 2 * HP * f + g, :], TT[p][:, g, :], start=True, stop=False)
                        pe.matmul(og, X[p][r_, 0, q, :], ca_re[p][r_, q, :, :], start=False, stop=False)
                        mm = pe.matmul(og, X[p][r_, 1, q, :], ca_ni[p][r_, q, :, :], start=False, stop=True)
                    mm.then_inc(full[6 + i], 1)
                marks["y", f] = bk.count(7)

            s5_a(0)
            gates(2, None)
            s5_a(1)
            s5_b(0)
            gates(3, 0)
            s5_a(2)
            s5_b(1)
            s5_a(3)
            s5_b(2)
            s5_b(3)
            for b in (6, 7):
                pe.wait_ge(free[b], bk.count(b))
            for i in range(CL):
                o = begin(i)
                for k in range(4):
                    mm = pe.transpose(o[:, k * P:(k + 1) * P], Y[:, i, k * P:(k + 1) * P], ident[:, :])
                    if i == k == 0:
                        mm.then_inc(w_used[1], 1)
                mm.then_inc(full[i], 1)
            wg = weights2(4).rearrange("p (k c) -> p k c", k=4)
            pe.wait_ge(free[7], bk.count(7))
            for m in range(4):
                for n in range(2):
                    for br in range(2):
                        b = (4 * m + 2 * n + br) % 8
                        o = begin(b)
                        for k in range(4):
                            mm = pe.matmul(o, wg[:, k, (4 * br + m) * P:(4 * br + m + 1) * P],
                                           yT[:, k, n * 512:(n + 1) * 512], start=(k == 0), stop=(k == 3))
                        mm.then_inc(full[b], 1)
                    marks["glu", 2 * m + n] = (b, bk.count(b))
            gates(5, 0)
            qT_free = [bk.count(b) for b in range(8)]
            pe.wait_ge(s2_wk, 16)
            o = begin(0)
            for m in range(4):
                mm = pe.transpose(o[:, m * P:(m + 1) * P], wuk[:, m * P:(m + 1) * P], ident[:, :])
                if m == 0:
                    mm.then_inc(w_used[1], 1)
            mm.then_inc(full[0], 1)
            for b in range(8):
                pe.wait_ge(free[b], qT_free[b] + (b == 0))
            for h in range(H):
                for n in range(2):
                    b = (1 + 2 * h + n) % 8
                    o = begin(b)
                    r_ = slice(VD * (h % 2), VD * (h % 2) + VD)
                    pe.matmul(o, wukT[r_, h // 2, :], qT2[r_, h // 2, n * 512:(n + 1) * 512],
                              start=True, stop=True).then_inc(full[b], 1)
            marks["qlat"] = bk.count(0)
            marks["attention"] = list(bk.n)
            for b in range(8):
                pe.wait_ge(free[b], bk.count(b))
            pe.wait_ge(s2_wv, 16)

            def scores2(u):
                t, h = u // H, u % H
                b = 2 * (u % 2)
                begin(b)
                w = (t + 1) * P
                for n in range((w + 511) // 512):
                    mm = pe.matmul(PS[:, b + n, 0:min(512, w - 512 * n)], qlT[:, h, t * P:(t + 1) * P],
                                   c2T[:, n * 512:min(w, n * 512 + 512)], start=True, stop=True)
                mm.then_inc(full[b], 1)

            def p_turn2(u):
                t = u // H
                pe.wait_ge(free[2 * (u % 2)], bk.count(2 * (u % 2)))
                for j in range(2):
                    if 4 * j > t:
                        continue
                    o = begin(4 + j)
                    for c in range(4 * j, min(4 * j + 4, t + 1)):
                        mm = pe.transpose(o[:, (c % 4) * P:(c % 4 + 1) * P], Pb2[u % 2][:, c * P:(c + 1) * P], ident[:, :])
                    mm.then_inc(full[4 + j], 1)
                pt2[u] = (bk.count(4), bk.count(5))

            def latent_out(t, hg):
                u = H * t + 4 * hg + 3
                pe.wait_ge(free[4], pt2[u][0])
                pe.wait_ge(free[5], pt2[u][1])
                o = begin(6)
                for k in range(t + 1):
                    mm = pe.matmul(o, c2[:, k, :], PT2[hg][:, k, :], start=(k == 0), stop=(k == t))
                mm.then_inc(full[6], 1)
                ol_free[hg] = bk.count(6)

            def att_out(t):
                o = begin(7)
                pe.wait_ge(free[6], ol_free[1])
                for h in range(H):
                    mm = pe.matmul(o[:, h * VD:(h + 1) * VD], olT[h // 4][:, (h % 4) * P:(h % 4 + 1) * P], wuv[:, h, :],
                                   start=True, stop=True)
                mm.then_inc(full[7], 1)

            def att_turn(t):
                pe.wait_ge(free[7], bk.count(7))
                o = begin(6)
                for k in range(4):
                    mm = pe.transpose(o[:, k * P:(k + 1) * P], att[t % 2][:, k * P:(k + 1) * P], ident[:, :])
                mm.then_inc(full[6], 1)
                turn_free[0] = bk.count(6)

            def out_tile(t):
                pe.wait_ge(free[6], turn_free[0])
                if t == 0:
                    pe.wait_ge(s2_glu, 8)
                for n in range(2):
                    wo = k_of(weights2(6 + n)) if t == 0 else k_of(W[:, n, :])
                    o = begin(6 + n)
                    for k in range(KD):
                        mm = pe.matmul(o, mix[:, k, t * P:(t + 1) * P], wo[:, k, :], start=(k == 0), stop=(k == 7))
                    mm.then_inc(full[6 + n], 1)

            pt2, ol_free, turn_free = {}, {}, {}
            scores2(0)
            for u in range(H * NT):
                t, h = u // H, u % H
                if u + 1 < H * NT:
                    scores2(u + 1)
                p_turn2(u)
                if h == 5:
                    latent_out(t, 0)
                if t >= 1 and h in (1, 2, 3, 4):
                    [lambda: latent_out(t - 1, 1), lambda: att_out(t - 1), lambda: att_turn(t - 1),
                     lambda: out_tile(t - 1)][h - 1]()
            latent_out(NT - 1, 1)
            att_out(NT - 1)
            att_turn(NT - 1)
            out_tile(NT - 1)

        @block.sync
        def _(sp):
            sp.dma_start(x1[:, :, :], a["x"][0].rearrange("(t p) d -> p t d", p=P)).then_inc(s_xin, 16)
            sp.dma_start(ident[:, :], a["c_ident"]).then_inc(s_const, 16)
            sp.dma_start(dft_d[:, :], a["c_dft_d"]).then_inc(s_const, 16)
            sp.dma_start(cosT[:, :, :], a["c_cos"].rearrange("(t p) c -> p t c", p=P)).then_inc(s_const, 16)
            sp.dma_start(sinT[:, :, :], a["c_sin"].rearrange("(t p) c -> p t c", p=P)).then_inc(s_const, 16)
            sp.wait_ge(s_xin, 16)

            def chunk(l, i):
                n, name = CHUNKS[i]
                if n == 0:
                    return
                s = i % W_SLOTS
                takes = 1 + l * W_TAKES[s] + sum(c[0] > 0 for c in CHUNKS[s:i:W_SLOTS])
                sp.wait_ge(w_used[s], takes)
                slot = W[:, s, :]
                k512 = slot.rearrange("p (k c) -> p k c", k=8)

                def load(dst, src):
                    sp.dma_start(dst, src).then_inc(w_in_slot[s], 16)

                def win(c0, w=512):
                    return a["w_in"][l, :, c0:c0 + w].rearrange("(k p) c -> p k c", p=P)

                if name == "c":
                    load(k512, win(0))
                elif name == "u":
                    load(k512, win(C_U))
                elif name == "up":
                    load(slot[:, 0:2 * H * QK].rearrange("p (k c) -> p k c", k=2),
                         a["w_uq"][l].rearrange("(k p) c -> p k c", p=P))
                    load(slot[:, 2 * H * QK:2 * H * QK + 2048].rearrange("p (k c) -> p k c", k=2),
                         a["w_ukv"][l].rearrange("(k p) c -> p k c", p=P))
                elif name[:3] == "dft":
                    n0 = 512 * int(name[3])
                    load(k512, a["c_dft_s"][:, n0:n0 + 512].rearrange("(k p) c -> p k c", p=P))
                elif name == "za":
                    load(k512, win(C_ZA))
                elif name == "zf":
                    load(k512, win(C_ZF))
                elif name[:4] == "gate":
                    m = int(name[4:]) * P
                    g = slot[:, 0:24 * P].rearrange("p (k c) -> p k c", c=P)
                    load(g[:, 0:8, :], win(C_GA + m, P))
                    load(g[:, 8:16, :], win(C_GF + m, P))
                    load(g[:, 16:20, :], a["w_attn_proj"][l, :, m:m + P].rearrange("(k p) c -> p k c", p=P))
                    load(g[:, 20:24, :], a["w_fourier_proj"][l, :, m:m + P].rearrange("(k p) c -> p k c", p=P))
                else:
                    n0 = 512 * int(name[3])
                    load(k512, a["w_out"][l, :, n0:n0 + 512].rearrange("(k p) c -> p k c", p=P))

            sp.wait_ge(s_init, 3)
            with sp.Fori(0, L) as l:
                sp.wait_ge(s_xnew, l + 1)
                for dst, name, n in [(0, "norm_g", KD), (KD, "q_latent_g", 2), (KD + 2, "kv_latent_g", 2)]:
                    sp.dma_start(rows[dst:dst + n, :], a[name][l].rearrange("(k p) -> k p", p=P)).then_inc(s_par, 16)
                sp.dma_start(rows[KD + 4:N_ROWS, :],
                             a["b_merge"][l].rearrange("b (k p) -> (b k) p", p=P)).then_inc(s_par, 16)
                sp.dma_start(gq[:, :], a["q_head_g"][l].partition_broadcast(P)).then_inc(s_par, 16)
                sp.dma_start(gk[:, :], a["k_head_g"][l].partition_broadcast(P)).then_inc(s_par, 16)
                chunk(l, 0)
                sp.dma_start(wpe[:, :, :], a["w_in"][l, :, C_PE:C_PE + ROPE].rearrange("(k p) c -> p k c", p=P)
                             ).then_inc(s_wpe, 16)
                chunk(l, 1)
                sp.dma_start(xres.rearrange("(t p) d -> p t d", p=P), x1[:, :, :]).then_inc(s_xsave, 16)
                for i in range(2, 7):
                    chunk(l, i)
                sp.wait_ge(s_o, l + 1)
                sp.wait_ge(s_xsave, l * 16 + 16)
                sp.dma_start(x1[:, :, :], xres.rearrange("(t p) d -> p t d", p=P)).then_inc(s_xback, 16)
                for i in range(7, len(CHUNKS)):
                    chunk(l, i)
            sp.wait_ge(s_xnew, L + 1)
            def small(dst, src, q):
                sp.dma_start(dst, src).then_inc(q, 16)

            def load2(i, srcs):
                sl = i % W_SLOTS
                sp.wait_ge(w_used[sl], 1 + L * W_TAKES[sl] + i // W_SLOTS)
                for dst, src in srcs(W[:, sl, :]):
                    sp.dma_start(dst, src).then_inc(w_in_slot[sl], 16)

            def cols(c0, w):
                return lambda slot: [(slot[:, 0:KD * w].rearrange("p (k c) -> p k c", k=KD),
                                      a["w_in_2"][0, :, c0:c0 + w].rearrange("(k p) c -> p k c", p=P))]

            small(rows[0:KD, :], a["b_glu_2"][0].rearrange("(k p) -> k p", p=P), s2_rows)
            for i, n in enumerate(["a_re_2", "a_im_2"]):
                small(prow[0:NPAIR, 1 + i, :], a[n][0].rearrange("(q h) p -> q (h p)", h=2), s2_rows)
            small(lrow, a["log_dt_2"][0].rearrange("(q h) -> q h", h=2), s2_rows)
            small(drow, a["d_skip_2"][0], s2_rows)
            small(tri, a["c_tri"], s2_rows)
            small(kvg, a["kv_norm_g_2"][0].partition_broadcast(P), s2_rows)
            load2(0, cols(C2_C, NIDX))
            for i, n in enumerate(["c_re_2", "c_im_2"]):
                for hh in range(2):
                    small(craw[:, 4 * i:4 * i + 4, hh * NST:(hh + 1) * NST],
                          a[n][0].rearrange("g c p -> (g c) p").rearrange("(k r) p -> r k p", r=P), s2_par)
            for i, n in enumerate(["b_re_2", "b_im_2"]):
                small(Braw[:, i], a[n][0].rearrange("(q h) p c -> (h p) q c", h=2), s2_par)
            load2(1, cols(C2_U, SW))
            small(xres.rearrange("(t p) d -> p t d", p=P), x1[:, :, :], s_xsave)
            load2(2, cols(C2_GA, AW))
            load2(3, cols(C2_GS, SW))
            for f in range(4):
                if f >= 2:
                    sp.wait_ge(full[7], marks["y", f - 2])
                sp.wait_ge(s2_K, f + 1)
                for j in range(CL):
                    sp.dma_start(TT[f % 2][j * CH:(j + 1) * CH, :, j * CH:P], K16[f % 2][:, :, 0:(CL - j) * CH]
                                 ).then_inc(s2_TT[f % 2], 16)
            load2(4, lambda slot: [(slot.rearrange("p (k c) -> p k c", k=4),
                                    a["w_glu_2"][0].rearrange("(k p) c -> p k c", p=P))])
            load2(5, cols(0, AW))
            sp.wait_ge(full[7], marks["y", 3])
            small(wuk.rearrange("p (h d) -> p h d", h=H), a["w_uk_2"][0].rearrange("h c d -> c h d"), s2_wk)
            small(wuv, a["w_uv_2"][0].rearrange("h c d -> c h d"), s2_wv)
            for n in range(2):
                load2(6 + n, lambda slot, n=n: [(slot.rearrange("p (k c) -> p k c", k=KD),
                      a["w_out_2"][0, :, n * 512:(n + 1) * 512].rearrange("(k p) c -> p k c", p=P))])
            sp.wait_ge(full[0], marks["qlat"])
            small(lng, a["ln_g_2"][0].partition_broadcast(P), s2_ln)
            small(lnb, a["ln_b_2"][0].partition_broadcast(P), s2_ln)
            sp.wait_ge(s_xsave, 16 * (L + 1))
            for t in range(NT):
                if t >= 2:
                    sp.wait_ge(s2_od[t % 2], 16 * (t // 2))
                small(xt[t % 2], xres[t * P:(t + 1) * P, :], s2_xt[t % 2])
                if t >= 1:
                    sp.wait_ge(s2_o, t)
                    small(out[0, (t - 1) * P:t * P, :], xt[(t - 1) % 2], s2_od[(t - 1) % 2])
            sp.wait_ge(s2_o, NT)
            small(out[0, (NT - 1) * P:, :], xt[(NT - 1) % 2], s2_od[(NT - 1) % 2])
            for i in range(2):
                sp.wait_ge(s2_od[i], 16 * (NT // 2))

        @block.scalar
        def _(act):
            bk = Banks(full, free)
            st = Steps(act, s_act)
            PER = NT + 2 * NT
            act.wait_ge(s_init, 3)
            act.wait_ge(s_xin, 16)

            def arrive(b):
                act.wait_ge(full[b], bk.take(b) + 1)
                return PS[:, b, :]

            with act.Fori(0, L) as l:
                bk.enter(l)
                st.enter(l, PER)
                act.wait_ge(s_xnew, l + 1)
                for t in range(NT):
                    st.link(act.activation(xn[t], x1[:, t, :], ACT.Square, accum_out=ssx[:, t:t + 1]))
                    act.activation(ssx[:, t:t + 1], ssx[:, t:t + 1], ACT.Sqrt, bias=eps[:, :], scale=1.0 / D
                                   ).then_inc(s_std, 1)
                bk.skip(ROUND[0])
                for t in range(NT):
                    o = arrive(t % 8)
                    act.activation(c_tok[:, t, :], o, ACT.Copy)
                    for j in range(2):
                        i = act.activation(cT[:, j, 0:256], o[:, j * 256:(j + 1) * 256], ACT.Square,
                                           accum_out=ssc[:, 2 * t + j:2 * t + j + 1])
                        st.done(i)
                    st.wait()
                    act.activation(ssc[:, 2 * t:2 * t + 2], ssc[:, 2 * t:2 * t + 2], ACT.Sqrt, bias=eps[:, :],
                                   scale=1.0 / QL).then_inc(free[t % 8], 1)
                o = arrive(0)
                act.activation(kpe[:, :, :], o[:, 0:NT * ROPE].rearrange("p (t c) -> p t c", t=NT), ACT.Copy
                               ).then_inc(free[0], 1)
                for b in range(8):
                    o = arrive(b)
                    act.activation(uT[:, b // 2, (b % 2) * 512:(b % 2 + 1) * 512], o, ACT.Copy).then_inc(free[b], 1)
                bk.skip(ROUND[3])
                for t in range(NT):
                    for j in range(4):
                        i = 4 * t + j
                        b = i % 8
                        o = arrive(b)
                        n_before = l * 4 * NT + i - 1
                        if i >= 2:
                            act.wait_ge(s_ss, n_before)
                        if j < 2:
                            act.activation(q_tok[:, t, j * 4 * QK:(j + 1) * 4 * QK], o[:, 0:4 * QK], ACT.Copy)
                            act.activation(tmp[:, i % 2, 0:4 * QK], o[:, 0:4 * QK], ACT.Square).then_inc(free[b], 1)
                        else:
                            act.activation(tmp[:, i % 2, 0:4 * NOPE].rearrange("p (h c) -> p h c", h=4),
                                           o.rearrange("p (h c) -> p h c", h=4)[:, :, 0:NOPE], ACT.Square
                                           ).then_inc(s_sq, 1)
                for j in range(NT):
                    o = arrive(j)
                    act.activation(V[:, j, :], o, ACT.Copy).then_inc(free[j], 1)
                for b in range(8):
                    o = arrive(b)
                    g, n = b % 4, b // 4
                    act.activation(fT[:, g, n * 512:(n + 1) * 512], o, ACT.Copy).then_inc(free[b], 1)
                act.wait_ge(s_ssall, l + 1)
                act.activation(rsh[:, :, :, :], ssh[:, :, :, :], ACT.Sqrt, bias=eps[:, :], scale=1.0 / QK
                               ).then_inc(s_hstd, 1)

                def qk_copy(h, i):
                    o = arrive(7)
                    dst = (qT if i < 2 else kT)[h % 2]
                    act.activation(dst[0:QK, (i % 2) * 512:(i % 2 + 1) * 512], o[0:QK, :], ACT.Copy
                                   ).then_inc(free[7], 1)

                for i in range(4):
                    qk_copy(0, i)
                for u in range(UNITS + 1):
                    if u >= 1:
                        o = arrive(5)
                        bk.take(4)
                        act.activation(PT[(u - 1) % 2][:, 512:1024], o, ACT.Copy).then_inc(free[5], 1)
                    if u < UNITS:
                        b = 2 * (u % 2)
                        bk.take(b)
                        act.wait_ge(s_nm, l * UNITS + u + 1)
                        act.activation(Pb[u % 2], PS[:, b:b + 2, :].rearrange("p a c -> p (a c)"), ACT.Exp,
                                       bias=negm[:, u:u + 1], accum_out=rsum[:, u:u + 1]).then_inc(free[b], 1)
                    if 1 <= u % NT <= 4 and u // NT + 1 < H:
                        qk_copy(u // NT + 1, u % NT - 1)
                for h in range(H):
                    bk.take(6)
                for t in range(NT):
                    o = arrive(t)
                    act.activation(oT[:, :, t * P:(t + 1) * P], o.rearrange("p (k c) -> p k c", k=4), ACT.Copy
                                   ).then_inc(free[t], 1)
                for i in range(16):
                    b = i % 8
                    o = arrive(b)
                    if i >= 2:
                        act.wait_ge(s_sm, l * 16 + i - 1)
                    act.activation(tmp[:, i % 2, :], o, ACT.Silu).then_inc(free[b], 1)
                for m in range(KD):
                    for n in range(2):
                        i = 2 * m + n
                        if i >= 2:
                            act.wait_ge(s_mT, l * 16 + i - 1)
                        for br in range(2):
                            o = arrive(4 * n + br)
                            act.activation(sg[:, 2 * (i % 2) + br, :], o, ACT.Sigmoid,
                                           bias=pT[:, KD + 4 + br * KD + m:KD + 5 + br * KD + m]
                                           ).then_inc(free[4 * n + br], 1)
                        bk.take(4 * n + 2)
                        bk.take(4 * n + 3)
                bk.skip(ROUND[11])
            bk.leave(L)
            st.leave(L)

            def flat_bank(b, lo, hi):
                return PS[:, b:b + 2, :].rearrange("p a c -> p (a c)")[:, lo:hi]

            for t in range(NT):
                b = (2 * t) % 8
                o = arrive(b)
                act.activation(xT[:, 0:4, t * P:(t + 1) * P], o.rearrange("p (k c) -> p k c", k=4), ACT.Copy
                               ).then_inc(free[b], 1)
                bk.take(b + 1)
            bk.take(0)
            for i in range(6):
                o = arrive(i)
                m, n = i // 2, i % 2
                dst = qiT[:, m, n * 512:(n + 1) * 512] if m < 2 else kiT[:, n * 512:(n + 1) * 512]
                act.activation(dst, o, ACT.Copy).then_inc(free[i], 1)
            for t in range(NT):
                b = (6 + t) % 8
                o = arrive(b)
                act.activation(c2[:, t, :], o[:, 0:KVC], ACT.Copy)
                act.activation(wtok[:, t, :], o[:, KVC:KVC + IH], ACT.Copy)
                st.link(act.activation(cosT[:, :, :].rearrange("p a b -> p (a b)"), o[:, 0:KVC], ACT.Square, accum_out=ssx[:, t:t + 1]))
                act.activation(ssx[:, t:t + 1], ssx[:, t:t + 1], ACT.Sqrt, bias=eps[:, :], scale=1.0 / KVC
                               ).then_inc(free[b], 1)
            for i, b in enumerate((7, 0)):
                o = arrive(b).rearrange("p (q h c) -> p q h c", q=NPAIR, h=2)
                act.activation(CT[0:NST, i], o[0:NST, :, 0, :], ACT.Copy, scale=1.0 - 2 * i)
                act.activation(CT[NST:P, i], o[NST:P, :, 1, :], ACT.Copy, scale=1.0 - 2 * i).then_inc(free[b], 1)
            for v in range((NT - 2) * IH):
                b = 2 * (v % 4)
                arrive(b)
                w = (3 + v // IH) * P
                if v >= 2:
                    act.wait_ge(s2_acc, v - 1)
                act.activation(rl[v % 2][:, 0:w], flat_bank(b, 0, w), ACT.Relu).then_inc(free[b], 1)
            for j in range(2):
                o = arrive(j)
                act.activation(c2T[:, j * 512:(j + 1) * 512], o, ACT.Copy).then_inc(free[j], 1)
            for j in range(CL):
                o = arrive(j)
                act.activation(U4[:, :, j, :], o.rearrange("p (g c) -> p g c", g=NG), ACT.Copy).then_inc(free[j], 1)
            for b in range(8):
                o = arrive(b)
                act.activation(UT[:, 4 * b:4 * b + 4, :], o.rearrange("p (g c) -> p g c", g=4), ACT.Copy
                               ).then_inc(free[b], 1)

            def silu_gates(k0):
                for b in range(8):
                    o = arrive(b)
                    act.activation(mix[:, k0 + b // 2, (b % 2) * 512:(b % 2 + 1) * 512], o, ACT.Silu
                                   ).then_inc(free[b], 1)

            def s5_a(f):
                p = f % 2
                for i in range(2):
                    o = arrive(i)
                    act.activation(M1[p][:, i], o.rearrange("p (q c) -> p q c", q=HP), ACT.Copy).then_inc(free[i], 1)
                for i in range(2):
                    o = arrive(2 + i)
                    act.activation(K16[p][:, i:2 * HP:2, :], o[0:CH, :].rearrange("p (g c) -> p g c", g=HP), ACT.Copy
                                   ).then_inc(free[2 + i], 1)
                for i in range(2):
                    o = arrive(4 + i)
                    act.activation(st_[p][:, i], o.rearrange("p (q c) -> p q c", q=HP), ACT.Copy
                                   ).then_inc(free[4 + i], 1)

            def s5_b(f):
                for i in range(2):
                    o = arrive(6 + i)
                    g0 = 2 * HP * f
                    y = Y[:, :, g0 * CH:(g0 + 2 * HP) * CH].rearrange("p i (q h c) -> p h q i c", q=HP, h=2)
                    act.activation(y[:, i], o.rearrange("p (q i c) -> p q i c", q=HP, i=CL), ACT.Gelu_apprx_tanh
                                   ).then_inc(free[6 + i], 1)

            s5_a(0)
            act.wait_ge(s_xsave, 16 * (L + 1))
            silu_gates(0)
            s5_a(1)
            s5_b(0)
            silu_gates(4)
            s5_a(2)
            s5_b(1)
            s5_a(3)
            s5_b(2)
            s5_b(3)
            for i in range(CL):
                o = arrive(i)
                act.activation(yT[:, :, i:S:CL], o.rearrange("p (k c) -> p k c", k=4), ACT.Copy).then_inc(free[i], 1)
            for m in range(4):
                for n in range(2):
                    i = 2 * m + n
                    if i >= 2:
                        act.wait_ge(s2_glu, i - 1)
                    b = (4 * m + 2 * n) % 8
                    o = arrive(b)
                    act.activation(vb[i % 2], o, ACT.Identity, bias=pT[:, m:m + 1]).then_inc(free[b], 1)
                    o = arrive(b + 1)
                    act.activation(gb[i % 2], o, ACT.Sigmoid, bias=pT[:, 4 + m:5 + m]).then_inc(free[b + 1], 1)
            for b in range(8):
                o = arrive(b)
                act.activation(qT2[:, b // 2, (b % 2) * 512:(b % 2 + 1) * 512], o, ACT.Copy).then_inc(free[b], 1)
            o = arrive(0)
            act.activation(wukT[:, :, :], o.rearrange("p (m c) -> p m c", m=4), ACT.Copy).then_inc(free[0], 1)
            for h in range(H):
                for n in range(2):
                    b = (1 + 2 * h + n) % 8
                    o = arrive(b)
                    act.activation(qlT[:, h, n * 512:(n + 1) * 512], o, ACT.Copy, scale=64.0 ** -0.5
                                   ).then_inc(free[b], 1)

            def latent_copy(hg):
                o = arrive(6)
                act.activation(olT[hg], o, ACT.Copy).then_inc(free[6], 1)

            def ln_std(t):
                act.wait_ge(s2_r, t + 1)
                st.link(act.activation(r2b[:, 3072:4096], xt[t % 2], ACT.Square, accum_out=rsx[:, t:t + 1]))
                act.activation(rsx[:, t:t + 1], rsx[:, t:t + 1], ACT.Sqrt, bias=epsl[:, :], scale=1.0 / D
                               ).then_inc(s2_sq, 1)

            for u in range(H * NT):
                t, h = u // H, u % H
                if u >= 1:
                    tp = (u - 1) // H
                    hp = (u - 1) % H
                    bk.take(4)
                    if tp >= 4:
                        o = arrive(5)
                        n = tp - 3
                        act.activation(PT2[hp // 4][:, 4:4 + n, (hp % 4) * P:(hp % 4 + 1) * P],
                                       o[:, 0:n * P].rearrange("p (k c) -> p k c", k=n), ACT.Copy).then_inc(free[5], 1)
                b = 2 * (u % 2)
                bk.take(b)
                act.wait_ge(s2_nm, u + 1)
                w = (t + 1) * P
                act.activation(Pb2[u % 2][:, 0:w], Pb2[u % 2][:, 0:w], ACT.Exp, scale=-1.0,
                               bias=negm[:, u:u + 1], accum_out=rsum[:, u:u + 1]).then_inc(free[b], 1)
                if h == 5:
                    latent_copy(0)
                if t >= 1 and h == 1:
                    latent_copy(1)
                if t >= 1 and h == 2:
                    bk.take(7)
                if t >= 1 and h == 3:
                    bk.take(6)
                if t >= 1 and h == 4:
                    bk.take(6)
                    bk.take(7)
                if t >= 1 and h == 6:
                    ln_std(t - 1)
            bk.take(4)
            o = arrive(5)
            act.activation(PT2[1][:, 4:8, 3 * P:4 * P], o.rearrange("p (k c) -> p k c", k=4), ACT.Copy
                           ).then_inc(free[5], 1)
            latent_copy(1)
            ln_std(NT - 1)

        @block.vector
        def _(dve):
            bk = Banks(full, free)
            st = Steps(dve, s_dve)
            PER = 1 + NT + NT + 4 + 2 * NT + 9 + H
            for q in (*full, *free, *w_used, s_xnew):
                dve.sem_inc(q, 1)
            dve.memset(eps[:, :], EPS).then_inc(s_init, 1)
            dve.memset(rows[:, :], 0.0).then_inc(s_init, 1)
            dve.memset(u_mid[:, :, :], 0.0).then_inc(s_init, 1)
            dve.wait_ge(s_init, 3)
            dve.wait_ge(s_const, 64)
            dve.wait_ge(s_xin, 16)

            def arrive(b):
                dve.wait_ge(full[b], bk.take(b) + 1)
                return PS[:, b, :]

            with dve.Fori(0, L) as l:
                bk.enter(l)
                st.enter(l, PER)
                o = arrive(0)
                dve.tensor_copy(pT[:, :], o[:, 0:N_ROWS]).then_inc(free[0], 1)
                dve.wait_ge(free[0], bk.count(0))
                dve.wait_ge(s_par, 96 * l + 96)
                st.done(dve.tensor_scalar(gq[:, :], gq[:, :], float(QK) ** -0.5, None, ALU.mult))

                def norm(t):
                    dve.wait_ge(s_std, l * NT + t + 1)
                    st.link(dve.reciprocal(rsx[:, t:t + 1], ssx[:, t:t + 1]))
                    dve.tensor_scalar(xn[t], x1[:, t, :], rsx[:, t:t + 1], None, ALU.mult).then_inc(s_xn, 1)

                norm(0)
                for t in range(NT):
                    if t + 1 < NT:
                        norm(t + 1)
                    for j in range(2):
                        b = (1 + 2 * t + j) % 8
                        o = arrive(b)
                        dve.tensor_tensor(hT[:, 4 * j:4 * j + 4, t * P:(t + 1) * P],
                                          o.rearrange("p (k c) -> p k c", k=4),
                                          pT[:, 4 * j:4 * j + 4].unsqueeze(2).broadcast_to([P, 4, P]), ALU.mult
                                          ).then_inc(free[b], 1)
                for t in range(NT):
                    bk.take(t)
                    dve.wait_ge(free[t], bk.count(t))
                    st.link(dve.reciprocal(rsc[:, 2 * t:2 * t + 2], ssc[:, 2 * t:2 * t + 2]))
                    c = c_tok[:, t, :].rearrange("p (j c) -> p j c", j=2)
                    dve.tensor_tensor(c, c, rsc[:, 2 * t:2 * t + 2].unsqueeze(2).broadcast_to([P, 2, 256]), ALU.mult
                                      ).then_inc(s_cn, 1)
                bk.take(0)
                bk.skip(ROUND[2])
                u_free = [bk.count(b) for b in range(8)]
                for t in range(NT):
                    o = arrive(t % 8)
                    dve.tensor_tensor(cT[:, :, t * P:(t + 1) * P], o.rearrange("p (k c) -> p k c", k=4),
                                      pT[:, KD:KD + 4].unsqueeze(2).broadcast_to([P, 4, P]), ALU.mult
                                      ).then_inc(free[t % 8], 1)
                for b in range(8):
                    dve.wait_ge(free[b], u_free[b])
                h2 = S // 2
                st.done(dve.tensor_tensor(fold[:, :, 0, 1:h2], uT[:, :, 1:h2], uT[:, :, S - 1:h2:-1], ALU.add))
                st.done(dve.tensor_tensor(fold[:, :, 1, 1:h2], uT[:, :, 1:h2], uT[:, :, S - 1:h2:-1], ALU.subtract))
                st.done(dve.tensor_copy(fold[:, :, 0, 0:1], uT[:, :, 0:1]))
                st.link(dve.memset(fold[:, :, 1, 0:1], 0.0))
                dve.tensor_copy(u_mid[:, :, 0:1], uT[:, :, h2:h2 + 1]).then_inc(s_fold, 1)
                dve.wait_ge(s_xsave, 16 * l + 16)
                for t in range(NT):
                    for j in range(4):
                        i = 4 * t + j
                        b = i % 8
                        o = arrive(b)
                        qk, h0 = j // 2, 4 * (j % 2)
                        w = QK if j < 2 else NOPE
                        o4 = o.rearrange("p (h c) -> p h c", h=4)
                        if j < 2:
                            dve.wait_ge(free[b], bk.count(b))
                        else:
                            dve.wait_ge(s_sq, l * 2 * NT + 2 * t + j - 1)
                            st.done(dve.tensor_copy(k_tok[:, t, h0:h0 + 4, :], o4[:, :, 0:NOPE]))
                        dve.tensor_reduce(ssh[:, qk, t, h0:h0 + 4],
                                          tmp[:, i % 2, 0:4 * w].rearrange("p (h c) -> p h c", h=4), AX.X, ALU.add
                                          ).then_inc(s_ss, 1)
                        if j >= 2:
                            dve.tensor_copy(v_tok[:, t, h0:h0 + 4, :], o4[:, :, NOPE:]).then_inc(free[b], 1)
                st.link(dve.tensor_tensor(kro[:, :, :], kpe[:, :, :], kpe[:, :, :], ALU.mult))
                st.link(dve.tensor_reduce(kss[:, :], kro[:, :, :], AX.X, ALU.add))
                dve.wait_ge(s_ss, l * 4 * NT + 4 * NT)
                dve.tensor_tensor(ssh[:, 1, :, :], ssh[:, 1, :, :], kss[:, :].unsqueeze(2).broadcast_to([P, NT, H]),
                                  ALU.add).then_inc(s_ssall, 1)
                st.link(dve.tensor_tensor(kpe[:, :, :], kpe[:, :, :],
                                          gk[:, NOPE:QK].unsqueeze(1).broadcast_to([P, NT, ROPE]), ALU.mult))
                a1, a2 = kpe[:, :, 0:HR], kpe[:, :, HR:ROPE]
                st.done(dve.tensor_tensor(rt[:, 0], a1, cosT[:, :, :], ALU.mult))
                st.done(dve.tensor_tensor(rt[:, 1], a2, sinT[:, :, :], ALU.mult))
                st.done(dve.tensor_tensor(rt[:, 2], a2, cosT[:, :, :], ALU.mult))
                st.link(dve.tensor_tensor(rt[:, 3], a1, sinT[:, :, :], ALU.mult))
                st.done(dve.tensor_tensor(kro[:, :, 0:HR], rt[:, 0], rt[:, 1], ALU.subtract))
                st.link(dve.tensor_tensor(kro[:, :, HR:ROPE], rt[:, 2], rt[:, 3], ALU.add))
                dve.wait_ge(s_hstd, l + 1)
                dve.reciprocal(rsh[:, :, :, :], rsh[:, :, :, :]).then_inc(s_hrs, 1)
                bk.skip(ROUND[5])
                bk.skip(ROUND[6])

                def head_out(h):
                    dve.wait_ge(free[2], sums_ready[h])
                    st.link(dve.reciprocal(rinv[:, NT * h:NT * h + NT], rsum[:, NT * h:NT * h + NT]))
                    o = arrive(6)
                    dve.tensor_tensor(o_tok[:, :, h * VD:(h + 1) * VD], o.rearrange("p (t c) -> p t c", t=NT),
                                      rinv[:, NT * h:NT * h + NT].unsqueeze(2).broadcast_to([P, NT, VD]), ALU.mult
                                      ).then_inc(free[6], 1)

                for h in range(H):
                    for _ in range(4):
                        bk.take(7)
                sums_ready = []
                for u in range(UNITS + 1):
                    if u < UNITS:
                        b = 2 * (u % 2)
                        arrive(b)
                        if u % NT == NT - 1:
                            sums_ready.append(bk.count(b))
                        dve.tensor_reduce(negm[:, u:u + 1], PS[:, b:b + 2, :].rearrange("p a c -> p (a c)"), AX.X,
                                          ALU.max, negate=True).then_inc(s_nm, 1)
                    if u >= 1:
                        o = arrive(4)
                        bk.take(5)
                        dve.tensor_copy(PT[(u - 1) % 2][:, 0:512], o).then_inc(free[4], 1)
                    if u >= NT and u % NT == 1:
                        head_out(u // NT - 1)
                head_out(H - 1)
                dve.wait_ge(free[6], bk.count(6))
                dve.memset(mark[:, :], 0.0).then_inc(s_o, 1)
                bk.skip(ROUND[7])
                for b in range(8):
                    dve.wait_ge(free[b], bk.count(b))
                for i in range(16):
                    b = i % 8
                    bk.take(b)
                    dve.wait_ge(free[b], bk.count(b))
                    m, n = (i % 8) // 2, i % 2
                    y = (oT if i < 8 else fT)[:, m, n * 512:(n + 1) * 512]
                    dve.tensor_tensor(y, y, tmp[:, i % 2, :], ALU.mult).then_inc(s_sm, 1)
                for m in range(KD):
                    for n in range(2):
                        i = 2 * m + n
                        for br in range(2):
                            bk.take(4 * n + br)
                            dve.wait_ge(free[4 * n + br], bk.count(4 * n + br))
                            o = arrive(4 * n + 2 + br)
                            g = sg[:, 2 * (i % 2) + br, :]
                            dve.tensor_tensor(g, g, o, ALU.mult).then_inc(free[4 * n + 2 + br], 1)
                            dve.wait_ge(free[4 * n + 2 + br], bk.count(4 * n + 2 + br))
                        dve.tensor_tensor(mT[:, m, n * 512:(n + 1) * 512], sg[:, 2 * (i % 2), :],
                                          sg[:, 2 * (i % 2) + 1, :], ALU.add).then_inc(s_mT, 1)
                dve.wait_ge(s_xback, 16 * l + 16)
                for n in range(2):
                    for t in range(NT):
                        o = arrive(t)
                        xx = x1[:, t, n * 512:(n + 1) * 512]
                        dve.tensor_tensor(xx, xx, o, ALU.add).then_inc(free[t], 1)
                for b in range(8):
                    dve.wait_ge(free[b], bk.count(b))
                dve.memset(mark[:, :], 0.0).then_inc(s_xnew, 1)
            bk.leave(L)
            st.leave(L)

            dve.memset(epsl[:, :], LN_EPS).then_inc(s_init, 1)
            dve.wait_ge(s2_rows, 16 * 7)
            dve.tensor_copy(prow[0:NPAIR, 0, :].rearrange("q (h p) -> q h p", h=2),
                            lrow.unsqueeze(2).broadcast_to([NPAIR, 2, NST])).then_inc(s2_ld, 1)
            for t in range(NT):
                b = (2 * t) % 8
                bk.take(b)
                o = arrive(b + 1)
                dve.tensor_copy(xT[:, 4:8, t * P:(t + 1) * P], o.rearrange("p (k c) -> p k c", k=4)
                                ).then_inc(free[b + 1], 1)

            o = arrive(0)
            st.done(dve.tensor_copy(r3b[:, 1024:1072], o[:, 0:48]))
            st.done(dve.tensor_copy(DT, o[0:CH, 64:64 + NG]))
            st.wait()
            dve.tensor_copy(pT[:, 0:KD], o[:, P:P + KD]).then_inc(free[0], 1)
            dve.wait_ge(w_in_slot[0], 16 * (L * W_DMAS[0] + 1))
            wk = W[:, 0, 0:KD * NIDX].rearrange("p (k c) -> p k c", k=KD)[:, :, KVC + IH * ID:KVC + IH * ID + ID]
            dve.tensor_copy(ki4.rearrange("p k (r c) -> p k r c", r=4), wk.unsqueeze(2).broadcast_to([P, KD, 4, ID])
                            ).then_inc(s2_ki, 1)
            dve.wait_ge(s2_par, 16 * S5_LOADS)
            slot = iter(range(40))
            names = {}

            def v(name):
                if name not in names:
                    names[name] = scr[:, next(slot), :]
                return names[name]

            def ts(out_, in_, a1, a2, op0, op1=None):
                st.link(dve.tensor_scalar(out_, in_, a1, a2, op0, op1) if op1 is not None else
                        dve.tensor_scalar(out_, in_, a1, None, op0))

            def stt(out_, in0, c, in1, op0, op1):
                st.link(dve.scalar_tensor_tensor(out=out_, in0=in0, scalar=c, in1=in1, op0=op0, op1=op1))

            def tt(out_, in0, in1, op):
                st.link(dve.tensor_tensor(out_, in0, in1, op))

            ROUNDER = 1.5 * 2.0 ** 23

            def exp(dst, src):
                x, k, rr, p = v("ex"), v("ek"), v("er"), v("ep")
                ts(x, src, -87.0, 88.0, ALU.max, ALU.min)
                ts(k, x, 1.4426950408889634, ROUNDER, ALU.mult, ALU.add)
                ts(k, k, -ROUNDER, None, ALU.add)
                stt(rr, k, -0.693359375, x, ALU.mult, ALU.add)
                stt(rr, k, 2.12194440e-4, rr, ALU.mult, ALU.add)
                ts(p, rr, 1 / 5040.0, 1 / 720.0, ALU.mult, ALU.add)
                for c in (1 / 120.0, 1 / 24.0, 1 / 6.0, 0.5, 1.0):
                    tt(p, p, rr, ALU.mult)
                    ts(p, p, c, None, ALU.add)
                tt(p, p, rr, ALU.mult)
                ts(p, p, 1.0, None, ALU.add)
                ki = v("eki").bitcast(mybir.dt.int32)
                ts(ki, k, 127.0, 8388608.0, ALU.add, ALU.mult)
                tt(dst, p, v("eki"), ALU.mult)

            def sincos(sn, cs, z):
                n, rr, x2, p, q, m, b0, b1 = (v(i) for i in ("sn", "sr", "sx", "sp", "sq", "sm", "sb0", "sb1"))
                ts(n, z, 0.6366197723675814, ROUNDER, ALU.mult, ALU.add)
                ts(n, n, -ROUNDER, None, ALU.add)
                rest = np.pi / 2
                cur = z
                for bits in (9, 20, 31):
                    part_ = float(np.floor(rest * 2.0 ** bits) / 2.0 ** bits)
                    stt(rr, n, -part_, cur, ALU.mult, ALU.add)
                    rest -= part_
                    cur = rr
                stt(rr, n, -float(rest), rr, ALU.mult, ALU.add)
                tt(x2, rr, rr, ALU.mult)
                ts(p, x2, 1 / 362880.0, -1 / 5040.0, ALU.mult, ALU.add)
                for c in (1 / 120.0, -1 / 6.0):
                    tt(p, p, x2, ALU.mult)
                    ts(p, p, c, None, ALU.add)
                tt(p, p, x2, ALU.mult)
                tt(p, p, rr, ALU.mult)
                tt(p, p, rr, ALU.add)
                ts(q, x2, -1 / 3628800.0, 1 / 40320.0, ALU.mult, ALU.add)
                for c in (-1 / 720.0, 1 / 24.0, -0.5):
                    tt(q, q, x2, ALU.mult)
                    ts(q, q, c, None, ALU.add)
                tt(q, q, x2, ALU.mult)
                ts(q, q, 1.0, None, ALU.add)
                for src, half, bit in ((n, m, b0), (m, x2, b1)):
                    ts(half, src, 0.5, -0.25, ALU.mult, ALU.add)
                    ts(half, half, ROUNDER, None, ALU.add)
                    ts(half, half, -ROUNDER, None, ALU.add)
                    stt(bit, half, -2.0, src, ALU.mult, ALU.add)
                ts(n, b0, -1.0, 1.0, ALU.mult, ALU.add)
                ts(b1, b1, -2.0, 1.0, ALU.mult, ALU.add)
                ts(m, b0, -2.0, 1.0, ALU.mult, ALU.add)
                tt(m, m, b1, ALU.mult)
                tt(x2, p, n, ALU.mult)
                tt(rr, q, b0, ALU.mult)
                tt(x2, x2, rr, ALU.add)
                tt(sn, x2, b1, ALU.mult)
                tt(x2, q, n, ALU.mult)
                tt(rr, p, b0, ALU.mult)
                tt(x2, x2, rr, ALU.add)
                tt(cs, x2, m, ALU.mult)

            dt_, zr, zi = v("dt"), v("zr"), v("zi")
            exp(dt_, lam[:, 0, :])
            tt(zr, lam[:, 1, :], dt_, ALU.mult)
            tt(zi, lam[:, 2, :], dt_, ALU.mult)
            er, sn, cs = v("size"), v("sine"), v("cosine")
            exp(er, zr)
            sincos(sn, cs, zi)
            tt(apow[:, 0, :, 0], er, cs, ALU.mult)
            tt(apow[:, 1, :, 0], er, sn, ALU.mult)
            m1, m2 = v("m1"), v("m2")
            for n0 in (1, 2, 4):
                for j in range(n0):
                    ar, ai = apow[:, 0, :, n0 - 1], apow[:, 1, :, n0 - 1]
                    br, bi = apow[:, 0, :, j], apow[:, 1, :, j]
                    tt(m1, ar, br, ALU.mult)
                    tt(m2, ai, bi, ALU.mult)
                    tt(apow[:, 0, :, n0 + j], m1, m2, ALU.subtract)
                    tt(m1, ar, bi, ALU.mult)
                    tt(m2, ai, br, ALU.mult)
                    tt(apow[:, 1, :, n0 + j], m1, m2, ALU.add)
            for _ in range(3):
                tt(er, er, er, ALU.mult)
                tt(m1, cs, cs, ALU.mult)
                tt(m2, sn, sn, ALU.mult)
                tt(sn, sn, cs, ALU.mult)
                ts(sn, sn, 2.0, None, ALU.mult)
                tt(cs, m1, m2, ALU.subtract)
            for i, x in enumerate((er, cs, sn)):
                st.link(dve.tensor_copy(s5c[:, i, :], x))
            lr, li = lam[:, 1, :], lam[:, 2, :]
            tt(m1, lr, lr, ALU.mult)
            tt(m2, li, li, ALU.mult)
            tt(m1, m1, m2, ALU.add)
            inv, fr, fi, am = v("inv"), v("fr"), v("fi"), v("am")
            st.link(dve.reciprocal(inv, m1))
            ts(am, apow[:, 0, :, 0], -1.0, None, ALU.add)
            ai = apow[:, 1, :, 0]
            tt(m1, am, lr, ALU.mult)
            tt(m2, ai, li, ALU.mult)
            tt(fr, m1, m2, ALU.add)
            tt(fr, fr, inv, ALU.mult)
            tt(m1, ai, lr, ALU.mult)
            tt(m2, am, li, ALU.mult)
            tt(fi, m1, m2, ALU.subtract)
            tt(fi, fi, inv, ALU.mult)

            def wide(x):
                return x.unsqueeze(2).broadcast_to([P, NPAIR, CH])

            tt(Bb[:, 0], Braw[:, 0], wide(fr), ALU.mult)
            tt(Bb[:, 1], Braw[:, 0], wide(fi), ALU.mult)
            tt(Braw[:, 0], Braw[:, 1], wide(fi), ALU.mult)
            tt(Bb[:, 0], Bb[:, 0], Braw[:, 0], ALU.subtract)
            tt(Braw[:, 1], Braw[:, 1], wide(fr), ALU.mult)
            dve.tensor_tensor(Bb[:, 1], Bb[:, 1], Braw[:, 1], ALU.add).then_inc(s2_prep, 1)

            for i in range(6):
                bk.take(i)
            dve.wait_ge(s2_rows, 16 * 7)
            for t in range(NT):
                b = (6 + t) % 8
                bk.take(b)
                dve.wait_ge(free[b], bk.count(b))
                st.link(dve.reciprocal(ssx[:, t:t + 1], ssx[:, t:t + 1]))
                dve.scalar_tensor_tensor(out=c2[:, t, :], in0=c2[:, t, :], scalar=ssx[:, t:t + 1], in1=kvg,
                                         op0=ALU.mult, op1=ALU.mult).then_inc(s2_c, 1)
            for b in (7, 0):
                bk.take(b)
            st.done(dve.memset(sel[1][:, 0:P], 0.0))
            st.done(dve.tensor_copy(sel[1][:, P:2 * P], tri[:, :]))
            st.done(dve.tensor_copy(sel[0], tri[:, :]))
            for i in range((NT - 2) * IH):
                t, h = 2 + i // IH, i % IH
                b = 2 * (i % 4)
                bk.take(b)
                dve.wait_ge(free[b], bk.count(b))
                src, w = rl[i % 2][:, 0:(t + 1) * P], wtok[:, t, h:h + 1]
                if h == 0:
                    dve.tensor_scalar(sel[t], src, w, None, ALU.mult).then_inc(s2_acc, 1)
                else:
                    dve.wait_ge(s2_acc, i)
                    dve.scalar_tensor_tensor(out=sel[t], in0=src, scalar=w, in1=sel[t], op0=ALU.mult, op1=ALU.add
                                             ).then_inc(s2_acc, 1)
                if h == IH - 1:
                    dve.wait_ge(s2_acc, i + 1)
                    diag = sel[t][:, t * P:(t + 1) * P]
                    st.done(dve.tensor_tensor(diag, diag, tri[:, :], ALU.add))
            st.wait()

            def select(t):
                for _ in range(TOPK // 8):
                    st.link(dve.max(m8, sel[t]))
                    st.link(dve.match_replace(sel[t], m8, sel[t], TAKEN))
                ts(sel[t], sel[t], TAKEN, MASKED, ALU.is_gt, ALU.mult)

            def scan(f):
                p = f % 2
                dve.wait_ge(s2_w, f + 1)
                for i in range(2):
                    for q in range(HP):
                        qq = f * HP + q
                        if (i, q) == (1, HP - 1):
                            st.wait()
                        z = dve.tensor_tensor_scan(st_[p][:, i, q, :], s5c[:, 0, qq:qq + 1].broadcast_to([P, NC]),
                                                   M1[p][:, i, q, :], 0.0, ALU.mult, ALU.add)
                        if (i, q) == (1, HP - 1):
                            z.then_inc(s2_z, 1)
                        else:
                            st.done(z)

            select(2)
            scan(0)
            select(3)
            scan(1)
            select(4)
            scan(2)
            select(5)
            scan(3)
            select(6)
            select(7)
            bk.n = list(marks["attention"])
            dve.wait_ge(s2_glu, 8)
            dve.wait_ge(s2_ln, 32)

            def att_norm(t):
                dve.wait_ge(free[2], sums2[t])
                st.link(dve.reciprocal(rinv[:, H * t:H * t + H], rsum[:, H * t:H * t + H]))
                o = arrive(7)
                dve.tensor_tensor(att[t % 2].rearrange("p (h d) -> p h d", h=H), o.rearrange("p (h d) -> p h d", h=H),
                                  rinv[:, H * t:H * t + H].unsqueeze(2).broadcast_to([P, H, VD]), ALU.mult
                                  ).then_inc(free[7], 1)

            def att_gate(t):
                o = arrive(6)
                m = mix[:, 0:4, t * P:(t + 1) * P]
                dve.tensor_tensor(m, m, o.rearrange("p (k c) -> p k c", k=4), ALU.mult).then_inc(free[6], 1)

            def residual(t):
                x = xt[t % 2]
                dve.wait_ge(s2_xt[t % 2], 16 * (t // 2 + 1))
                for n in range(2):
                    o = arrive(6 + n)
                    xx = x[:, n * 512:(n + 1) * 512]
                    dve.scalar_tensor_tensor(out=xx, in0=xx, scalar=ALPHA, in1=o, op0=ALU.mult, op1=ALU.add
                                             ).then_inc(free[6 + n], 1)
                for n in range(2):
                    dve.wait_ge(free[6 + n], bk.count(6 + n))
                st.link(dve.tensor_reduce(ssc[:, t:t + 1], x, AX.X, ALU.add))
                ts(ssc[:, t:t + 1], ssc[:, t:t + 1], -1.0 / D, None, ALU.mult)
                dve.tensor_scalar(x, x, ssc[:, t:t + 1], None, ALU.add).then_inc(s2_r, 1)

            def layer_norm(t):
                x = xt[t % 2]
                dve.wait_ge(s2_sq, t + 1)
                st.link(dve.reciprocal(rsx[:, t:t + 1], rsx[:, t:t + 1]))
                stt(x, x, rsx[:, t:t + 1], lng, ALU.mult, ALU.mult)
                dve.tensor_tensor(x, x, lnb, ALU.add).then_inc(s2_o, 1)

            def turned(u):
                t, h = u // H, u % H
                n = min(4, t + 1)
                o = arrive(4)
                if t >= 4:
                    bk.take(5)
                dve.tensor_copy(PT2[h // 4][:, 0:n, (h % 4) * P:(h % 4 + 1) * P],
                                o[:, 0:n * P].rearrange("p (k c) -> p k c", k=n)).then_inc(free[4], 1)

            sums2 = {}
            for u in range(H * NT):
                t, h = u // H, u % H
                b = 2 * (u % 2)
                arrive(b)
                w = (t + 1) * P
                if h == H - 1:
                    sums2[t] = bk.count(b)
                if u >= 2:
                    bp = 2 * (u % 2)
                    dve.wait_ge(full[4 + (((u - 2) // H) >= 4)], bk.count(4 + (((u - 2) // H) >= 4)))
                dve.tensor_tensor_reduce(Pb2[u % 2][:, 0:w], PS[:, b:b + 2, :].rearrange("p a c -> p (a c)")[:, 0:w],
                                         sel[t], -1.0, 3.4e38, ALU.add, ALU.min, negm[:, u:u + 1]).then_inc(s2_nm, 1)
                if u >= 1:
                    turned(u - 1)
                if h == 5:
                    bk.take(6)
                if t >= 1:
                    if h == 1:
                        bk.take(6)
                    if h == 2:
                        att_norm(t - 1)
                    if h == 3:
                        att_gate(t - 1)
                    if h == 4:
                        residual(t - 1)
                    if h == 7:
                        layer_norm(t - 1)
            turned(H * NT - 1)
            bk.take(6)
            att_norm(NT - 1)
            att_gate(NT - 1)
            residual(NT - 1)
            layer_norm(NT - 1)

        @block.gpsimd
        def _(pool):
            bk = Banks(full, free)
            st = Steps(pool, s_pool)
            q3 = q_tok.rearrange("p t (h c) -> p t h c", h=H)
            pool.wait_ge(s_const, 64)
            with pool.Fori(0, L) as l:
                bk.enter(l)
                st.enter(l, 9 * H)
                for n in ROUND[:7]:
                    bk.skip(n)
                pool.wait_ge(s_hrs, l + 1)
                qs, ks = stage[:, 0], stage[:, 1]
                x1p, x2p = qs[:, :, NOPE:NOPE + HR], qs[:, :, NOPE + HR:QK]

                def over(gain, n):
                    return gain.unsqueeze(1).broadcast_to([P, NT, n])

                for h in range(H):
                    rq = rsh[:, 0, :, h:h + 1]
                    rk = rsh[:, 1, :, h:h + 1]
                    if h >= 1:
                        pool.wait_ge(full[7], bk.count(7) - 2)
                    st.link(pool.tensor_tensor(qs, q3[:, :, h, :], rq.broadcast_to([P, NT, QK]), ALU.mult))
                    st.link(pool.tensor_tensor(qs, qs, over(gq[:, :], QK), ALU.mult))
                    st.done(pool.tensor_tensor(rtp[:, 0], x1p, cosT[:, :, :], ALU.mult))
                    st.done(pool.tensor_tensor(rtp[:, 1], x2p, sinT[:, :, :], ALU.mult))
                    st.done(pool.tensor_tensor(rtp[:, 2], x2p, cosT[:, :, :], ALU.mult))
                    st.link(pool.tensor_tensor(rtp[:, 3], x1p, sinT[:, :, :], ALU.mult))
                    st.link(pool.tensor_tensor(x1p, rtp[:, 0], rtp[:, 1], ALU.subtract))
                    pool.tensor_tensor(x2p, rtp[:, 2], rtp[:, 3], ALU.add).then_inc(s_stage, 1)
                    if h >= 1:
                        pool.wait_ge(full[7], bk.count(7))
                    st.link(pool.tensor_tensor(ks[:, :, 0:NOPE], k_tok[:, :, h, :],
                                               rk.broadcast_to([P, NT, NOPE]), ALU.mult))
                    st.link(pool.tensor_tensor(ks[:, :, 0:NOPE], ks[:, :, 0:NOPE], over(gk[:, 0:NOPE], NOPE),
                                               ALU.mult))
                    pool.tensor_tensor(ks[:, :, NOPE:QK], kro[:, :, :], rk.broadcast_to([P, NT, ROPE]), ALU.mult
                                       ).then_inc(s_stage, 1)
                    for _ in range(4):
                        bk.take(7)
                for b, n in enumerate(FIXED):
                    if b != 7:
                        bk.n[b] += n
                for n in ROUND[7:]:
                    bk.skip(n)
            bk.leave(L)
            st.leave(L)

            pool.wait_ge(s2_prep, 1)
            def mul(o, x, y):
                st.done(pool.tensor_tensor(o, x, y, ALU.mult))

            def add(o, x, y, op=ALU.add):
                return pool.tensor_tensor(o, x, y, op)

            def prep(f):
                p = f % 2
                if f == 0:
                    pool.wait_ge(free[7], marks["C"][0])
                    pool.wait_ge(free[0], marks["C"][1])
                if f >= 2:
                    pool.wait_ge(full[7], marks["y", f - 2])
                qs = slice(f * HP, (f + 1) * HP)
                g = [G[p][:, i] for i in range(2)]
                tmp0 = ca_re[p]
                tmp1 = ca_ni[p]
                b4 = [Bb[:, i, qs, :].unsqueeze(2).broadcast_to([P, HP, CL, CH]) for i in range(2)]
                a4 = [apow[:, i, qs, :].unsqueeze(3).broadcast_to([P, HP, CL, CH]) for i in range(2)]
                b3 = [Bb[:, i, qs, :].unsqueeze(2).broadcast_to([P, HP, CL - 1, CH]) for i in range(2)]
                r3 = [apow[:, i, qs, CL - 2::-1].unsqueeze(3).broadcast_to([P, HP, CL - 1, CH]) for i in range(2)]
                lo = slice(0, CL - 1)
                mul(g[0][:, :, lo], b3[0], r3[0])
                mul(tmp0[:, :, lo], b3[1], r3[1])
                mul(g[1][:, :, lo], b3[0], r3[1])
                mul(tmp1[:, :, lo], b3[1], r3[0])
                st.done(pool.tensor_copy(g[0][:, :, CL - 1], Bb[:, 0, qs, :]))
                st.done(pool.tensor_copy(g[1][:, :, CL - 1], Bb[:, 1, qs, :]))
                st.wait()
                st.link(add(g[0][:, :, lo], g[0][:, :, lo], tmp0[:, :, lo], ALU.subtract))
                add(g[1][:, :, lo], g[1][:, :, lo], tmp1[:, :, lo]).then_inc(s2_G, 1)
                pool.wait_ge(s2_G, f + 1)
                c4 = [CT[:, i, qs, :].unsqueeze(2).broadcast_to([P, HP, CL, CH]) for i in range(2)]
                s4 = part(r3a, 0, f)[:, 0:512].rearrange("p (q i c) -> p q i c", q=HP, i=CL)
                mul(ca_re[p], c4[0], a4[0])
                mul(s4, c4[1], a4[1])
                mul(ca_ni[p], c4[1], a4[0])
                st.wait()
                st.link(add(ca_re[p], ca_re[p], s4))
                mul(s4, c4[0], a4[1])
                st.wait()
                add(ca_ni[p], ca_ni[p], s4, ALU.subtract).then_inc(s2_CA, 1)
                pool.wait_ge(free[3], marks["kernel", f])
                gs = slice(2 * HP * f, 2 * HP * (f + 1))
                st.link(pool.tensor_tensor(dtmp, ident[0:CH, 0:CH].unsqueeze(1).broadcast_to([CH, 2 * HP, CH]),
                                           DT[:, gs].unsqueeze(2).broadcast_to([CH, 2 * HP, CH]), ALU.mult))
                add(K16[p][:, :, 0:CH], K16[p][:, :, 0:CH], dtmp).then_inc(s2_K, 1)

            def rotate(f):
                p = f % 2
                pool.wait_ge(s2_TT[f % 2], 16 * CL * (f // 2 + 1))
                R = rot[p]
                qs = slice(f * HP, (f + 1) * HP)
                st.done(pool.memset(R[:, 0, :, 0:1], 1.0))
                st.done(pool.memset(R[:, 1, :, 0:1], 0.0))
                st.done(pool.tensor_copy(R[:, 0, :, 1:2], s5c[:, 1, qs].unsqueeze(2)))
                st.done(pool.tensor_copy(R[:, 1, :, 1:2], s5c[:, 2, qs].unsqueeze(2)))
                st.wait()
                W0, W1 = M1[p][:, 0], M1[p][:, 1]
                pool.wait_ge(full[5], marks["states", f])
                n = 2
                while n < NC:
                    hr, hi = R[:, 0, :, n // 2:n // 2 + 1], R[:, 1, :, n // 2:n // 2 + 1]
                    dr, di = R[:, 0, :, n:n + 1], R[:, 1, :, n:n + 1]
                    t0, t1 = W0[:, :, 0:1], W0[:, :, 1:2]
                    mul(t0, hr, hr)
                    mul(t1, hi, hi)
                    mul(di, hr, hi)
                    st.wait()
                    st.done(add(dr, t0, t1, ALU.subtract))
                    st.link(add(di, di, di))
                    if n > 1:
                        m = n - 1
                        br = dr.broadcast_to([P, HP, m])
                        bi = di.broadcast_to([P, HP, m])
                        cr, ci = R[:, 0, :, 1:n], R[:, 1, :, 1:n]
                        er_, ei_ = R[:, 0, :, n + 1:2 * n], R[:, 1, :, n + 1:2 * n]
                        w0, w1 = W0[:, :, 0:m], W1[:, :, 0:m]
                        mul(er_, cr, br)
                        mul(w0, ci, bi)
                        mul(ei_, cr, bi)
                        mul(w1, ci, br)
                        st.wait()
                        st.done(add(er_, er_, w0, ALU.subtract))
                        st.link(add(ei_, ei_, w1))
                    n *= 2
                pool.wait_ge(free[5], marks["states", f])
                sr, si = st_[p][:, 0], st_[p][:, 1]
                mul(W0, R[:, 0], sr)
                mul(W1, R[:, 1], si)
                st.wait()
                st.link(add(W0, W0, W1))
                mul(W1, R[:, 0], si)
                mul(sr, R[:, 1], sr)
                st.wait()
                add(W1, W1, sr, ALU.subtract).then_inc(s2_w, 1)

            def rotate_back(f):
                p = f % 2
                pool.wait_ge(s2_z, f + 1)
                m = NC - 1
                zr, zi = st_[p][:, 0, :, 0:m], st_[p][:, 1, :, 0:m]
                Rr, Ri = rot[p][:, 0, :, 0:m], rot[p][:, 1, :, 0:m]
                X0, X1 = X[p][:, 0, :, 1:NC], X[p][:, 1, :, 1:NC]
                st.done(pool.memset(X[p][:, 0, :, 0:1], 0.0))
                st.done(pool.memset(X[p][:, 1, :, 0:1], 0.0))
                mul(X0, Rr, zr)
                mul(X1, Ri, zr)
                st.wait()
                mul(zr, Ri, zi)
                mul(zi, Rr, zi)
                st.wait()
                st.link(add(X0, X0, zr, ALU.subtract))
                add(X1, X1, zi).then_inc(s2_X, 1)

            pool.wait_ge(s2_acc, (NT - 2) * IH)
            st.link(pool.memset(TT[0], 0.0))
            pool.memset(TT[1], 0.0).then_inc(s2_TT0, 1)
            pool.wait_ge(s2_TT0, 1)
            prep(0)
            for f in range(4):
                if f < 3:
                    prep(f + 1)
                rotate(f)
                rotate_back(f)
            for m in range(4):
                for n in range(2):
                    i = 2 * m + n
                    b, c = marks["glu", i]
                    pool.wait_ge(free[b], c)
                    y = mix[:, 4 + m, n * 512:(n + 1) * 512]
                    st.link(pool.tensor_tensor(vb[i % 2], vb[i % 2], gb[i % 2], ALU.mult))
                    pool.tensor_tensor(y, y, vb[i % 2], ALU.mult).then_inc(s2_glu, 1)


def tables():
    inv = 10000.0 ** (-np.arange(HR, dtype=np.float32) / HR)
    ang = np.arange(S, dtype=np.float32)[:, None] * inv[None].astype(np.float32)
    d = np.arange(P, dtype=np.float64)
    pd = 2 * np.pi * ((d[:, None] * d[None]) % P) / P
    s = np.arange(S // 2)[:, None] * np.arange(S)[None]
    ps = 2 * np.pi * (s % S).astype(np.float64) / S
    seq = np.concatenate([np.cos(ps), -np.sin(ps)])
    seq[S // 2] = 1 - 2.0 * (np.arange(S) % 2)
    f = np.float32
    return {
        "c_ident": np.eye(P, dtype=f),
        "c_cos": np.cos(ang.astype(np.float64)).astype(f), "c_sin": np.sin(ang.astype(np.float64)).astype(f),
        "c_tri": np.where(np.arange(P)[None] <= np.arange(P)[:, None], 0, MASKED).astype(f),
        "c_dft_d": np.concatenate([np.cos(pd), np.sin(pd)], 1).astype(f),
        "c_dft_s": (seq / np.sqrt(S * P)).astype(f),
    }


def kernel(**inputs):
    import concourse.bacc as _bacc
    from concourse.bass_utils import run_bass_kernel_spmd as _run

    nc = _bacc.Bacc("TRN2", target_bir_lowering=False, num_devices=1)
    arrays, a = {}, {}
    for name, v in {**inputs, **tables()}.items():
        v = np.ascontiguousarray(v)
        arrays[f"in_{name}"] = v
        a[name] = nc.dram_tensor(f"in_{name}", v.shape, mybir.dt.from_np(v.dtype), kind="ExternalInput").ap()
    out = nc.dram_tensor("out_0", (1, S, D), F32, kind="ExternalOutput").ap()
    build(nc, a, out)
    r = _run(nc, [arrays], core_ids=[0])
    return r.results[0]["out_0"]
```

```python
from contextlib import ExitStack

import numpy as np

import concourse.bass as bass
from concourse import mybir

ALU = mybir.AluOpType
ACT = mybir.ActivationFunctionType
AX = mybir.AxisListType
F32 = mybir.dt.float32
F32R = mybir.dt.float32r

P = 128
S = 1024
D = 1024
NT = S // P
KD = D // P
L = 2
H = 8
QL = KVL = 256
NOPE, ROPE, VD = 64, 32, 64
QK = NOPE + ROPE
HR = ROPE // 2
AW = H * VD
FW = 512
FG = FW // P
HF = S // 2 + 1
EPS = 1e-6
C_PE, C_ZA, C_U, C_ZF = 512, 544, 1056, 1568
C_GA, C_GF = 2080, 3104
H_ACT = 6
N_SPLIT = 8 + 2 * KD
UNITS = H * NT
N_ROWS = KD + 4 + 2 * KD

ROUND = [1 + 2 * NT, 2 * NT, 8, NT, 4 * NT, NT + 1, 9, NT, 8, 8, 8 * KD, 2 * NT]
FIXED = [UNITS // 2, 0, UNITS // 2, 0, UNITS, UNITS, H, 4 * H]
BANK_USES = [sum((n + 7 - b) // 8 for n in ROUND) + FIXED[b] for b in range(8)]

CHUNKS = [(3, "c"), (1, "u"), (2, "up"), (1, "dft"), (1, "za"), (1, "zf")]
CHUNKS += [(4, f"gate{m}") for m in range(KD)] + [(1, "out0"), (1, "out1")]
W_SLOTS = 2
C_COLS = QL + KVL + ROPE
W_DMAS = [sum(n for n, _ in CHUNKS[s::W_SLOTS]) for s in range(W_SLOTS)]
W_TAKES = [sum(n > 0 for n, _ in CHUNKS[s::W_SLOTS]) for s in range(W_SLOTS)]

KVC = 128
IH, ID = 8, 32
TOPK = 256
CH, NG, NST = 16, 32, 64
SW = CH * NG
CL = 8
NC = S // CL
NPAIR = NG // 2
HP = NPAIR // 4
ALPHA = 2 ** 0.25
LN_EPS = 1e-5
MASKED = -3.0e38
TAKEN = -3.4e38
C2_C, C2_GA, C2_U, C2_GS = 512, 936, 1448, 1960
NIDX = C2_GA - C2_C
S5_LOADS = 4 + 2
CHUNKS2 = ["idx", "u", "ga", "gs", "glu", "q", "out0", "out1"]


class Banks:

    def __init__(self, full, free):
        self.full, self.free = full, free
        self.n = [1] * 8
        self.layer = None

    def enter(self, layer):
        self.layer, self.start = layer, list(self.n)

    def leave(self, layers):
        assert [n - s for n, s in zip(self.n, self.start)] == BANK_USES, (self.n, self.start, BANK_USES)
        self.layer = None
        self.n = [s + layers * u for s, u in zip(self.start, BANK_USES)]

    def count(self, b):
        return self.n[b] if self.layer is None else self.layer * BANK_USES[b] + self.n[b]

    def take(self, b):
        self.n[b] += 1
        return self.count(b) - 1 if self.layer is None else self.layer * BANK_USES[b] + (self.n[b] - 1)

    def skip(self, n):
        for i in range(n):
            self.n[i % 8] += 1


class Steps:

    def __init__(self, eng, sem):
        self.eng, self.sem, self.n, self.layer, self.per = eng, sem, 0, None, 0

    def enter(self, layer, per):
        self.layer, self.per, self.start = layer, per, self.n

    def leave(self, layers):
        assert self.n - self.start == self.per, (self.n - self.start, self.per)
        self.layer, self.n = None, self.start + layers * self.per

    def done(self, ins):
        ins.then_inc(self.sem, 1)
        self.n += 1

    def wait(self):
        self.eng.wait_ge(self.sem, self.n if self.layer is None else self.layer * self.per + self.n)

    def link(self, ins):
        self.done(ins)
        self.wait()


def build(nc, a, out, dbg=None):
    with ExitStack() as ctx:
        def sb(name, shape, dt=F32):
            return ctx.enter_context(nc.sbuf_tensor(name, shape, dt))

        def sb2(name, rounded, shape):
            with nc.sbuf_tensor(name, shape, F32) as plain:
                pass
            return plain, sb(rounded, shape, F32R)

        def sem(name):
            return ctx.enter_context(nc.semaphore(name))

        PS = ctx.enter_context(nc.psum_tensor("PS", [P, 8, 512], F32))

        hT, hHi = sb2("hT", "hHi", [P, KD, S])
        R0 = sb("R0", [P, 8, 1024])
        R1, hLo = sb2("R1", "hLo", [P, 8, 1024])
        R2a, R2aR = sb2("R2a", "R2aR", [P, 4, 1024])
        R2b = sb("R2b", [P, 4, 1024])
        R3a, R3aR = sb2("R3a", "R3aR", [P, 4, 1024])
        R3b = sb("R3b", [P, 4, 1024])
        W, WR = sb2("W", "WR", [P, W_SLOTS, KD * C_COLS])
        ident = sb("ident", [P, P])
        dft_d = sb("dft_d", [P, 2 * P])
        u_mid = sb("u_mid", [P, FG, P])
        cosT = sb("cosT", [P, NT, HR])
        sinT = sb("sinT", [P, NT, HR])
        eps = sb("eps", [P, 1])
        rows = sb("rows", [P, P])
        pT = sb("pT", [P, N_ROWS])
        gq = sb("gq", [P, QK])
        gk = sb("gk", [P, QK])
        ssx = sb("ssx", [P, NT])
        rsx = sb("rsx", [P, NT])
        ssc = sb("ssc", [P, 2 * NT])
        ssh = sb("ssh", [P, 2, NT, H])
        rsh = sb("rsh", [P, 2, NT, H])
        kpe = sb("kpe", [P, NT, ROPE])
        kro = sb("kro", [P, NT, ROPE])
        rt = sb("rt", [P, 4, NT, HR])
        rtp = sb("rtp", [P, 4, NT, HR])
        negm = sb("negm", [P, UNITS])
        rsum = sb("rsum", [P, UNITS])
        rinv = sb("rinv", [P, UNITS])

        mark = sb("mark", [P, 1])
        epsl = sb("epsl", [P, 1])

        x1 = R1
        xn = [R2a[:, t, :] if t < 4 else R2b[:, t - 4, :] for t in range(NT)]
        c_tok = R2a[:, :, :].rearrange("p a b -> p (a b)").rearrange("p (t c) -> p t c", t=NT)
        cT = R2b
        uT = R3a
        fold = R3b[:, :, :].rearrange("p a b -> p (a b)").rearrange("p (g e s) -> p g e s", g=FG, e=2)
        V = R3a[:, :, :].rearrange("p a b -> p (a b)").rearrange("p (j c) -> p j c", j=NT)
        fT = R3b
        odd = R2a[:, 0:2, :].rearrange("p a b -> p (a b)").rearrange("p (g s) -> p g s", g=FG)
        v_mid = R2a[0:1, 2, 0:512]
        r0 = R0[:, :, :].rearrange("p a b -> p (a b)")
        r1 = R1[:, :, :].rearrange("p a b -> p (a b)")
        q_tok = r0[:, 0:NT * H * QK].rearrange("p (t c) -> p t c", t=NT)
        stage = r0[:, NT * H * QK:NT * H * QK + 2 * NT * QK].rearrange("p (s t c) -> p s t c", s=2, t=NT)
        tmp = r0[:, NT * H * QK:NT * H * QK + 1024].rearrange("p (i c) -> p i c", i=2)
        k_tok = r1[:, 0:4096].rearrange("p (t h c) -> p t h c", t=NT, h=H)
        v_tok = r1[:, 4096:8192].rearrange("p (t h c) -> p t h c", t=NT, h=H)
        r2a = R2a[:, :, :].rearrange("p a b -> p (a b)")
        o_tok = r2a.rearrange("p (t c) -> p t c", t=NT)
        Pb = [R2b[:, 0, :], R2b[:, 1, :]]
        PT = [R2b[:, 2, :], R2b[:, 3, :]]
        qkT = [[R3aR[:, i, :], R3aR[:, 2 + i, :]] for i in range(2)]
        qk_lo = WR[:, 1, 0:4096].rearrange("p (i s) -> p i s", i=4)
        qkT_lo = [[qk_lo[:, i, :], qk_lo[:, 2 + i, :]] for i in range(2)]
        oT = R2b
        mT = R0
        hTmp = [R3aR[:, 2 * (k % 2), :] if k < 4 else R3aR[:, k - 4, :] for k in range(KD)]
        wHi = [R2aR[:, 2 * i, :].rearrange("p (k c) -> p k c", k=8) for i in range(2)]
        wLo = [R2aR[:, 2 * i + 1, :].rearrange("p (k c) -> p k c", k=8) for i in range(2)]
        sg = R3a[:, :, :].rearrange("p a b -> p (a b)").rearrange("p (i c) -> p i c", c=512)

        def flat(t):
            return t[:, :, :].rearrange("p a b -> p (a b)")

        r3a, r3b, r2b, hTf = flat(R3a), flat(R3b), flat(R2b), flat(hT)
        xT = hT
        sel, at = [], 0
        for t in range(NT):
            w = (t + 1) * P
            half, lo = (r2a, at) if t < 7 else (r2b, 0)
            sel.append(half[:, lo:lo + w])
            at += w
        c2 = r2b[:, 1024:2048].rearrange("p (t c) -> p t c", t=NT)
        c2T = r2b[:, 2048:3072]
        kiz = r0[:, 0:4096].rearrange("p (i s) -> p i s", i=4)
        qiT = r3a[:, 0:2048].rearrange("p (m s) -> p m s", m=2)
        rl = [r3a[:, 2048:3072], r3a[:, 3072:4096]]
        wtok = ssh[:, 0, :, :]
        m8 = ssc[:, 0:8]
        U = r0[:, 0:4096].rearrange("p (j c) -> p j c", j=CL)
        U4 = r0[:, 0:4096].rearrange("p (g j c) -> p g j c", g=NG, j=CL)
        Y = U
        UT = r0[:, 4096:8192].rearrange("p (g c) -> p g c", g=NG)
        yT = r0[:, 4096:8192].rearrange("p (k s) -> p k s", k=4)
        prow = r3b[:, 3328:3712].rearrange("p (i c) -> p i c", i=3)
        lrow = r3b[0:NPAIR, 3712:3714]
        drow = r3b[0:NG, 3716:3716 + CH]
        craw = r3b[:, 0:1024].rearrange("p (i c) -> p i c", i=8)
        lam = r3b[:, 1024:1072].rearrange("p (i q) -> p i q", i=3)
        scr = r3b[:, 1088:1088 + 40 * NPAIR].rearrange("p (i q) -> p i q", i=40)
        CT = flat(u_mid).rearrange("p (i q c) -> p i q c", i=2, q=NPAIR)
        Bb = rt[:, :, :, :].rearrange("p a b c -> p (a b c)").rearrange("p (i q c) -> p i q c", i=2, q=NPAIR)
        Braw = r3b[:, 1728:2240].rearrange("p (i q c) -> p i q c", i=2, q=NPAIR)
        s5c = gk[:, 0:3 * NPAIR].rearrange("p (i q) -> p i q", i=3)
        apow = kpe[:, :, :].rearrange("p a b -> p (a b)").rearrange("p (i q j) -> p i q j", i=2, q=NPAIR)

        def part(t, lo, f, n=1024):
            return t[:, lo + n * (f % 2):lo + n * (f % 2) + n]

        G = [part(r3b, 0, f).rearrange("p (i q j c) -> p i q j c", i=2, q=HP, j=CL) for f in range(2)]
        st_ = [part(r3b, 0, f).rearrange("p (i q c) -> p i q c", i=2, q=HP) for f in range(2)]
        M1 = [part(r3b, 2048, f).rearrange("p (i q c) -> p i q c", i=2, q=HP) for f in range(2)]
        X = M1
        K16 = [part(r3a, 0, f)[0:CH].rearrange("p (g c) -> p g c", g=2 * HP) for f in range(2)]
        rot = [part(r3a, 0, f).rearrange("p (i q c) -> p i q c", i=2, q=HP) for f in range(2)]
        TT = [part(r3a, 2048, f).rearrange("p (g c) -> p g c", g=2 * HP) for f in range(2)]
        ca_re = [part(r2b, 3072, f, 512).rearrange("p (q i c) -> p q i c", q=HP, i=CL) for f in range(2)]
        ca_ni = [x.rearrange("p (q i c) -> p q i c", q=HP, i=CL) for x in
                 (r2a[:, 3584:4096], rtp[:, :, :, :].rearrange("p a b c -> p (a b c)"))]
        mix = R1
        DT = rinv[0:CH, 0:NG]
        dtmp = kro[0:CH, 0:2 * HP, 0:CH]
        vb = [r3b[:, 0:512], r3b[:, 512:1024]]
        gb = [r3b[:, 1024:1536], r3b[:, 1536:2048]]
        kvg = sinT[:, :, :].rearrange("p a b -> p (a b)")
        qT2 = R3a
        wuk = r3b[:, 2048:2560]
        wukT = CT.rearrange("p i q c -> p (i q c)").rearrange("p (m c) -> p m c", m=4)
        wuv = Bb.rearrange("p i q c -> p (i q c)").rearrange("p (h d) -> p h d", h=H)
        qlT = R0
        Pb2 = [r3b[:, 0:1024], r3b[:, 1024:2048]]
        xt = [r3b[:, 2048:3072], r3b[:, 3072:4096]]
        lng, lnb = r3a[:, 0:1024], r3a[:, 1024:2048]
        att = [r3a[:, 2048:2560], r3a[:, 2560:3072]]
        olT = [r3a[:, 3072:3584], r3a[:, 3584:4096]]
        PT2 = [hTf[:, i * 4096:(i + 1) * 4096].rearrange("p (k c) -> p k c", k=NT) for i in range(2)]
        tri = dft_d[:, 0:P]
        ki4 = r3b[:, 2304:2304 + KD * 4 * ID].rearrange("p (k c) -> p k c", k=KD)

        xres = nc.dram_tensor("xres", (S, D), F32, kind="Internal").ap()

        full = [sem(f"bank_full{b}") for b in range(8)]
        free = [sem(f"bank_free{b}") for b in range(8)]
        w_in_slot = [sem(f"w_loaded{s}") for s in range(W_SLOTS)]
        w_used = [sem(f"w_used{s}") for s in range(W_SLOTS)]
        s_const = sem("constants_loaded")
        s_xin = sem("x_loaded")
        s_par = sem("parameters_loaded")
        s_xsave = sem("x_saved")
        s_xback = sem("x_reloaded")
        s_init = sem("memsets_done")
        s_std = sem("x_std_ready")
        s_xn = sem("x_normed")
        s_hT = sem("hT_ready")
        s_pT = sem("parameters_turned")
        s_c = sem("c_evacuated")
        s_cstd = sem("c_std_ready")
        s_cn = sem("c_normed")
        s_cT = sem("cT_ready")
        s_kpe = sem("kpe_evacuated")
        s_uT = sem("uT_ready")
        s_fold = sem("folded")
        s_V = sem("spectrum_ready")
        s_fT = sem("fT_ready")
        s_sq = sem("head_squares_ready")
        s_ss = sem("head_sums_ready")
        s_q = sem("q_evacuated")
        s_ssall = sem("all_head_sums_ready")
        s_hstd = sem("head_std_ready")
        s_hrs = sem("head_rstd_ready")
        s_stage = sem("qk_staged")
        s_qkT = sem("qkT_rounded")
        s_nm = sem("neg_max_ready")
        s_o = sem("head_output_ready")
        s_oT = sem("oT_ready")
        s_hhi = sem("h_rounded")
        s_hlo = sem("h_rest_ready")
        s_hin = [sem(f"h_rounded_in_place_{e}") for e in ("act", "pool")]
        s_whi = sem("unit_weights_rounded")
        s_wlo = sem("unit_weights_rest_ready")
        s_wdone = sem("unit_weights_used")
        s_sm = sem("silu_multiplied")
        s_sig = sem("sigmoid_ready")
        s_sigused = sem("sigmoid_used")
        s_mT = sem("mT_ready")
        s_xnew = sem("x_new_ready")
        s2_par = sem("second_parameters_loaded")
        s2_rows = sem("second_rows_loaded")
        s2_ld = sem("log_dt_spread")
        s2_ki = sem("indexer_key_weights_repeated")
        s2_kz = sem("indexer_key_zeros_ready")
        s2_c = sem("second_latent_normed")
        s2_relu = sem("index_relu_ready")
        s2_acc = sem("index_relu_added")
        s2_sel = sem("selection_ready")
        s2_prep = sem("s5_parameters_ready")
        s2_G = sem("s5_input_powers_ready")
        s2_CA = sem("s5_output_powers_ready")
        s2_K = sem("s5_kernel_ready")
        s2_TT = [sem(f"s5_toeplitz_loaded{i}") for i in range(2)]
        s2_TT0 = sem("s5_toeplitz_zeroed")
        s2_R = sem("s5_rotations_ready")
        s2_w = sem("s5_states_turned_back")
        s2_z = sem("s5_scanned")
        s2_X = sem("s5_states_ready")
        s2_glu = sem("glu_ready")
        s2_wk = sem("wuk_loaded")
        s2_wv = sem("wuv_loaded")
        s2_ln = sem("ln_parameters_loaded")
        s2_nm = sem("masked_scores_ready")
        s2_xt = [sem(f"x_tile_loaded{i}") for i in range(2)]
        s2_r = sem("centred_ready")
        s2_sq = sem("ln_std_ready")
        s2_o = sem("out_tile_ready")
        s2_od = [sem(f"out_tile_written{i}") for i in range(2)]
        s_dve = sem("dve_steps")
        s_act = sem("act_steps")
        s_pool = sem("pool_steps")
        s_out = sem("output_written")

        def unit_chunk(c):
            return 4 + c // 4 if c < 8 else 6 + (c - 8) // 2

        def unit_weights(eng, l, c):
            i = unit_chunk(c)
            s = i % W_SLOTS
            eng.wait_ge(w_in_slot[s], 16 * (l * W_DMAS[s] + sum(n for n, _ in CHUNKS[s:i + 1:W_SLOTS])))
            if c < 8:
                return W[:, s, 0:4096].rearrange("p (k c) -> p k c", k=8)[:, :, (c % 4) * P:(c % 4 + 1) * P]
            return W[:, s, (c % 2) * 1024:(c % 2 + 1) * 1024].rearrange("p (k c) -> p k c", k=8)

        marks = {}
        block = ctx.enter_context(nc.Block())

        @block.tensor
        def _(pe):
            bk = Banks(full, free)
            pe.wait_ge(s_const, 64)
            pe.wait_ge(s_init, 3)

            def begin(b):
                pe.wait_ge(free[b], bk.take(b))
                return PS[:, b, :]

            def weights(l, i):
                s = i % W_SLOTS
                pe.wait_ge(w_in_slot[s], 16 * (l * W_DMAS[s] + sum(n for n, _ in CHUNKS[s:i + 1:W_SLOTS])))
                return W[:, s, :]

            def k_of(slot):
                return slot[:, 0:4096].rearrange("p (k c) -> p k c", k=8)

            with pe.Fori(0, L) as l:
                bk.enter(l)
                pe.wait_ge(s_par, 96 * l + 96)
                b0 = begin(0)
                pe.transpose(b0[:, 0:P], rows[:, :], ident[:, :]).then_inc(full[0], 1)
                hT_free = []
                for t in range(NT):
                    pe.wait_ge(s_xn, l * NT + t + 1)
                    for j in range(2):
                        b = (1 + 2 * t + j) % 8
                        o = begin(b)
                        for k in range(4):
                            f = 4 * j + k
                            mm = pe.transpose(o[:, k * P:(k + 1) * P], xn[t][:, f * P:(f + 1) * P], ident[:, :])
                        mm.then_inc(full[b], 1)
                    hT_free.append((b, bk.count(b)))
                wc = weights(l, 0).rearrange("p (k c) -> p k c", k=8)
                for t in range(NT):
                    pe.wait_ge(free[hT_free[t][0]], hT_free[t][1])
                    b = (2 * t) % 8
                    for lo, hi, o in ((0, QL + ROPE, begin(b)), (QL + ROPE, C_COLS, begin(b + 1))):
                        for k in range(KD):
                            mm = pe.matmul(o[:, 0:hi - lo], hT[:, k, t * P:(t + 1) * P], wc[:, k, lo:hi],
                                           start=(k == 0), stop=(k == 7))
                        mm.then_inc(full[b + (lo > 0)], 1)
                wu = k_of(weights(l, 1))
                for m in range(4):
                    for n in range(2):
                        b = 2 * m + n
                        o = begin(b)
                        for k in range(KD):
                            mm = pe.matmul(o, wu[:, k, m * P:(m + 1) * P], hT[:, k, n * 512:(n + 1) * 512],
                                           start=(k == 0), stop=(k == 7))
                            if m == n == k == 0:
                                mm.then_inc(w_used[0], 1)
                        mm.then_inc(full[b], 1)
                for t in range(NT):
                    pe.wait_ge(s_cn, l * NT + t + 1)
                    o = begin(t % 8)
                    for k in range(4):
                        mm = pe.transpose(o[:, k * P:(k + 1) * P], c_tok[:, t, k * P:(k + 1) * P], ident[:, :])
                        if t == k == 0:
                            mm.then_inc(w_used[1], 1)
                    mm.then_inc(full[t % 8], 1)
                cT_free = [bk.count(b) for b in range(8)]
                wup = weights(l, 2)
                wq = wup[:, 0:2 * H * QK].rearrange("p (k c) -> p k c", k=2)
                wkv = wup[:, 2 * H * QK:2 * H * QK + 2048].rearrange("p (k c) -> p k c", k=2)
                for t in range(NT):
                    pe.wait_ge(free[t], cT_free[t])
                    for j in range(4):
                        b = (4 * t + j) % 8
                        o = begin(b)
                        for k in range(2):
                            if j < 2:
                                mm = pe.matmul(o[:, 0:4 * QK], cT[:, k, t * P:(t + 1) * P],
                                               wq[:, k, j * 4 * QK:(j + 1) * 4 * QK], start=(k == 0), stop=(k == 1))
                            else:
                                mm = pe.matmul(o, cT[:, 2 + k, t * P:(t + 1) * P],
                                               wkv[:, k, (j - 2) * 512:(j - 1) * 512], start=(k == 0), stop=(k == 1))
                        mm.then_inc(full[b], 1)
                pe.wait_ge(s_fold, l + 1)
                for j in range(NT):
                    o = begin(j % 8)
                    e, s0 = j // 4, (j % 4) * P
                    for g in range(FG):
                        og = o[:, g * P:(g + 1) * P]
                        mm = pe.matmul(og, fold[:, g, e, s0:s0 + P], dft_d[:, e * P:(e + 1) * P],
                                       start=True, stop=True)
                        if j == g == 0:
                            mm.then_inc(w_used[0], 1)
                    mm.then_inc(full[j % 8], 1)
                o = begin(0)
                for g in range(FG):
                    mm = pe.matmul(o[0:1, g * P:(g + 1) * P], u_mid[:, g, 0:1], dft_d[:, 0:P], start=True, stop=True)
                mm.then_inc(full[0], 1)
                pe.wait_ge(free[7], bk.count(7))
                pe.wait_ge(free[0], bk.count(0))
                wd = weights(l, 3)[:, 0:KD * HF].rearrange("p (k c) -> p k c", k=8)
                for g in range(FG):
                    gs = slice(g * P, (g + 1) * P)
                    o = begin(g)
                    for j in range(4):
                        pe.matmul(o, V[:, j, gs], wd[:, j, 0:512], start=(j == 0), stop=False)
                    pe.matmul(o, v_mid[:, gs], wd[0:1, 4, 0:512], start=False, stop=True).then_inc(full[g], 1)
                    o = begin(4 + g)
                    for j in range(4, 8):
                        mm = pe.matmul(o, V[:, j, gs], wd[:, j, 0:512], start=(j == 4), stop=(j == 7))
                    mm.then_inc(full[4 + g], 1)
                o = begin(0)
                for g in range(FG):
                    gs = slice(g * P, (g + 1) * P)
                    for j in range(4):
                        pe.matmul(o[:, g:g + 1], V[:, j, gs], wd[:, j, 512:HF], start=(j == 0), stop=False)
                    mm = pe.matmul(o[:, g:g + 1], v_mid[:, gs], wd[0:1, 4, 512:HF], start=False, stop=True)
                mm.then_inc(full[0], 1)

                def qk_turn(h, i):
                    pe.wait_ge(s_stage, l * 2 * H + 2 * h + i // 2 + 1)
                    o = begin(7)
                    for j in range(4):
                        t = 4 * (i % 2) + j
                        mm = pe.transpose(o[0:QK, j * P:(j + 1) * P], stage[:, i // 2, t, :], ident[:, :])
                        if h == i == j == 0:
                            mm.then_inc(w_used[1], 1)
                    mm.then_inc(full[7], 1)

                def scores(u):
                    h, t = u // NT, u % NT
                    b = 2 * (u % 2)
                    if u < 2:
                        pe.wait_ge(free[b + 1], bk.count(b + 1))
                    begin(b)
                    if t == 0:
                        pe.wait_ge(free[7], bk.count(7))
                    (qh, kh), (ql, kl) = qkT[h % 2], qkT_lo[h % 2]
                    for n in range(2):
                        for i, (x, y) in enumerate(((qh, kh), (qh, kl), (ql, kh))):
                            mm = pe.matmul(PS[:, b + n, :], x[0:QK, t * P:(t + 1) * P],
                                           y[0:QK, n * 512:(n + 1) * 512], start=(i == 0), stop=(i == 2))
                    mm.then_inc(full[b], 1)

                def p_turn(u):
                    pe.wait_ge(free[2 * (u % 2)], bk.count(2 * (u % 2)))
                    for j in range(2):
                        o = begin(4 + j)
                        for k in range(4):
                            c = 4 * j + k
                            mm = pe.transpose(o[:, k * P:(k + 1) * P], Pb[u % 2][:, c * P:(c + 1) * P], ident[:, :])
                        mm.then_inc(full[4 + j], 1)
                    pt_count.append((bk.count(4), bk.count(5)))

                def pv(u):
                    h, t = u // NT, u % NT
                    if t == 0:
                        begin(6)
                    pe.wait_ge(free[4], pt_count[u][0])
                    pe.wait_ge(free[5], pt_count[u][1])
                    for k in range(NT):
                        mm = pe.matmul(PS[:, 6, t * VD:(t + 1) * VD], PT[u % 2][:, k * P:(k + 1) * P],
                                       v_tok[:, k, h, :], start=(k == 0), stop=(k == 7))
                    if t == NT - 1:
                        mm.then_inc(full[6], 1)

                pt_count = []
                for i in range(4):
                    qk_turn(0, i)
                scores(0)
                for u in range(UNITS + 1):
                    if u + 1 < UNITS:
                        scores(u + 1)
                    if u >= 1:
                        pv(u - 1)
                    if u < UNITS:
                        p_turn(u)
                    if 1 <= u % NT <= 4 and u // NT + 1 < H:
                        qk_turn(u // NT + 1, u % NT - 1)

                pe.wait_ge(s_o, l + 1)
                for t in range(NT):
                    o = begin(t % 8)
                    for k in range(4):
                        mm = pe.transpose(o[:, k * P:(k + 1) * P], o_tok[:, t, k * P:(k + 1) * P], ident[:, :])
                    mm.then_inc(full[t % 8], 1)
                def follows(c):
                    return 0 < c <= 8 or c % 2 == 1

                def unit(c, n, o, last_used=None):
                    ns = slice(n * 512, (n + 1) * 512)
                    if n == 0:
                        pe.wait_ge(s_wlo, l * N_SPLIT + c + 1)
                    for k in range(KD):
                        if c == n == 0:
                            if k < H_ACT:
                                pe.wait_ge(s_hin[0], l * H_ACT + k + 1)
                            else:
                                pe.wait_ge(s_hin[1], l * (KD - H_ACT) + k - H_ACT + 1)
                        mm = pe.matmul(o, wHi[c % 2][:, k, :], hHi[:, k, ns], start=(k == 0), stop=False)
                        if k == n == 0 and follows(c):
                            mm.then_inc(s_wdone, 1)
                        mm = pe.matmul(o, wHi[c % 2][:, k, :], hLo[:, k, ns], start=False, stop=False)
                        if k == n == 0 and last_used is not None:
                            mm.then_inc(w_used[last_used], 1)
                        mm = pe.matmul(o, wLo[c % 2][:, k, :], hHi[:, k, ns], start=False, stop=(k == 7))
                    return mm

                for c in range(8):
                    for n in range(2):
                        b = (2 * c + n) % 8
                        o = begin(b)
                        unit(c, n, o, 0 if c == 4 else None).then_inc(full[b], 1)
                for m in range(KD):
                    g = weights(l, 6 + m)[:, 0:24 * P].rearrange("p (k c) -> p k c", c=P)
                    for br in range(2):
                        for n in range(2):
                            b = 4 * n + br
                            o = begin(b)
                            unit(8 + 2 * m + br, n, o, (5 + m) % W_SLOTS if br == 0 else None).then_inc(full[b], 1)
                    if m == 0:
                        pe.wait_ge(s_sm, l * 16 + 16)
                    for br in range(2, 4):
                        for n in range(2):
                            b = 4 * n + br
                            o = begin(b)
                            k0, rhs = [(16, oT), (20, fT)][br - 2]
                            for k in range(4):
                                mm = pe.matmul(o, g[:, k0 + k, :], rhs[:, k, n * 512:(n + 1) * 512],
                                               start=(k == 0), stop=(k == 3))
                                if (br, n, k) == (2, 0, 0):
                                    mm.then_inc(s_wdone, 1)
                            mm.then_inc(full[b], 1)
                for n in range(2):
                    wo = k_of(weights(l, 14 + n))
                    for t in range(NT):
                        b = t % 8
                        o = begin(b)
                        if n == 0 and t == 0:
                            pe.wait_ge(s_mT, l * 16 + 16)
                        for k in range(KD):
                            mm = pe.matmul(o, mT[:, k, t * P:(t + 1) * P], wo[:, k, :], start=(k == 0), stop=(k == 7))
                            if t == k == 0:
                                mm.then_inc(w_used[(13 + n) % W_SLOTS], 1)
                        mm.then_inc(full[b], 1)
                pe.wait_ge(free[7], bk.count(7))
                pe.nop().then_inc(w_used[1], 1)
            bk.leave(L)

            def weights2(i):
                sl = i % W_SLOTS
                pe.wait_ge(w_in_slot[sl], 16 * (L * W_DMAS[sl] + i // W_SLOTS + (3 if sl == 0 else 1)))
                return W[:, sl, :]

            pe.wait_ge(s_xnew, L + 1)
            for t in range(NT):
                for j in range(2):
                    b = (2 * t + j) % 8
                    o = begin(b)
                    for k in range(4):
                        f = 4 * j + k
                        mm = pe.transpose(o[:, k * P:(k + 1) * P], x1[:, t, f * P:(f + 1) * P], ident[:, :])
                    mm.then_inc(full[b], 1)
            x_done = [bk.count(b) for b in range(8)]
            pe.wait_ge(s2_rows, 16 * 7)
            pe.wait_ge(s2_ld, 1)
            o = begin(0)
            for i in range(3):
                pe.transpose(o[:, i * NPAIR:(i + 1) * NPAIR], prow[0:NPAIR, i, :], ident[0:NPAIR, 0:NPAIR])
            pe.transpose(o[0:CH, 64:64 + NG], drow, ident[0:NG, 0:NG])
            pe.transpose(o[:, P:P + KD], rows[0:KD, :], ident[0:KD, 0:KD]).then_inc(full[0], 1)
            wi = weights2(0)[:, 0:KD * NIDX].rearrange("p (k c) -> p k c", k=KD)
            for b in range(8):
                pe.wait_ge(free[b], x_done[b])
            for i in range(6):
                m, n = i // 2, i % 2
                if i == 4:
                    pe.wait_ge(s2_ki, 1)
                o = begin(i)
                for k in range(KD):
                    if m < 2:
                        w = wi[:, k, KVC + IH + m * P:KVC + IH + (m + 1) * P]
                    else:
                        w = ki4[:, k, :]
                    mm = pe.matmul(o, w, xT[:, k, n * 512:(n + 1) * 512], start=(k == 0), stop=(k == 7))
                mm.then_inc(full[i], 1)
            for t in range(NT):
                b = (6 + t) % 8
                o = begin(b)
                for k in range(KD):
                    mm = pe.matmul(o[:, 0:KVC + IH], xT[:, k, t * P:(t + 1) * P], wi[:, k, 0:KVC + IH],
                                   start=(k == 0), stop=(k == 7))
                mm.then_inc(full[b], 1)
            pe.wait_ge(s2_par, 16 * S5_LOADS)
            for i in range(2):
                b = (7 + i) % 8
                o = begin(b)
                for k in range(4):
                    mm = pe.transpose(o[:, k * P:(k + 1) * P], craw[:, 4 * i + k, :], ident[:, :])
                mm.then_inc(full[b], 1)
            marks["C"] = (bk.count(7), bk.count(0))
            def gates(i, last, tiles=range(4)):
                wz = k_of(weights2(i))
                for m in tiles:
                    for n in range(2):
                        b = 2 * m + n
                        o = begin(b)
                        for k in range(KD):
                            mm = pe.matmul(o, wz[:, k, m * P:(m + 1) * P], xT[:, k, n * 512:(n + 1) * 512],
                                           start=(k == 0), stop=(k == 7))
                            if m == n == k == 0 and last is not None:
                                mm.then_inc(w_used[last], 1)
                        mm.then_inc(full[b], 1)

            m1_free = {}

            def s5_kernel(f):
                p = f % 2
                pe.wait_ge(s2_G, f + 1)
                pe.wait_ge(s2_CA, f + 1)
                for i in range(2):
                    o = begin(i)
                    for q in range(HP):
                        mm = pe.transpose(o[:, q * P:(q + 1) * P], G[p][:, i, q, :, :], ident[:, :])
                    mm.then_inc(full[i], 1)
                m1_free[f] = bk.count(1)
                for i in range(2):
                    o = begin(2 + i)
                    for k in range(HP):
                        q, r_ = k, slice(NST * i, NST * i + NST)
                        qq = f * HP + q
                        for (lo, hi, cr, ci) in ((0, CH, CT[r_, 0, qq, :], CT[r_, 1, qq, :]),
                                                 (CH, P, ca_re[p][r_, q, 0:CL - 1, :], ca_ni[p][r_, q, 0:CL - 1, :])):
                            oo = o[0:CH, k * P + lo:k * P + hi]
                            pe.matmul(oo, Bb[r_, 0, qq, :], cr, start=True, stop=False)
                            mm = pe.matmul(oo, Bb[r_, 1, qq, :], ci, start=False, stop=True)
                    mm.then_inc(full[2 + i], 1)
                marks["kernel", f] = bk.count(3)

            def s5_states(f):
                p = f % 2
                pe.wait_ge(free[1], m1_free[f])
                for i in range(2):
                    o = begin(4 + i)
                    for q in range(HP):
                        for hh in range(2):
                            mm = pe.matmul(o[hh * NST:(hh + 1) * NST, q * NC:(q + 1) * NC],
                                           M1[p][:, i, q, hh * NST:(hh + 1) * NST], UT[:, 2 * (f * HP + q) + hh, :],
                                           start=True, stop=True)
                    mm.then_inc(full[4 + i], 1)
                marks["states", f] = bk.count(5)

            def s5_outputs(f):
                p = f % 2
                pe.wait_ge(s2_TT[f % 2], 16 * CL * (f // 2 + 1))
                pe.wait_ge(s2_X, f + 1)
                for i in range(2):
                    o = begin(6 + i)
                    for k in range(HP):
                        g = 2 * k + i
                        q, r_ = k, slice(NST * i, NST * i + NST)
                        og = o[:, k * P:(k + 1) * P]
                        pe.matmul(og, UT[:, 2 * HP * f + g, :], TT[p][:, g, :], start=True, stop=False)
                        pe.matmul(og, X[p][r_, 0, q, :], ca_re[p][r_, q, :, :], start=False, stop=False)
                        mm = pe.matmul(og, X[p][r_, 1, q, :], ca_ni[p][r_, q, :, :], start=False, stop=True)
                    mm.then_inc(full[6 + i], 1)
                marks["y", f] = bk.count(7)

            for b in range(8):
                pe.wait_ge(free[b], bk.count(b))
            for v in range((NT - 2) * IH):
                t, h = 2 + v // IH, v % IH
                b = 2 * (v % 4)
                begin(b)
                w = (t + 1) * P
                for n in range((w + 511) // 512):
                    mm = pe.matmul(PS[:, b + n, 0:min(512, w - 512 * n)],
                                   qiT[:, h // 4, t * P:(t + 1) * P],
                                   kiz[:, h % 4, n * 512:min(w, n * 512 + 512)], start=True, stop=True)
                    if n == 0 and w > 512 and v == 2 * IH:
                        mm.then_inc(w_used[0], 1)
                mm.then_inc(full[b], 1)
            for b in range(0, 8, 2):
                pe.wait_ge(free[b], bk.count(b))
            s5_kernel(0)
            s5_kernel(1)
            for j in range(2):
                o = begin(j)
                for k in range(4):
                    t = 4 * j + k
                    pe.wait_ge(s2_c, t + 1)
                    mm = pe.transpose(o[:, k * P:(k + 1) * P], c2[:, t, :], ident[:, :])
                mm.then_inc(full[j], 1)
            wu = k_of(weights2(1))
            for j in range(CL):
                o = begin(j)
                for k in range(KD):
                    mm = pe.matmul(o, xT[:, k, j:S:CL], wu[:, k, :], start=(k == 0), stop=(k == 7))
                mm.then_inc(full[j], 1)
            for b in range(8):
                pe.wait_ge(free[b], bk.count(b))
            for b in range(8):
                o = begin(b)
                for k in range(4):
                    g = 4 * b + k
                    mm = pe.transpose(o[:, k * P:(k + 1) * P], r0[:, g * P:(g + 1) * P], ident[:, :])
                    if b == k == 0:
                        mm.then_inc(w_used[1], 1)
                mm.then_inc(full[b], 1)

            s5_states(0)
            s5_states(1)
            gates(2, None)
            s5_outputs(0)
            s5_outputs(1)
            gates(3, 0, (0, 1))
            s5_kernel(2)
            s5_kernel(3)
            gates(3, None, (2, 3))
            s5_states(2)
            s5_states(3)
            s5_outputs(2)
            s5_outputs(3)
            for b in (6, 7):
                pe.wait_ge(free[b], bk.count(b))
            for i in range(CL):
                o = begin(i)
                for k in range(4):
                    mm = pe.transpose(o[:, k * P:(k + 1) * P], Y[:, i, k * P:(k + 1) * P], ident[:, :])
                    if i == k == 0:
                        mm.then_inc(w_used[1], 1)
                mm.then_inc(full[i], 1)
            wg = weights2(4)[:, 0:4096].rearrange("p (k c) -> p k c", k=4)
            pe.wait_ge(free[7], bk.count(7))
            for m in range(4):
                for n in range(2):
                    for br in range(2):
                        b = (4 * m + 2 * n + br) % 8
                        o = begin(b)
                        for k in range(4):
                            mm = pe.matmul(o, wg[:, k, (4 * br + m) * P:(4 * br + m + 1) * P],
                                           yT[:, k, n * 512:(n + 1) * 512], start=(k == 0), stop=(k == 3))
                        mm.then_inc(full[b], 1)
                    marks["glu", 2 * m + n] = (b, bk.count(b))
            gates(5, 0)
            qT_free = [bk.count(b) for b in range(8)]
            pe.wait_ge(s2_wk, 16)
            o = begin(0)
            for m in range(4):
                mm = pe.transpose(o[:, m * P:(m + 1) * P], wuk[:, m * P:(m + 1) * P], ident[:, :])
                if m == 0:
                    mm.then_inc(w_used[1], 1)
            mm.then_inc(full[0], 1)
            for b in range(8):
                pe.wait_ge(free[b], qT_free[b] + (b == 0))
            for h in range(H):
                for n in range(2):
                    b = (1 + 2 * h + n) % 8
                    o = begin(b)
                    r_ = slice(VD * (h % 2), VD * (h % 2) + VD)
                    pe.matmul(o, wukT[r_, h // 2, :], qT2[r_, h // 2, n * 512:(n + 1) * 512],
                              start=True, stop=True).then_inc(full[b], 1)
            marks["qlat"] = bk.count(0)
            marks["attention"] = list(bk.n)
            for b in range(8):
                pe.wait_ge(free[b], bk.count(b))
            pe.wait_ge(s2_wv, 16)

            def scores2(u):
                t, h = u // H, u % H
                b = 2 * (u % 2)
                begin(b)
                w = (t + 1) * P
                for n in range((w + 511) // 512):
                    mm = pe.matmul(PS[:, b + n, 0:min(512, w - 512 * n)], qlT[:, h, t * P:(t + 1) * P],
                                   c2T[:, n * 512:min(w, n * 512 + 512)], start=True, stop=True)
                mm.then_inc(full[b], 1)

            def p_turn2(u):
                t = u // H
                pe.wait_ge(free[2 * (u % 2)], bk.count(2 * (u % 2)))
                for j in range(2):
                    if 4 * j > t:
                        continue
                    o = begin(4 + j)
                    for c in range(4 * j, min(4 * j + 4, t + 1)):
                        mm = pe.transpose(o[:, (c % 4) * P:(c % 4 + 1) * P], Pb2[u % 2][:, c * P:(c + 1) * P], ident[:, :])
                    mm.then_inc(full[4 + j], 1)
                pt2[u] = (bk.count(4), bk.count(5))

            def latent_out(t, hg):
                u = H * t + 4 * hg + 3
                pe.wait_ge(free[4], pt2[u][0])
                pe.wait_ge(free[5], pt2[u][1])
                o = begin(6)
                for k in range(t + 1):
                    mm = pe.matmul(o, c2[:, k, :], PT2[hg][:, k, :], start=(k == 0), stop=(k == t))
                mm.then_inc(full[6], 1)
                ol_free[hg] = bk.count(6)

            def att_out(t):
                o = begin(7)
                pe.wait_ge(free[6], ol_free[1])
                for h in range(H):
                    mm = pe.matmul(o[:, h * VD:(h + 1) * VD], olT[h // 4][:, (h % 4) * P:(h % 4 + 1) * P], wuv[:, h, :],
                                   start=True, stop=True)
                mm.then_inc(full[7], 1)

            def att_turn(t):
                pe.wait_ge(free[7], bk.count(7))
                o = begin(6)
                for k in range(4):
                    mm = pe.transpose(o[:, k * P:(k + 1) * P], att[t % 2][:, k * P:(k + 1) * P], ident[:, :])
                mm.then_inc(full[6], 1)
                turn_free[0] = bk.count(6)

            def out_half(t, n, half):
                if (n, half) == (1, 0):
                    pe.wait_ge(free[6], turn_free[0])
                    if t == 0:
                        pe.wait_ge(s2_glu, 8)
                wo = k_of(weights2(6 + n)) if t == half == 0 else k_of(W[:, n, :])
                o = begin(6 + n) if half == 0 else PS[:, 6 + n, :]
                for k in range(4 * half, 4 * half + 4):
                    mm = pe.matmul(o, mix[:, k, t * P:(t + 1) * P], wo[:, k, :], start=(k == 0), stop=(k == 7))
                if half == 1:
                    mm.then_inc(full[6 + n], 1)

            pt2, ol_free, turn_free = {}, {}, {}
            scores2(0)
            for u in range(H * NT):
                t, h = u // H, u % H
                if u + 1 < H * NT:
                    scores2(u + 1)
                if h == 5:
                    latent_out(t, 0)
                if t >= 1:
                    if h == 1:
                        latent_out(t - 1, 1)
                    if h == 2:
                        att_out(t - 1)
                    if h == 3:
                        att_turn(t - 1)
                    if h >= 4:
                        out_half(t - 1, 1 - (h - 4) // 2, h % 2)
                p_turn2(u)
            latent_out(NT - 1, 1)
            att_out(NT - 1)
            att_turn(NT - 1)
            for i in range(4):
                out_half(NT - 1, 1 - i // 2, i % 2)

        @block.sync
        def _(sp):
            sp.dma_start(x1[:, :, :], a["x"][0].rearrange("(t p) d -> p t d", p=P)).then_inc(s_xin, 16)
            sp.dma_start(ident[:, :], a["c_ident"]).then_inc(s_const, 16)
            sp.dma_start(dft_d[:, :], a["c_dft_d"]).then_inc(s_const, 16)
            sp.dma_start(cosT[:, :, :], a["c_cos"].rearrange("(t p) c -> p t c", p=P)).then_inc(s_const, 16)
            sp.dma_start(sinT[:, :, :], a["c_sin"].rearrange("(t p) c -> p t c", p=P)).then_inc(s_const, 16)
            sp.wait_ge(s_xin, 16)

            def chunk(l, i):
                n, name = CHUNKS[i]
                if n == 0:
                    return
                s = i % W_SLOTS
                takes = 1 + l * W_TAKES[s] + sum(c[0] > 0 for c in CHUNKS[s:i:W_SLOTS])
                sp.wait_ge(w_used[s], takes)
                slot = W[:, s, 0:4096]
                k512 = slot.rearrange("p (k c) -> p k c", k=8)

                def load(dst, src):
                    sp.dma_start(dst, src).then_inc(w_in_slot[s], 16)

                def win(c0, w=512):
                    return a["w_in"][l, :, c0:c0 + w].rearrange("(k p) c -> p k c", p=P)

                if name == "c":
                    c = W[:, s, :].rearrange("p (k c) -> p k c", k=8)
                    load(c[:, :, 0:QL], win(0, QL))
                    load(c[:, :, QL:QL + ROPE], win(C_PE, ROPE))
                    load(c[:, :, QL + ROPE:C_COLS], win(QL, KVL))
                elif name == "u":
                    load(k512, win(C_U))
                elif name == "up":
                    load(slot[:, 0:2 * H * QK].rearrange("p (k c) -> p k c", k=2),
                         a["w_uq"][l].rearrange("(k p) c -> p k c", p=P))
                    load(slot[:, 2 * H * QK:2 * H * QK + 2048].rearrange("p (k c) -> p k c", k=2),
                         a["w_ukv"][l].rearrange("(k p) c -> p k c", p=P))
                elif name == "dft":
                    load(W[:, s, 0:KD * HF].rearrange("p (k c) -> p k c", k=8),
                         a["c_dft_s"].rearrange("(k p) c -> p k c", p=P))
                elif name == "za":
                    load(k512, win(C_ZA))
                elif name == "zf":
                    load(k512, win(C_ZF))
                elif name[:4] == "gate":
                    m = int(name[4:]) * P
                    g = slot[:, 0:24 * P].rearrange("p (k c) -> p k c", c=P)
                    load(g[:, 0:8, :], win(C_GA + m, P))
                    load(g[:, 8:16, :], win(C_GF + m, P))
                    load(g[:, 16:20, :], a["w_attn_proj"][l, :, m:m + P].rearrange("(k p) c -> p k c", p=P))
                    load(g[:, 20:24, :], a["w_fourier_proj"][l, :, m:m + P].rearrange("(k p) c -> p k c", p=P))
                else:
                    n0 = 512 * int(name[3])
                    load(k512, a["w_out"][l, :, n0:n0 + 512].rearrange("(k p) c -> p k c", p=P))

            sp.wait_ge(s_init, 3)
            with sp.Fori(0, L) as l:
                sp.wait_ge(s_xnew, l + 1)
                for dst, name, n in [(0, "norm_g", KD), (KD, "q_latent_g", 2), (KD + 2, "kv_latent_g", 2)]:
                    sp.dma_start(rows[dst:dst + n, :], a[name][l].rearrange("(k p) -> k p", p=P)).then_inc(s_par, 16)
                sp.dma_start(rows[KD + 4:N_ROWS, :],
                             a["b_merge"][l].rearrange("b (k p) -> (b k) p", p=P)).then_inc(s_par, 16)
                sp.dma_start(gq[:, :], a["q_head_g"][l].partition_broadcast(P)).then_inc(s_par, 16)
                sp.dma_start(gk[:, :], a["k_head_g"][l].partition_broadcast(P)).then_inc(s_par, 16)
                chunk(l, 0)
                chunk(l, 1)
                sp.dma_start(xres.rearrange("(t p) d -> p t d", p=P), x1[:, :, :]).then_inc(s_xsave, 16)
                for i in range(2, 5):
                    chunk(l, i)
                sp.wait_ge(s_o, l + 1)
                chunk(l, 5)
                for i in range(6, len(CHUNKS)):
                    chunk(l, i)
                sp.wait_ge(s_xsave, l * 16 + 16)
                sp.dma_start(x1[:, :, :], xres.rearrange("(t p) d -> p t d", p=P)).then_inc(s_xback, 16)
            sp.wait_ge(s_xnew, L + 1)
            def small(dst, src, q):
                sp.dma_start(dst, src).then_inc(q, 16)

            def load2(i, srcs):
                sl = i % W_SLOTS
                sp.wait_ge(w_used[sl], 1 + L * W_TAKES[sl] + i // W_SLOTS)
                for dst, src in srcs(W[:, sl, 0:4096]):
                    sp.dma_start(dst, src).then_inc(w_in_slot[sl], 16)

            def cols(c0, w):
                return lambda slot: [(slot[:, 0:KD * w].rearrange("p (k c) -> p k c", k=KD),
                                      a["w_in_2"][0, :, c0:c0 + w].rearrange("(k p) c -> p k c", p=P))]

            small(rows[0:KD, :], a["b_glu_2"][0].rearrange("(k p) -> k p", p=P), s2_rows)
            for i, n in enumerate(["a_re_2", "a_im_2"]):
                small(prow[0:NPAIR, 1 + i, :], a[n][0].rearrange("(q h) p -> q (h p)", h=2), s2_rows)
            small(lrow, a["log_dt_2"][0].rearrange("(q h) -> q h", h=2), s2_rows)
            small(drow, a["d_skip_2"][0], s2_rows)
            small(tri, a["c_tri"], s2_rows)
            small(kvg, a["kv_norm_g_2"][0].partition_broadcast(P), s2_rows)
            def idx_cols(slot):
                dst = slot[:, 0:KD * NIDX].rearrange("p (k c) -> p k c", k=KD)
                parts, at_ = [], 0
                for c0, w in ((0, KVC), (KVC + IH * ID + ID, IH), (KVC, IH * ID + ID)):
                    parts.append((dst[:, :, at_:at_ + w], a["w_in_2"][0, :, C2_C + c0:C2_C + c0 + w]
                                  .rearrange("(k p) c -> p k c", p=P)))
                    at_ += w
                return parts

            load2(0, idx_cols)
            for i, n in enumerate(["c_re_2", "c_im_2"]):
                for hh in range(2):
                    small(craw[:, 4 * i:4 * i + 4, hh * NST:(hh + 1) * NST],
                          a[n][0].rearrange("g c p -> (g c) p").rearrange("(k r) p -> r k p", r=P), s2_par)
            for i, n in enumerate(["b_re_2", "b_im_2"]):
                small(Braw[:, i], a[n][0].rearrange("(q h) p c -> (h p) q c", h=2), s2_par)
            load2(1, cols(C2_U, SW))
            small(xres.rearrange("(t p) d -> p t d", p=P), x1[:, :, :], s_xsave)
            load2(2, cols(C2_GA, AW))
            for f in range(4):
                if f == 2:
                    load2(3, cols(C2_GS, SW))
                if f >= 2:
                    sp.wait_ge(full[7], marks["y", f - 2])
                sp.wait_ge(s2_K, f + 1)
                for j in range(CL):
                    sp.dma_start(TT[f % 2][j * CH:(j + 1) * CH, :, j * CH:P], K16[f % 2][:, :, 0:(CL - j) * CH]
                                 ).then_inc(s2_TT[f % 2], 16)
            load2(4, lambda slot: [(slot.rearrange("p (k c) -> p k c", k=4),
                                    a["w_glu_2"][0].rearrange("(k p) c -> p k c", p=P))])
            load2(5, cols(0, AW))
            sp.wait_ge(full[7], marks["y", 3])
            small(wuk.rearrange("p (h d) -> p h d", h=H), a["w_uk_2"][0].rearrange("h c d -> c h d"), s2_wk)
            small(wuv, a["w_uv_2"][0].rearrange("h c d -> c h d"), s2_wv)
            for n in range(2):
                load2(6 + n, lambda slot, n=n: [(slot.rearrange("p (k c) -> p k c", k=KD),
                      a["w_out_2"][0, :, n * 512:(n + 1) * 512].rearrange("(k p) c -> p k c", p=P))])
            sp.wait_ge(full[0], marks["qlat"])
            small(lng, a["ln_g_2"][0].partition_broadcast(P), s2_ln)
            small(lnb, a["ln_b_2"][0].partition_broadcast(P), s2_ln)
            sp.wait_ge(s_xsave, 16 * (L + 1))
            for t in range(NT):
                if t >= 2:
                    sp.wait_ge(s2_od[t % 2], 16 * (t // 2))
                small(xt[t % 2], xres[t * P:(t + 1) * P, :], s2_xt[t % 2])
                if t >= 1:
                    sp.wait_ge(s2_o, t)
                    small(out[0, (t - 1) * P:t * P, :], xt[(t - 1) % 2], s2_od[(t - 1) % 2])
            sp.wait_ge(s2_o, NT)
            small(out[0, (NT - 1) * P:, :], xt[(NT - 1) % 2], s2_od[(NT - 1) % 2])
            for i in range(2):
                sp.wait_ge(s2_od[i], 16 * (NT // 2))

        @block.scalar
        def _(act):
            bk = Banks(full, free)
            st = Steps(act, s_act)
            PER = NT + 2 * NT
            act.wait_ge(s_init, 3)
            act.wait_ge(s_xin, 16)

            def arrive(b):
                act.wait_ge(full[b], bk.take(b) + 1)
                return PS[:, b, :]

            with act.Fori(0, L) as l:
                bk.enter(l)
                st.enter(l, PER)
                act.wait_ge(s_xnew, l + 1)
                for t in range(NT):
                    st.link(act.activation(xn[t], x1[:, t, :], ACT.Square, accum_out=ssx[:, t:t + 1]))
                    act.activation(ssx[:, t:t + 1], ssx[:, t:t + 1], ACT.Sqrt, bias=eps[:, :], scale=1.0 / D
                                   ).then_inc(s_std, 1)
                bk.skip(ROUND[0])
                for t in range(NT):
                    b = (2 * t) % 8
                    for j in range(2):
                        o = arrive(b + j)
                        st.done(act.activation(cT[:, j, 0:256], o[:, 0:256], ACT.Square,
                                               accum_out=ssc[:, 2 * t + j:2 * t + j + 1]))
                        act.activation(c_tok[:, t, j * 256:(j + 1) * 256], o[:, 0:256], ACT.Copy)
                        if j == 0:
                            act.activation(kpe[:, t, :], o[:, QL:QL + ROPE], ACT.Copy).then_inc(free[b], 1)
                    st.wait()
                    act.activation(ssc[:, 2 * t:2 * t + 2], ssc[:, 2 * t:2 * t + 2], ACT.Sqrt, bias=eps[:, :],
                                   scale=1.0 / QL).then_inc(free[b + 1], 1)
                for b in range(8):
                    o = arrive(b)
                    act.activation(uT[:, b // 2, (b % 2) * 512:(b % 2 + 1) * 512], o, ACT.Copy).then_inc(free[b], 1)
                bk.skip(ROUND[3])
                for t in range(NT):
                    for j in range(4):
                        i = 4 * t + j
                        b = i % 8
                        o = arrive(b)
                        n_before = l * 4 * NT + i - 1
                        if i >= 2:
                            act.wait_ge(s_ss, n_before)
                        if j < 2:
                            act.activation(q_tok[:, t, j * 4 * QK:(j + 1) * 4 * QK], o[:, 0:4 * QK], ACT.Copy)
                            act.activation(tmp[:, i % 2, 0:4 * QK], o[:, 0:4 * QK], ACT.Square).then_inc(free[b], 1)
                        else:
                            act.activation(tmp[:, i % 2, 0:4 * NOPE].rearrange("p (h c) -> p h c", h=4),
                                           o.rearrange("p (h c) -> p h c", h=4)[:, :, 0:NOPE], ACT.Square
                                           ).then_inc(s_sq, 1)
                for j in range(NT):
                    o = arrive(j)
                    act.activation(V[:, j, :], o, ACT.Copy).then_inc(free[j], 1)
                act.wait_ge(s_ssall, l + 1)
                act.activation(rsh[:, :, :, :], ssh[:, :, :, :], ACT.Sqrt, bias=eps[:, :], scale=1.0 / QK
                               ).then_inc(s_hstd, 1)
                o = arrive(0)
                act.activation(v_mid, o[0:1, :], ACT.Copy).then_inc(free[0], 1)
                for g in range(FG):
                    bk.take(g)
                    o = arrive(4 + g)
                    act.activation(odd[:, g, :], o, ACT.Copy).then_inc(free[4 + g], 1)
                o = arrive(0)
                act.activation(fT[:, :, S // 2:HF], o[:, 0:FG].unsqueeze(2), ACT.Copy).then_inc(free[0], 1)

                def qk_copy(h, i):
                    o = arrive(7)
                    dst = qkT[h % 2][i // 2]
                    act.activation(dst[0:QK, (i % 2) * 512:(i % 2 + 1) * 512], o[0:QK, :], ACT.Copy
                                   ).then_inc(s_qkT, 1)

                def round_h(k):
                    act.activation(hTmp[k], hT[:, k, :], ACT.Copy).then_inc(s_hhi, 1)

                def in_place(k):
                    act.wait_ge(s_hlo, l * KD + k + 1)
                    act.activation(hHi[:, k, :], hT[:, k, :], ACT.Copy).then_inc(s_hin[0], 1)

                for i in range(4):
                    qk_copy(0, i)
                for u in range(UNITS + 1):
                    if u < UNITS:
                        b = 2 * (u % 2)
                        bk.take(b)
                        act.wait_ge(s_nm, l * UNITS + u + 1)
                        act.activation(Pb[u % 2], PS[:, b:b + 2, :].rearrange("p a c -> p (a c)"), ACT.Exp,
                                       bias=negm[:, u:u + 1], accum_out=rsum[:, u:u + 1]).then_inc(free[b], 1)
                    if u >= 1:
                        o = arrive(5)
                        bk.take(4)
                        act.activation(PT[(u - 1) % 2][:, 512:1024], o, ACT.Copy).then_inc(free[5], 1)
                    if 2 <= u % NT <= 5 and u // NT + 1 < H:
                        qk_copy(u // NT + 1, u % NT - 2)
                    if u // NT + 1 == H:
                        if 2 <= u % NT <= 5:
                            in_place(u % NT - 2)
                        if 1 <= u % NT <= 4:
                            round_h(u % NT - 1)
                for h in range(H):
                    bk.take(6)
                def turned_out(t):
                    o = arrive(t)
                    act.activation(oT[:, :, t * P:(t + 1) * P], o.rearrange("p (k c) -> p k c", k=4), ACT.Copy
                                   ).then_inc(free[t], 1)

                act.wait_ge(s_o, l + 1)
                for k in range(4, KD):
                    round_h(k)
                for t in range(NT):
                    if 4 + t < H_ACT:
                        in_place(4 + t)
                    turned_out(t)

                def round_weights(c):
                    w = unit_weights(act, l, c)
                    if c >= 2:
                        act.wait_ge(s_wdone, l * N_SPLIT + c - 1)
                    act.activation(wHi[c % 2], w, ACT.Copy).then_inc(s_whi, 1)

                round_weights(0)
                round_weights(1)
                for i in range(16):
                    b = i % 8
                    o = arrive(b)
                    if i >= 2:
                        act.wait_ge(s_sm, l * 16 + i - 1)
                    act.activation(tmp[:, i % 2, :], o, ACT.Silu).then_inc(free[b], 1)
                    if i % 2 == 1:
                        round_weights(i // 2 + 2)
                for m in range(KD):
                    for n in range(2):
                        i = 2 * m + n
                        if i >= 2:
                            act.wait_ge(s_mT, l * 16 + i - 1)
                        for br in range(2):
                            o = arrive(4 * n + br)
                            act.activation(sg[:, 2 * (i % 2) + br, :], o, ACT.Sigmoid,
                                           bias=pT[:, KD + 4 + br * KD + m:KD + 5 + br * KD + m]
                                           ).then_inc(free[4 * n + br], 1)
                        bk.take(4 * n + 2)
                        bk.take(4 * n + 3)
                    if m + 1 < KD:
                        round_weights(8 + 2 * m + 2)
                        round_weights(8 + 2 * m + 3)
                bk.skip(ROUND[11])
            bk.leave(L)
            st.leave(L)

            def flat_bank(b, lo, hi):
                return PS[:, b:b + 2, :].rearrange("p a c -> p (a c)")[:, lo:hi]

            for t in range(NT):
                b = (2 * t) % 8
                o = arrive(b)
                act.activation(xT[:, 0:4, t * P:(t + 1) * P], o.rearrange("p (k c) -> p k c", k=4), ACT.Copy
                               ).then_inc(free[b], 1)
                bk.take(b + 1)
            bk.take(0)
            for i in range(6):
                o = arrive(i)
                m, n = i // 2, i % 2
                if m < 2:
                    act.activation(qiT[:, m, n * 512:(n + 1) * 512], o, ACT.Copy).then_inc(free[i], 1)
                    continue
                act.wait_ge(s2_kz, 1)
                for j in range(4):
                    r_ = slice(ID * j, ID * (j + 1))
                    cp = act.activation(kiz[r_, j, n * 512:(n + 1) * 512], o[r_, :], ACT.Copy)
                cp.then_inc(free[i], 1)
            for t in range(NT):
                b = (6 + t) % 8
                o = arrive(b)
                act.activation(c2[:, t, :], o[:, 0:KVC], ACT.Copy)
                act.activation(wtok[:, t, :], o[:, KVC:KVC + IH], ACT.Copy)
                st.link(act.activation(cosT[:, :, :].rearrange("p a b -> p (a b)"), o[:, 0:KVC], ACT.Square, accum_out=ssx[:, t:t + 1]))
                act.activation(ssx[:, t:t + 1], ssx[:, t:t + 1], ACT.Sqrt, bias=eps[:, :], scale=1.0 / KVC
                               ).then_inc(free[b], 1)
            for i, b in enumerate((7, 0)):
                o = arrive(b).rearrange("p (q h c) -> p q h c", q=NPAIR, h=2)
                act.activation(CT[0:NST, i], o[0:NST, :, 0, :], ACT.Copy, scale=1.0 - 2 * i)
                act.activation(CT[NST:P, i], o[NST:P, :, 1, :], ACT.Copy, scale=1.0 - 2 * i).then_inc(free[b], 1)
            for v in range((NT - 2) * IH):
                b = 2 * (v % 4)
                arrive(b)
                w = (3 + v // IH) * P
                if v >= 2:
                    act.wait_ge(s2_acc, v - 1)
                act.activation(rl[v % 2][:, 0:w], flat_bank(b, 0, w), ACT.Relu).then_inc(free[b], 1)
            def silu_gates(k0, banks=range(8)):
                for b in banks:
                    o = arrive(b)
                    act.activation(mix[:, k0 + b // 2, (b % 2) * 512:(b % 2 + 1) * 512], o, ACT.Silu
                                   ).then_inc(free[b], 1)

            def s5_kernel(f):
                p = f % 2
                for i in range(2):
                    o = arrive(i)
                    act.activation(M1[p][:, i], o.rearrange("p (q c) -> p q c", q=HP), ACT.Copy).then_inc(free[i], 1)
                for i in range(2):
                    o = arrive(2 + i)
                    act.activation(K16[p][:, i:2 * HP:2, :], o[0:CH, :].rearrange("p (g c) -> p g c", g=HP), ACT.Copy
                                   ).then_inc(free[2 + i], 1)

            def s5_states(f):
                p = f % 2
                act.wait_ge(s2_R, f + 1)
                for i in range(2):
                    o = arrive(4 + i)
                    act.activation(st_[p][:, i], o.rearrange("p (q c) -> p q c", q=HP), ACT.Copy
                                   ).then_inc(free[4 + i], 1)

            def s5_outputs(f):
                for i in range(2):
                    o = arrive(6 + i)
                    g0 = 2 * HP * f
                    y = Y[:, :, g0 * CH:(g0 + 2 * HP) * CH].rearrange("p i (q h c) -> p h q i c", q=HP, h=2)
                    act.activation(y[:, i], o.rearrange("p (q i c) -> p q i c", q=HP, i=CL), ACT.Gelu_apprx_tanh
                                   ).then_inc(free[6 + i], 1)

            s5_kernel(0)
            s5_kernel(1)
            for j in range(2):
                o = arrive(j)
                act.activation(c2T[:, j * 512:(j + 1) * 512], o, ACT.Copy).then_inc(free[j], 1)
            for j in range(CL):
                o = arrive(j)
                act.activation(U4[:, :, j, :], o.rearrange("p (g c) -> p g c", g=NG), ACT.Copy).then_inc(free[j], 1)
            for b in range(8):
                o = arrive(b)
                act.activation(UT[:, 4 * b:4 * b + 4, :], o.rearrange("p (g c) -> p g c", g=4), ACT.Copy
                               ).then_inc(free[b], 1)

            s5_states(0)
            s5_states(1)
            act.wait_ge(s_xsave, 16 * (L + 1))
            silu_gates(0)
            s5_outputs(0)
            s5_outputs(1)
            silu_gates(4, range(0, 4))
            s5_kernel(2)
            s5_kernel(3)
            silu_gates(4, range(4, 8))
            s5_states(2)
            s5_states(3)
            s5_outputs(2)
            s5_outputs(3)
            for i in range(CL):
                o = arrive(i)
                act.activation(yT[:, :, i:S:CL], o.rearrange("p (k c) -> p k c", k=4), ACT.Copy).then_inc(free[i], 1)
            for m in range(4):
                for n in range(2):
                    i = 2 * m + n
                    if i >= 2:
                        act.wait_ge(s2_glu, i - 1)
                    b = (4 * m + 2 * n) % 8
                    o = arrive(b)
                    act.activation(vb[i % 2], o, ACT.Identity, bias=pT[:, m:m + 1]).then_inc(free[b], 1)
                    o = arrive(b + 1)
                    act.activation(gb[i % 2], o, ACT.Sigmoid, bias=pT[:, 4 + m:5 + m]).then_inc(free[b + 1], 1)
            for b in range(8):
                o = arrive(b)
                act.activation(qT2[:, b // 2, (b % 2) * 512:(b % 2 + 1) * 512], o, ACT.Copy).then_inc(free[b], 1)
            o = arrive(0)
            act.activation(wukT[:, :, :], o.rearrange("p (m c) -> p m c", m=4), ACT.Copy).then_inc(free[0], 1)
            for h in range(H):
                for n in range(2):
                    b = (1 + 2 * h + n) % 8
                    o = arrive(b)
                    act.activation(qlT[:, h, n * 512:(n + 1) * 512], o, ACT.Copy, scale=64.0 ** -0.5
                                   ).then_inc(free[b], 1)

            def latent_copy(hg):
                o = arrive(6)
                act.activation(olT[hg], o, ACT.Copy).then_inc(free[6], 1)

            def ln_std(t):
                act.wait_ge(s2_r, t + 1)
                st.link(act.activation(r2b[:, 3072:4096], xt[t % 2], ACT.Square, accum_out=rsx[:, t:t + 1]))
                act.activation(rsx[:, t:t + 1], rsx[:, t:t + 1], ACT.Sqrt, bias=epsl[:, :], scale=1.0 / D
                               ).then_inc(s2_sq, 1)

            for u in range(H * NT):
                t, h = u // H, u % H
                if u >= 1:
                    tp = (u - 1) // H
                    hp = (u - 1) % H
                    bk.take(4)
                    if tp >= 4:
                        o = arrive(5)
                        n = tp - 3
                        act.activation(PT2[hp // 4][:, 4:4 + n, (hp % 4) * P:(hp % 4 + 1) * P],
                                       o[:, 0:n * P].rearrange("p (k c) -> p k c", k=n), ACT.Copy).then_inc(free[5], 1)
                b = 2 * (u % 2)
                bk.take(b)
                act.wait_ge(s2_nm, u + 1)
                w = (t + 1) * P
                act.activation(Pb2[u % 2][:, 0:w], Pb2[u % 2][:, 0:w], ACT.Exp, scale=-1.0,
                               bias=negm[:, u:u + 1], accum_out=rsum[:, u:u + 1]).then_inc(free[b], 1)
                if h == 5:
                    latent_copy(0)
                if t >= 1 and h == 1:
                    latent_copy(1)
                if t >= 1 and h == 2:
                    bk.take(7)
                if t >= 1 and h == 3:
                    bk.take(6)
                if t >= 1 and h == 5:
                    bk.take(7)
                if t >= 1 and h == 7:
                    bk.take(6)
                if t >= 2 and h == 2:
                    ln_std(t - 2)
            bk.take(4)
            o = arrive(5)
            act.activation(PT2[1][:, 4:8, 3 * P:4 * P], o.rearrange("p (k c) -> p k c", k=4), ACT.Copy
                           ).then_inc(free[5], 1)
            latent_copy(1)
            ln_std(NT - 2)
            ln_std(NT - 1)

        @block.vector
        def _(dve):
            bk = Banks(full, free)
            st = Steps(dve, s_dve)
            PER = 1 + NT + NT + 4 + 2 * NT + 9 + H
            for q in (*full, *free, *w_used, s_xnew):
                dve.sem_inc(q, 1)
            dve.memset(eps[:, :], EPS).then_inc(s_init, 1)
            dve.memset(rows[:, :], 0.0).then_inc(s_init, 1)
            dve.memset(u_mid[:, :, :], 0.0).then_inc(s_init, 1)
            dve.wait_ge(s_init, 3)
            dve.wait_ge(s_const, 64)
            dve.wait_ge(s_xin, 16)

            def arrive(b):
                dve.wait_ge(full[b], bk.take(b) + 1)
                return PS[:, b, :]

            with dve.Fori(0, L) as l:
                bk.enter(l)
                st.enter(l, PER)
                o = arrive(0)
                dve.tensor_copy(pT[:, :], o[:, 0:N_ROWS]).then_inc(free[0], 1)
                dve.wait_ge(free[0], bk.count(0))
                dve.wait_ge(s_par, 96 * l + 96)
                st.done(dve.tensor_scalar(gq[:, :], gq[:, :], float(QK) ** -0.5, None, ALU.mult))

                def norm(t):
                    dve.wait_ge(s_std, l * NT + t + 1)
                    st.link(dve.reciprocal(rsx[:, t:t + 1], ssx[:, t:t + 1]))
                    dve.tensor_scalar(xn[t], x1[:, t, :], rsx[:, t:t + 1], None, ALU.mult).then_inc(s_xn, 1)

                norm(0)
                for t in range(NT):
                    if t + 1 < NT:
                        norm(t + 1)
                    for j in range(2):
                        b = (1 + 2 * t + j) % 8
                        o = arrive(b)
                        dve.tensor_tensor(hT[:, 4 * j:4 * j + 4, t * P:(t + 1) * P],
                                          o.rearrange("p (k c) -> p k c", k=4),
                                          pT[:, 4 * j:4 * j + 4].unsqueeze(2).broadcast_to([P, 4, P]), ALU.mult
                                          ).then_inc(free[b], 1)
                for t in range(NT):
                    b = (2 * t) % 8
                    bk.take(b)
                    bk.take(b + 1)
                    dve.wait_ge(free[b + 1], bk.count(b + 1))
                    st.link(dve.reciprocal(ssc[:, 2 * t:2 * t + 2], ssc[:, 2 * t:2 * t + 2]))
                    c = c_tok[:, t, :].rearrange("p (j c) -> p j c", j=2)
                    dve.tensor_tensor(c, c, ssc[:, 2 * t:2 * t + 2].unsqueeze(2).broadcast_to([P, 2, 256]), ALU.mult
                                      ).then_inc(s_cn, 1)
                bk.skip(ROUND[2])
                u_free = [bk.count(b) for b in range(8)]
                for t in range(NT):
                    o = arrive(t % 8)
                    dve.tensor_tensor(cT[:, :, t * P:(t + 1) * P], o.rearrange("p (k c) -> p k c", k=4),
                                      pT[:, KD:KD + 4].unsqueeze(2).broadcast_to([P, 4, P]), ALU.mult
                                      ).then_inc(free[t % 8], 1)
                for b in range(8):
                    dve.wait_ge(free[b], u_free[b])
                h2 = S // 2
                st.done(dve.tensor_tensor(fold[:, :, 0, 1:h2], uT[:, :, 1:h2], uT[:, :, S - 1:h2:-1], ALU.add))
                st.done(dve.tensor_tensor(fold[:, :, 1, 1:h2], uT[:, :, 1:h2], uT[:, :, S - 1:h2:-1], ALU.subtract))
                st.done(dve.tensor_copy(fold[:, :, 0, 0:1], uT[:, :, 0:1]))
                st.link(dve.memset(fold[:, :, 1, 0:1], 0.0))
                dve.tensor_copy(u_mid[:, :, 0:1], uT[:, :, h2:h2 + 1]).then_inc(s_fold, 1)
                dve.wait_ge(s_xsave, 16 * l + 16)
                for t in range(NT):
                    for j in range(4):
                        i = 4 * t + j
                        b = i % 8
                        o = arrive(b)
                        qk, h0 = j // 2, 4 * (j % 2)
                        w = QK if j < 2 else NOPE
                        o4 = o.rearrange("p (h c) -> p h c", h=4)
                        if j < 2:
                            dve.wait_ge(free[b], bk.count(b))
                        else:
                            dve.wait_ge(s_sq, l * 2 * NT + 2 * t + j - 1)
                            st.done(dve.tensor_copy(k_tok[:, t, h0:h0 + 4, :], o4[:, :, 0:NOPE]))
                        dve.tensor_reduce(ssh[:, qk, t, h0:h0 + 4],
                                          tmp[:, i % 2, 0:4 * w].rearrange("p (h c) -> p h c", h=4), AX.X, ALU.add
                                          ).then_inc(s_ss, 1)
                        if j >= 2:
                            dve.tensor_copy(v_tok[:, t, h0:h0 + 4, :], o4[:, :, NOPE:]).then_inc(free[b], 1)
                st.link(dve.tensor_tensor(kro[:, :, :], kpe[:, :, :], kpe[:, :, :], ALU.mult))
                st.link(dve.tensor_reduce(ssx[:, :], kro[:, :, :], AX.X, ALU.add))
                dve.wait_ge(s_ss, l * 4 * NT + 4 * NT)
                dve.tensor_tensor(ssh[:, 1, :, :], ssh[:, 1, :, :], ssx[:, :].unsqueeze(2).broadcast_to([P, NT, H]),
                                  ALU.add).then_inc(s_ssall, 1)
                st.link(dve.tensor_tensor(kpe[:, :, :], kpe[:, :, :],
                                          gk[:, NOPE:QK].unsqueeze(1).broadcast_to([P, NT, ROPE]), ALU.mult))
                a1, a2 = kpe[:, :, 0:HR], kpe[:, :, HR:ROPE]
                st.done(dve.tensor_tensor(rt[:, 0], a1, cosT[:, :, :], ALU.mult))
                st.done(dve.tensor_tensor(rt[:, 1], a2, sinT[:, :, :], ALU.mult))
                st.done(dve.tensor_tensor(rt[:, 2], a2, cosT[:, :, :], ALU.mult))
                st.link(dve.tensor_tensor(rt[:, 3], a1, sinT[:, :, :], ALU.mult))
                st.done(dve.tensor_tensor(kro[:, :, 0:HR], rt[:, 0], rt[:, 1], ALU.subtract))
                st.link(dve.tensor_tensor(kro[:, :, HR:ROPE], rt[:, 2], rt[:, 3], ALU.add))
                dve.wait_ge(s_hstd, l + 1)
                dve.reciprocal(rsh[:, :, :, :], rsh[:, :, :, :]).then_inc(s_hrs, 1)
                bk.skip(ROUND[5])
                for g in range(FG):
                    bk.take(4 + g)
                    dve.wait_ge(free[4 + g], bk.count(4 + g))
                    o = arrive(g)
                    dve.tensor_tensor(fT[:, g, 0:h2], o, odd[:, g, :], ALU.add)
                    dve.tensor_tensor(fT[:, g, S - 1:h2:-1], o[:, 1:h2], odd[:, g, 1:h2], ALU.subtract
                                      ).then_inc(free[g], 1)
                bk.take(0)

                def head_out(h):
                    dve.wait_ge(free[2], sums_ready[h])
                    st.link(dve.reciprocal(rinv[:, NT * h:NT * h + NT], rsum[:, NT * h:NT * h + NT]))
                    o = arrive(6)
                    dve.tensor_tensor(o_tok[:, :, h * VD:(h + 1) * VD], o.rearrange("p (t c) -> p t c", t=NT),
                                      rinv[:, NT * h:NT * h + NT].unsqueeze(2).broadcast_to([P, NT, VD]), ALU.mult
                                      ).then_inc(free[6], 1)

                def qk_rest(h, i):
                    o = arrive(7)
                    at_ = slice((i % 2) * 512, (i % 2 + 1) * 512)
                    dve.wait_ge(s_qkT, l * 4 * H + 4 * h + i + 1)
                    dve.tensor_tensor(qkT_lo[h % 2][i // 2][0:QK, at_], o[0:QK, :],
                                      qkT[h % 2][i // 2][0:QK, at_].bitcast(F32), ALU.subtract).then_inc(free[7], 1)

                def rest_of_h(k):
                    dve.wait_ge(s_hhi, l * KD + k + 1)
                    dve.tensor_tensor(hLo[:, k, :], hT[:, k, :], hTmp[k].bitcast(F32), ALU.subtract
                                      ).then_inc(s_hlo, 1)

                for i in range(4):
                    qk_rest(0, i)
                sums_ready = []
                for u in range(UNITS + 1):
                    if u < UNITS:
                        b = 2 * (u % 2)
                        arrive(b)
                        if u % NT == NT - 1:
                            sums_ready.append(bk.count(b))
                        dve.tensor_reduce(negm[:, u:u + 1], PS[:, b:b + 2, :].rearrange("p a c -> p (a c)"), AX.X,
                                          ALU.max, negate=True).then_inc(s_nm, 1)
                    if u >= NT and u % NT == 1:
                        head_out(u // NT - 1)
                    if u >= 1:
                        o = arrive(4)
                        bk.take(5)
                        dve.tensor_copy(PT[(u - 1) % 2][:, 0:512], o).then_inc(free[4], 1)
                    if 2 <= u % NT <= 5 and u // NT + 1 < H:
                        qk_rest(u // NT + 1, u % NT - 2)
                    if 1 <= u % NT <= 4 and u // NT + 1 == H:
                        rest_of_h(u % NT - 1)
                head_out(H - 1)
                dve.wait_ge(free[6], bk.count(6))
                dve.memset(mark[:, :], 0.0).then_inc(s_o, 1)
                for k in range(4, KD):
                    rest_of_h(k)

                def rest(c):
                    w = unit_weights(dve, l, c)
                    dve.wait_ge(s_whi, l * N_SPLIT + c + 1)
                    dve.tensor_tensor(wLo[c % 2], w, wHi[c % 2].bitcast(F32), ALU.subtract).then_inc(s_wlo, 1)

                rest(0)
                rest(1)
                bk.skip(ROUND[7])
                for b in range(8):
                    dve.wait_ge(free[b], bk.count(b))
                for i in range(16):
                    b = i % 8
                    bk.take(b)
                    dve.wait_ge(free[b], bk.count(b))
                    m, n = (i % 8) // 2, i % 2
                    y = (oT if i < 8 else fT)[:, m, n * 512:(n + 1) * 512]
                    dve.tensor_tensor(y, y, tmp[:, i % 2, :], ALU.mult).then_inc(s_sm, 1)
                    if i % 2 == 1:
                        rest(i // 2 + 2)
                for m in range(KD):
                    if m + 1 < KD:
                        rest(8 + 2 * m + 2)
                        rest(8 + 2 * m + 3)
                    for n in range(2):
                        i = 2 * m + n
                        for br in range(2):
                            bk.take(4 * n + br)
                            dve.wait_ge(free[4 * n + br], bk.count(4 * n + br))
                            o = arrive(4 * n + 2 + br)
                            g = sg[:, 2 * (i % 2) + br, :]
                            dve.tensor_tensor(g, g, o, ALU.mult).then_inc(free[4 * n + 2 + br], 1)
                            dve.wait_ge(free[4 * n + 2 + br], bk.count(4 * n + 2 + br))
                        dve.tensor_tensor(mT[:, m, n * 512:(n + 1) * 512], sg[:, 2 * (i % 2), :],
                                          sg[:, 2 * (i % 2) + 1, :], ALU.add).then_inc(s_mT, 1)
                dve.wait_ge(s_xback, 16 * l + 16)
                for n in range(2):
                    for t in range(NT):
                        o = arrive(t)
                        xx = x1[:, t, n * 512:(n + 1) * 512]
                        dve.tensor_tensor(xx, xx, o, ALU.add).then_inc(free[t], 1)
                for b in range(8):
                    dve.wait_ge(free[b], bk.count(b))
                dve.memset(mark[:, :], 0.0).then_inc(s_xnew, 1)
            bk.leave(L)
            st.leave(L)

            dve.memset(epsl[:, :], LN_EPS).then_inc(s_init, 1)
            dve.wait_ge(s2_rows, 16 * 7)
            dve.tensor_copy(prow[0:NPAIR, 0, :].rearrange("q (h p) -> q h p", h=2),
                            lrow.unsqueeze(2).broadcast_to([NPAIR, 2, NST])).then_inc(s2_ld, 1)
            for t in range(NT):
                b = (2 * t) % 8
                bk.take(b)
                o = arrive(b + 1)
                dve.tensor_copy(xT[:, 4:8, t * P:(t + 1) * P], o.rearrange("p (k c) -> p k c", k=4)
                                ).then_inc(free[b + 1], 1)

            o = arrive(0)
            st.done(dve.tensor_copy(r3b[:, 1024:1072], o[:, 0:48]))
            st.done(dve.tensor_copy(DT, o[0:CH, 64:64 + NG]))
            st.wait()
            dve.tensor_copy(pT[:, 0:KD], o[:, P:P + KD]).then_inc(free[0], 1)
            dve.wait_ge(w_in_slot[0], 16 * (L * W_DMAS[0] + 3))
            wk = W[:, 0, 0:KD * NIDX].rearrange("p (k c) -> p k c", k=KD)[:, :, NIDX - ID:NIDX]
            dve.tensor_copy(ki4.rearrange("p k (r c) -> p k r c", r=4), wk.unsqueeze(2).broadcast_to([P, KD, 4, ID])
                            ).then_inc(s2_ki, 1)
            dve.wait_ge(s2_par, 16 * S5_LOADS)
            slot = iter(range(40))
            names = {}

            def v(name):
                if name not in names:
                    names[name] = scr[:, next(slot), :]
                return names[name]

            def ts(out_, in_, a1, a2, op0, op1=None):
                st.link(dve.tensor_scalar(out_, in_, a1, a2, op0, op1) if op1 is not None else
                        dve.tensor_scalar(out_, in_, a1, None, op0))

            def stt(out_, in0, c, in1, op0, op1):
                st.link(dve.scalar_tensor_tensor(out=out_, in0=in0, scalar=c, in1=in1, op0=op0, op1=op1))

            def tt(out_, in0, in1, op):
                st.link(dve.tensor_tensor(out_, in0, in1, op))

            ROUNDER = 1.5 * 2.0 ** 23

            def exp(dst, src):
                x, k, rr, p = v("ex"), v("ek"), v("er"), v("ep")
                ts(x, src, -87.0, 88.0, ALU.max, ALU.min)
                ts(k, x, 1.4426950408889634, ROUNDER, ALU.mult, ALU.add)
                ts(k, k, -ROUNDER, None, ALU.add)
                stt(rr, k, -0.693359375, x, ALU.mult, ALU.add)
                stt(rr, k, 2.12194440e-4, rr, ALU.mult, ALU.add)
                ts(p, rr, 1 / 5040.0, 1 / 720.0, ALU.mult, ALU.add)
                for c in (1 / 120.0, 1 / 24.0, 1 / 6.0, 0.5, 1.0):
                    tt(p, p, rr, ALU.mult)
                    ts(p, p, c, None, ALU.add)
                tt(p, p, rr, ALU.mult)
                ts(p, p, 1.0, None, ALU.add)
                ki = v("eki").bitcast(mybir.dt.int32)
                ts(ki, k, 127.0, 8388608.0, ALU.add, ALU.mult)
                tt(dst, p, v("eki"), ALU.mult)

            def sincos(sn, cs, z):
                n, rr, x2, p, q, m, b0, b1 = (v(i) for i in ("sn", "sr", "sx", "sp", "sq", "sm", "sb0", "sb1"))
                ts(n, z, 0.6366197723675814, ROUNDER, ALU.mult, ALU.add)
                ts(n, n, -ROUNDER, None, ALU.add)
                rest = np.pi / 2
                cur = z
                for bits in (9, 20, 31):
                    part_ = float(np.floor(rest * 2.0 ** bits) / 2.0 ** bits)
                    stt(rr, n, -part_, cur, ALU.mult, ALU.add)
                    rest -= part_
                    cur = rr
                stt(rr, n, -float(rest), rr, ALU.mult, ALU.add)
                tt(x2, rr, rr, ALU.mult)
                ts(p, x2, 1 / 362880.0, -1 / 5040.0, ALU.mult, ALU.add)
                for c in (1 / 120.0, -1 / 6.0):
                    tt(p, p, x2, ALU.mult)
                    ts(p, p, c, None, ALU.add)
                tt(p, p, x2, ALU.mult)
                tt(p, p, rr, ALU.mult)
                tt(p, p, rr, ALU.add)
                ts(q, x2, -1 / 3628800.0, 1 / 40320.0, ALU.mult, ALU.add)
                for c in (-1 / 720.0, 1 / 24.0, -0.5):
                    tt(q, q, x2, ALU.mult)
                    ts(q, q, c, None, ALU.add)
                tt(q, q, x2, ALU.mult)
                ts(q, q, 1.0, None, ALU.add)
                for src, half, bit in ((n, m, b0), (m, x2, b1)):
                    ts(half, src, 0.5, -0.25, ALU.mult, ALU.add)
                    ts(half, half, ROUNDER, None, ALU.add)
                    ts(half, half, -ROUNDER, None, ALU.add)
                    stt(bit, half, -2.0, src, ALU.mult, ALU.add)
                ts(n, b0, -1.0, 1.0, ALU.mult, ALU.add)
                ts(b1, b1, -2.0, 1.0, ALU.mult, ALU.add)
                ts(m, b0, -2.0, 1.0, ALU.mult, ALU.add)
                tt(m, m, b1, ALU.mult)
                tt(x2, p, n, ALU.mult)
                tt(rr, q, b0, ALU.mult)
                tt(x2, x2, rr, ALU.add)
                tt(sn, x2, b1, ALU.mult)
                tt(x2, q, n, ALU.mult)
                tt(rr, p, b0, ALU.mult)
                tt(x2, x2, rr, ALU.add)
                tt(cs, x2, m, ALU.mult)

            dt_, zr, zi = v("dt"), v("zr"), v("zi")
            exp(dt_, lam[:, 0, :])
            tt(zr, lam[:, 1, :], dt_, ALU.mult)
            tt(zi, lam[:, 2, :], dt_, ALU.mult)
            er, sn, cs = v("size"), v("sine"), v("cosine")
            exp(er, zr)
            sincos(sn, cs, zi)
            tt(apow[:, 0, :, 0], er, cs, ALU.mult)
            tt(apow[:, 1, :, 0], er, sn, ALU.mult)
            m1, m2 = v("m1"), v("m2")
            for n0 in (1, 2, 4):
                for j in range(n0):
                    ar, ai = apow[:, 0, :, n0 - 1], apow[:, 1, :, n0 - 1]
                    br, bi = apow[:, 0, :, j], apow[:, 1, :, j]
                    tt(m1, ar, br, ALU.mult)
                    tt(m2, ai, bi, ALU.mult)
                    tt(apow[:, 0, :, n0 + j], m1, m2, ALU.subtract)
                    tt(m1, ar, bi, ALU.mult)
                    tt(m2, ai, br, ALU.mult)
                    tt(apow[:, 1, :, n0 + j], m1, m2, ALU.add)
            for _ in range(3):
                tt(er, er, er, ALU.mult)
                tt(m1, cs, cs, ALU.mult)
                tt(m2, sn, sn, ALU.mult)
                tt(sn, sn, cs, ALU.mult)
                ts(sn, sn, 2.0, None, ALU.mult)
                tt(cs, m1, m2, ALU.subtract)
            for i, x in enumerate((er, cs, sn)):
                st.link(dve.tensor_copy(s5c[:, i, :], x))
            lr, li = lam[:, 1, :], lam[:, 2, :]
            tt(m1, lr, lr, ALU.mult)
            tt(m2, li, li, ALU.mult)
            tt(m1, m1, m2, ALU.add)
            inv, fr, fi, am = v("inv"), v("fr"), v("fi"), v("am")
            st.link(dve.reciprocal(inv, m1))
            ts(am, apow[:, 0, :, 0], -1.0, None, ALU.add)
            ai = apow[:, 1, :, 0]
            tt(m1, am, lr, ALU.mult)
            tt(m2, ai, li, ALU.mult)
            tt(fr, m1, m2, ALU.add)
            tt(fr, fr, inv, ALU.mult)
            tt(m1, ai, lr, ALU.mult)
            tt(m2, am, li, ALU.mult)
            tt(fi, m1, m2, ALU.subtract)
            tt(fi, fi, inv, ALU.mult)

            def wide(x):
                return x.unsqueeze(2).broadcast_to([P, NPAIR, CH])

            tt(Bb[:, 0], Braw[:, 0], wide(fr), ALU.mult)
            tt(Bb[:, 1], Braw[:, 0], wide(fi), ALU.mult)
            tt(Braw[:, 0], Braw[:, 1], wide(fi), ALU.mult)
            tt(Bb[:, 0], Bb[:, 0], Braw[:, 0], ALU.subtract)
            tt(Braw[:, 1], Braw[:, 1], wide(fr), ALU.mult)
            dve.tensor_tensor(Bb[:, 1], Bb[:, 1], Braw[:, 1], ALU.add).then_inc(s2_prep, 1)

            for i in range(6):
                bk.take(i)
            dve.wait_ge(s2_rows, 16 * 7)
            for t in range(NT):
                b = (6 + t) % 8
                bk.take(b)
                dve.wait_ge(free[b], bk.count(b))
                st.link(dve.reciprocal(ssx[:, t:t + 1], ssx[:, t:t + 1]))
                dve.scalar_tensor_tensor(out=c2[:, t, :], in0=c2[:, t, :], scalar=ssx[:, t:t + 1], in1=kvg,
                                         op0=ALU.mult, op1=ALU.mult).then_inc(s2_c, 1)
            for b in (7, 0):
                bk.take(b)
            st.done(dve.memset(sel[1][:, 0:P], 0.0))
            st.done(dve.tensor_copy(sel[1][:, P:2 * P], tri[:, :]))
            st.done(dve.tensor_copy(sel[0], tri[:, :]))
            for i in range((NT - 2) * IH):
                t, h = 2 + i // IH, i % IH
                b = 2 * (i % 4)
                bk.take(b)
                dve.wait_ge(free[b], bk.count(b))
                src, w = rl[i % 2][:, 0:(t + 1) * P], wtok[:, t, h:h + 1]
                if h == 0:
                    dve.tensor_scalar(sel[t], src, w, None, ALU.mult).then_inc(s2_acc, 1)
                else:
                    dve.wait_ge(s2_acc, i)
                    dve.scalar_tensor_tensor(out=sel[t], in0=src, scalar=w, in1=sel[t], op0=ALU.mult, op1=ALU.add
                                             ).then_inc(s2_acc, 1)
                if h == IH - 1:
                    dve.wait_ge(s2_acc, i + 1)
                    diag = sel[t][:, t * P:(t + 1) * P]
                    st.done(dve.tensor_tensor(diag, diag, tri[:, :], ALU.add))
            st.wait()

            def select(t):
                for _ in range(TOPK // 8):
                    st.link(dve.max(m8, sel[t]))
                    st.link(dve.match_replace(sel[t], m8, sel[t], TAKEN))
                ts(sel[t], sel[t], TAKEN, MASKED, ALU.is_gt, ALU.mult)

            def scan(f):
                p = f % 2
                dve.wait_ge(s2_w, f + 1)
                for i in range(2):
                    for q in range(HP):
                        qq = f * HP + q
                        if (i, q) == (1, HP - 1):
                            st.wait()
                        z = dve.tensor_tensor_scan(st_[p][:, i, q, :], s5c[:, 0, qq:qq + 1].broadcast_to([P, NC]),
                                                   M1[p][:, i, q, :], 0.0, ALU.mult, ALU.add)
                        if (i, q) == (1, HP - 1):
                            z.then_inc(s2_z, 1)
                        else:
                            st.done(z)

            select(2)
            select(3)
            scan(0)
            scan(1)
            select(4)
            select(5)
            scan(2)
            scan(3)
            select(6)
            select(7)
            bk.n = list(marks["attention"])
            dve.wait_ge(s2_glu, 8)
            dve.wait_ge(s2_ln, 32)

            def att_norm(t):
                dve.wait_ge(free[2], sums2[t])
                st.link(dve.reciprocal(rinv[:, H * t:H * t + H], rsum[:, H * t:H * t + H]))
                o = arrive(7)
                dve.tensor_tensor(att[t % 2].rearrange("p (h d) -> p h d", h=H), o.rearrange("p (h d) -> p h d", h=H),
                                  rinv[:, H * t:H * t + H].unsqueeze(2).broadcast_to([P, H, VD]), ALU.mult
                                  ).then_inc(free[7], 1)

            def att_gate(t):
                o = arrive(6)
                m = mix[:, 0:4, t * P:(t + 1) * P]
                dve.tensor_tensor(m, m, o.rearrange("p (k c) -> p k c", k=4), ALU.mult).then_inc(free[6], 1)

            def residual(t, n):
                x = xt[t % 2]
                if n == 1:
                    dve.wait_ge(s2_xt[t % 2], 16 * (t // 2 + 1))
                o = arrive(6 + n)
                xx = x[:, n * 512:(n + 1) * 512]
                dve.scalar_tensor_tensor(out=xx, in0=xx, scalar=ALPHA, in1=o, op0=ALU.mult, op1=ALU.add
                                         ).then_inc(free[6 + n], 1)
                if n == 1:
                    half_free[t] = bk.count(7)
                    return
                dve.wait_ge(free[7], half_free[t])
                dve.wait_ge(free[6], bk.count(6))
                st.link(dve.tensor_reduce(ssc[:, t:t + 1], x, AX.X, ALU.add))
                ts(ssc[:, t:t + 1], ssc[:, t:t + 1], -1.0 / D, None, ALU.mult)
                dve.tensor_scalar(x, x, ssc[:, t:t + 1], None, ALU.add).then_inc(s2_r, 1)

            half_free = {}

            def layer_norm(t):
                x = xt[t % 2]
                dve.wait_ge(s2_sq, t + 1)
                st.link(dve.reciprocal(rsx[:, t:t + 1], rsx[:, t:t + 1]))
                stt(x, x, rsx[:, t:t + 1], lng, ALU.mult, ALU.mult)
                dve.tensor_tensor(x, x, lnb, ALU.add).then_inc(s2_o, 1)

            def turned(u):
                t, h = u // H, u % H
                n = min(4, t + 1)
                o = arrive(4)
                if t >= 4:
                    bk.take(5)
                dve.tensor_copy(PT2[h // 4][:, 0:n, (h % 4) * P:(h % 4 + 1) * P],
                                o[:, 0:n * P].rearrange("p (k c) -> p k c", k=n)).then_inc(free[4], 1)

            sums2 = {}
            for u in range(H * NT):
                t, h = u // H, u % H
                b = 2 * (u % 2)
                arrive(b)
                w = (t + 1) * P
                if h == H - 1:
                    sums2[t] = bk.count(b)
                if u >= 2:
                    bp = 2 * (u % 2)
                    dve.wait_ge(full[4 + (((u - 2) // H) >= 4)], bk.count(4 + (((u - 2) // H) >= 4)))
                dve.tensor_tensor_reduce(Pb2[u % 2][:, 0:w], PS[:, b:b + 2, :].rearrange("p a c -> p (a c)")[:, 0:w],
                                         sel[t], -1.0, 3.4e38, ALU.add, ALU.min, negm[:, u:u + 1]).then_inc(s2_nm, 1)
                if u >= 1:
                    turned(u - 1)
                if h == 5:
                    bk.take(6)
                if t >= 2:
                    if h == 0:
                        residual(t - 2, 0)
                    if h == 4:
                        layer_norm(t - 2)
                if t >= 1:
                    if h == 1:
                        bk.take(6)
                    if h == 2:
                        att_norm(t - 1)
                    if h == 3:
                        att_gate(t - 1)
                    if h == 6:
                        residual(t - 1, 1)
            turned(H * NT - 1)
            residual(NT - 2, 0)
            bk.take(6)
            att_norm(NT - 1)
            att_gate(NT - 1)
            layer_norm(NT - 2)
            residual(NT - 1, 1)
            residual(NT - 1, 0)
            layer_norm(NT - 1)

        @block.gpsimd
        def _(pool):
            bk = Banks(full, free)
            st = Steps(pool, s_pool)
            q3 = q_tok.rearrange("p t (h c) -> p t h c", h=H)
            pool.wait_ge(s_const, 64)
            with pool.Fori(0, L) as l:
                bk.enter(l)
                st.enter(l, 9 * H)
                for n in ROUND[:7]:
                    bk.skip(n)
                pool.wait_ge(s_hrs, l + 1)
                qs, ks = stage[:, 0], stage[:, 1]
                x1p, x2p = qs[:, :, NOPE:NOPE + HR], qs[:, :, NOPE + HR:QK]

                def over(gain, n):
                    return gain.unsqueeze(1).broadcast_to([P, NT, n])

                for h in range(H):
                    rq = rsh[:, 0, :, h:h + 1]
                    rk = rsh[:, 1, :, h:h + 1]
                    if h >= 1:
                        pool.wait_ge(full[7], bk.count(7) - 2)
                    st.link(pool.tensor_tensor(qs, q3[:, :, h, :], rq.broadcast_to([P, NT, QK]), ALU.mult))
                    st.link(pool.tensor_tensor(qs, qs, over(gq[:, :], QK), ALU.mult))
                    st.done(pool.tensor_tensor(rtp[:, 0], x1p, cosT[:, :, :], ALU.mult))
                    st.done(pool.tensor_tensor(rtp[:, 1], x2p, sinT[:, :, :], ALU.mult))
                    st.done(pool.tensor_tensor(rtp[:, 2], x2p, cosT[:, :, :], ALU.mult))
                    st.link(pool.tensor_tensor(rtp[:, 3], x1p, sinT[:, :, :], ALU.mult))
                    st.link(pool.tensor_tensor(x1p, rtp[:, 0], rtp[:, 1], ALU.subtract))
                    pool.tensor_tensor(x2p, rtp[:, 2], rtp[:, 3], ALU.add).then_inc(s_stage, 1)
                    if h >= 1:
                        pool.wait_ge(full[7], bk.count(7))
                    st.link(pool.tensor_tensor(ks[:, :, 0:NOPE], k_tok[:, :, h, :],
                                               rk.broadcast_to([P, NT, NOPE]), ALU.mult))
                    st.link(pool.tensor_tensor(ks[:, :, 0:NOPE], ks[:, :, 0:NOPE], over(gk[:, 0:NOPE], NOPE),
                                               ALU.mult))
                    pool.tensor_tensor(ks[:, :, NOPE:QK], kro[:, :, :], rk.broadcast_to([P, NT, ROPE]), ALU.mult
                                       ).then_inc(s_stage, 1)
                    for _ in range(4):
                        bk.take(7)
                for k in range(H_ACT, KD):
                    pool.wait_ge(s_hlo, l * KD + k + 1)
                    pool.tensor_tensor(hHi[:, k, :], hT[:, k, :], hLo[:, k, :].bitcast(F32), ALU.subtract
                                       ).then_inc(s_hin[1], 1)
                for b, n in enumerate(FIXED):
                    if b != 7:
                        bk.n[b] += n
                for n in ROUND[7:]:
                    bk.skip(n)
            bk.leave(L)
            st.leave(L)

            pool.wait_ge(s_xnew, L + 1)
            pool.memset(kiz, 0.0).then_inc(s2_kz, 1)
            pool.wait_ge(s2_prep, 1)
            def mul(o, x, y):
                st.done(pool.tensor_tensor(o, x, y, ALU.mult))

            def add(o, x, y, op=ALU.add):
                return pool.tensor_tensor(o, x, y, op)

            def prep(f):
                p = f % 2
                if f == 0:
                    pool.wait_ge(free[7], marks["C"][0])
                    pool.wait_ge(free[0], marks["C"][1])
                if f >= 2:
                    pool.wait_ge(full[7], marks["y", f - 2])
                qs = slice(f * HP, (f + 1) * HP)
                g = [G[p][:, i] for i in range(2)]
                tmp0 = ca_re[p]
                tmp1 = ca_ni[p]
                b4 = [Bb[:, i, qs, :].unsqueeze(2).broadcast_to([P, HP, CL, CH]) for i in range(2)]
                a4 = [apow[:, i, qs, :].unsqueeze(3).broadcast_to([P, HP, CL, CH]) for i in range(2)]
                b3 = [Bb[:, i, qs, :].unsqueeze(2).broadcast_to([P, HP, CL - 1, CH]) for i in range(2)]
                r3 = [apow[:, i, qs, CL - 2::-1].unsqueeze(3).broadcast_to([P, HP, CL - 1, CH]) for i in range(2)]
                lo = slice(0, CL - 1)
                mul(g[0][:, :, lo], b3[0], r3[0])
                mul(tmp0[:, :, lo], b3[1], r3[1])
                mul(g[1][:, :, lo], b3[0], r3[1])
                mul(tmp1[:, :, lo], b3[1], r3[0])
                st.done(pool.tensor_copy(g[0][:, :, CL - 1], Bb[:, 0, qs, :]))
                st.done(pool.tensor_copy(g[1][:, :, CL - 1], Bb[:, 1, qs, :]))
                st.wait()
                st.link(add(g[0][:, :, lo], g[0][:, :, lo], tmp0[:, :, lo], ALU.subtract))
                add(g[1][:, :, lo], g[1][:, :, lo], tmp1[:, :, lo]).then_inc(s2_G, 1)
                pool.wait_ge(s2_G, f + 1)
                c4 = [CT[:, i, qs, :].unsqueeze(2).broadcast_to([P, HP, CL, CH]) for i in range(2)]
                s4 = part(r3b, 2048, f)[:, 0:512].rearrange("p (q i c) -> p q i c", q=HP, i=CL)
                mul(ca_re[p], c4[0], a4[0])
                mul(s4, c4[1], a4[1])
                mul(ca_ni[p], c4[1], a4[0])
                st.wait()
                st.link(add(ca_re[p], ca_re[p], s4))
                mul(s4, c4[0], a4[1])
                st.wait()
                add(ca_ni[p], ca_ni[p], s4, ALU.subtract).then_inc(s2_CA, 1)

            def skip(f):
                p = f % 2
                if f >= 1:
                    pool.wait_ge(s2_K, f)
                pool.wait_ge(free[3], marks["kernel", f])
                gs = slice(2 * HP * f, 2 * HP * (f + 1))
                st.link(pool.tensor_tensor(dtmp, ident[0:CH, 0:CH].unsqueeze(1).broadcast_to([CH, 2 * HP, CH]),
                                           DT[:, gs].unsqueeze(2).broadcast_to([CH, 2 * HP, CH]), ALU.mult))
                add(K16[p][:, :, 0:CH], K16[p][:, :, 0:CH], dtmp).then_inc(s2_K, 1)

            def rotations(f):
                p = f % 2
                pool.wait_ge(s2_TT[f % 2], 16 * CL * (f // 2 + 1))
                R = rot[p]
                qs = slice(f * HP, (f + 1) * HP)
                st.done(pool.memset(R[:, 0, :, 0:1], 1.0))
                st.done(pool.memset(R[:, 1, :, 0:1], 0.0))
                st.done(pool.tensor_copy(R[:, 0, :, 1:2], s5c[:, 1, qs].unsqueeze(2)))
                st.done(pool.tensor_copy(R[:, 1, :, 1:2], s5c[:, 2, qs].unsqueeze(2)))
                st.wait()
                W0, W1 = st_[p][:, 0], st_[p][:, 1]
                n = 2
                while n < NC:
                    hr, hi = R[:, 0, :, n // 2:n // 2 + 1], R[:, 1, :, n // 2:n // 2 + 1]
                    dr, di = R[:, 0, :, n:n + 1], R[:, 1, :, n:n + 1]
                    t0, t1 = W0[:, :, 0:1], W0[:, :, 1:2]
                    mul(t0, hr, hr)
                    mul(t1, hi, hi)
                    mul(di, hr, hi)
                    st.wait()
                    st.done(add(dr, t0, t1, ALU.subtract))
                    st.link(add(di, di, di))
                    if n > 1:
                        m = n - 1
                        br = dr.broadcast_to([P, HP, m])
                        bi = di.broadcast_to([P, HP, m])
                        cr, ci = R[:, 0, :, 1:n], R[:, 1, :, 1:n]
                        er_, ei_ = R[:, 0, :, n + 1:2 * n], R[:, 1, :, n + 1:2 * n]
                        w0, w1 = W0[:, :, 0:m], W1[:, :, 0:m]
                        mul(er_, cr, br)
                        mul(w0, ci, bi)
                        mul(ei_, cr, bi)
                        mul(w1, ci, br)
                        st.wait()
                        st.done(add(er_, er_, w0, ALU.subtract))
                        st.link(add(ei_, ei_, w1))
                    n *= 2
                pool.sem_inc(s2_R, 1)

            def rotate(f):
                p = f % 2
                R = rot[p]
                W0, W1 = M1[p][:, 0], M1[p][:, 1]
                pool.wait_ge(free[5], marks["states", f])
                sr, si = st_[p][:, 0], st_[p][:, 1]
                mul(W0, R[:, 0], sr)
                mul(W1, R[:, 1], si)
                st.wait()
                st.link(add(W0, W0, W1))
                mul(W1, R[:, 0], si)
                mul(sr, R[:, 1], sr)
                st.wait()
                add(W1, W1, sr, ALU.subtract).then_inc(s2_w, 1)

            def rotate_back(f):
                p = f % 2
                pool.wait_ge(s2_z, f + 1)
                m = NC - 1
                zr, zi = st_[p][:, 0, :, 0:m], st_[p][:, 1, :, 0:m]
                Rr, Ri = rot[p][:, 0, :, 0:m], rot[p][:, 1, :, 0:m]
                X0, X1 = X[p][:, 0, :, 1:NC], X[p][:, 1, :, 1:NC]
                st.done(pool.memset(X[p][:, 0, :, 0:1], 0.0))
                st.done(pool.memset(X[p][:, 1, :, 0:1], 0.0))
                mul(X0, Rr, zr)
                mul(X1, Ri, zr)
                st.wait()
                mul(zr, Ri, zi)
                mul(zi, Rr, zi)
                st.wait()
                st.link(add(X0, X0, zr, ALU.subtract))
                add(X1, X1, zi).then_inc(s2_X, 1)

            prep(0)
            prep(1)
            pool.wait_ge(s2_acc, (NT - 2) * IH)
            st.link(pool.memset(TT[0], 0.0))
            pool.memset(TT[1], 0.0).then_inc(s2_TT0, 1)
            pool.wait_ge(s2_TT0, 1)
            for f in (0, 2):
                if f:
                    prep(f)
                skip(f)
                if f:
                    prep(f + 1)
                skip(f + 1)
                for step in (rotations, rotate, rotate_back):
                    step(f)
                    step(f + 1)
            for m in range(4):
                for n in range(2):
                    i = 2 * m + n
                    b, c = marks["glu", i]
                    pool.wait_ge(free[b], c)
                    y = mix[:, 4 + m, n * 512:(n + 1) * 512]
                    st.link(pool.tensor_tensor(vb[i % 2], vb[i % 2], gb[i % 2], ALU.mult))
                    pool.tensor_tensor(y, y, vb[i % 2], ALU.mult).then_inc(s2_glu, 1)


def tables():
    inv = 10000.0 ** (-np.arange(HR, dtype=np.float32) / HR)
    ang = np.arange(S, dtype=np.float32)[:, None] * inv[None].astype(np.float32)
    d = np.arange(P, dtype=np.float64)
    pd = 2 * np.pi * ((d[:, None] * d[None]) % P) / P
    s = np.arange(S // 2)[:, None] * np.arange(HF)[None]
    ps = 2 * np.pi * (s % S).astype(np.float64) / S
    seq = np.concatenate([np.cos(ps), -np.sin(ps)])
    seq[S // 2] = 1 - 2.0 * (np.arange(HF) % 2)
    f = np.float32
    return {
        "c_ident": np.eye(P, dtype=f),
        "c_cos": np.cos(ang.astype(np.float64)).astype(f), "c_sin": np.sin(ang.astype(np.float64)).astype(f),
        "c_tri": np.where(np.arange(P)[None] <= np.arange(P)[:, None], 0, MASKED).astype(f),
        "c_dft_d": np.concatenate([np.cos(pd), np.sin(pd)], 1).astype(f),
        "c_dft_s": (seq / np.sqrt(S * P)).astype(f),
    }


def kernel(**inputs):
    import concourse.bacc as _bacc
    from concourse.bass_utils import run_bass_kernel_spmd as _run

    nc = _bacc.Bacc("TRN2", target_bir_lowering=False, num_devices=1)
    arrays, a = {}, {}
    for name, v in {**inputs, **tables()}.items():
        v = np.ascontiguousarray(v)
        arrays[f"in_{name}"] = v
        a[name] = nc.dram_tensor(f"in_{name}", v.shape, mybir.dt.from_np(v.dtype), kind="ExternalInput").ap()
    out = nc.dram_tensor("out_0", (1, S, D), F32, kind="ExternalOutput").ap()
    build(nc, a, out)
    r = _run(nc, [arrays], core_ids=[0])
    return r.results[0]["out_0"]
```
